# Optimizing a Trainium2 kernel written in Bass

```python
import jax, jax.numpy as jnp
from jax import lax
import numpy as np

D_MODEL = 1024
BATCH = 1
SEQ = 1024
DEPTH = 2

CHUNK = 64
N_MIXERS = 2
N_ATTN_LAYERS = (DEPTH + 1) // 2
N_REC_LAYERS = DEPTH // 2
ATTN_HEAD_DIM = 64
ATTN_Q_HEADS = D_MODEL // ATTN_HEAD_DIM
ATTN_KV_HEADS = max(1, ATTN_Q_HEADS // 8)
ATTN_GROUP = ATTN_Q_HEADS // ATTN_KV_HEADS
ATTN_Q_DIM = ATTN_Q_HEADS * ATTN_HEAD_DIM
ATTN_KV_DIM = ATTN_KV_HEADS * ATTN_HEAD_DIM
ATTN_IN_DIM = ATTN_Q_DIM + 2 * ATTN_KV_DIM
WINDOW = 128
WINDOW_CHUNKS = WINDOW // CHUNK
ROPE_THETA = 500000.0
ROPE_DIM = ATTN_HEAD_DIM // 4
REC_EXPAND = 128
REC_HEADS = D_MODEL // REC_EXPAND
REC_K = REC_EXPAND
REC_V = D_MODEL // REC_HEADS
REC_F_DIM = REC_HEADS * REC_K
REC_IN_DIM = 2 * REC_F_DIM + 2 * D_MODEL
D_FF = 2816
CONV_W = 3
EPS = 1e-6

kernel_name = "hybrid_swa_sink_hgrn2_convffn_adaln"

def rmsnorm(t, w):
    tf = t.astype(jnp.float32)
    tf = tf * lax.rsqrt(jnp.mean(tf * tf, axis=-1, keepdims=True) + EPS)
    return (tf * w.astype(jnp.float32)).astype(t.dtype)

def rope_cos_sin(positions):
    inv_freq = ROPE_THETA ** (-jnp.arange(0, ROPE_DIM, 2, dtype=jnp.float32) / ROPE_DIM)
    ang = positions.astype(jnp.float32)[..., None] * inv_freq
    return jnp.cos(ang)[:, :, None, :], jnp.sin(ang)[:, :, None, :]

def apply_partial_rope(t, cos, sin):
    half = ROPE_DIM // 2
    t1 = t[..., :half].astype(jnp.float32)
    t2 = t[..., half:ROPE_DIM].astype(jnp.float32)
    rot = jnp.concatenate([t1 * cos - t2 * sin, t2 * cos + t1 * sin], axis=-1).astype(t.dtype)
    return jnp.concatenate([rot, t[..., ROPE_DIM:]], axis=-1)

def shift_chunks(t, j):
    if j == 0:
        return t
    return jnp.concatenate([jnp.zeros_like(t[:, :j]), t[:, :-j]], axis=1)

def sliding_window_attention(h, positions, w_in, w_out, sinks):
    B, S, _ = h.shape
    nC = S // CHUNK
    proj = h @ w_in
    q = proj[..., :ATTN_Q_DIM].reshape(B, S, ATTN_Q_HEADS, ATTN_HEAD_DIM)
    k = proj[..., ATTN_Q_DIM:ATTN_Q_DIM + ATTN_KV_DIM].reshape(B, S, ATTN_KV_HEADS, ATTN_HEAD_DIM)
    v = proj[..., ATTN_Q_DIM + ATTN_KV_DIM:].reshape(B, S, ATTN_KV_HEADS, ATTN_HEAD_DIM)
    cos, sin = rope_cos_sin(positions)
    q = apply_partial_rope(q, cos, sin)
    k = apply_partial_rope(k, cos, sin)
    q = q.reshape(B, nC, CHUNK, ATTN_KV_HEADS, ATTN_GROUP, ATTN_HEAD_DIM)
    k = k.reshape(B, nC, CHUNK, ATTN_KV_HEADS, ATTN_HEAD_DIM)
    v = v.reshape(B, nC, CHUNK, ATTN_KV_HEADS, ATTN_HEAD_DIM)
    shifts = range(WINDOW_CHUNKS - 1, -1, -1)
    kb = jnp.concatenate([shift_chunks(k, j) for j in shifts], axis=2)
    vb = jnp.concatenate([shift_chunks(v, j) for j in shifts], axis=2)
    key_shift = jnp.repeat(jnp.arange(WINDOW_CHUNKS - 1, -1, -1), CHUNK)
    valid = (jnp.arange(nC)[:, None] - key_shift[None, :]) >= 0
    scores = jnp.einsum("bnqkgd,bnskd->bnkgqs", q, kb,
                        preferred_element_type=jnp.float32) * (ATTN_HEAD_DIM ** -0.5)
    scores = jnp.where(valid[None, :, None, None, None, :], scores, -jnp.inf)
    sink = sinks.astype(jnp.float32).reshape(1, 1, ATTN_KV_HEADS, ATTN_GROUP, 1, 1)
    m = jnp.maximum(jnp.max(scores, axis=-1, keepdims=True), sink)
    p = jnp.exp(scores - m)
    probs = p / (jnp.sum(p, axis=-1, keepdims=True) + jnp.exp(sink - m))
    o = jnp.einsum("bnkgqs,bnskd->bnqkgd", probs.astype(vb.dtype), vb)
    return o.reshape(B, S, ATTN_Q_DIM) @ w_out

def hgrn2(h, w_in, w_out, g_norm, lb):
    B, S, _ = h.shape
    nC = S // CHUNK
    proj = h @ w_in
    q = jax.nn.silu(proj[..., :REC_F_DIM].astype(jnp.float32))
    fl = proj[..., REC_F_DIM:2 * REC_F_DIM].astype(jnp.float32)
    i = proj[..., 2 * REC_F_DIM:2 * REC_F_DIM + D_MODEL].astype(jnp.float32)
    g = proj[..., 2 * REC_F_DIM + D_MODEL:]
    f = lb + (1.0 - lb) * jax.nn.sigmoid(fl)
    kk = 1.0 - f
    logf = jnp.log(f)

    def to_chunks(t, dim):
        return t.reshape(B, nC, CHUNK, REC_HEADS, dim).transpose(1, 0, 3, 2, 4)

    qc, kc, gc = to_chunks(q, REC_K), to_chunks(kk, REC_K), to_chunks(logf, REC_K)
    vc = to_chunks(i, REC_V)
    tri = jnp.tril(jnp.ones((CHUNK, CHUNK), dtype=bool))

    def step(state, xs):
        qt, kt, vt, gt = xs
        G = jnp.cumsum(gt, axis=2)
        inter = jnp.einsum("bhtk,bhkv->bhtv", qt * jnp.exp(G), state)
        diff = G[:, :, :, None, :] - G[:, :, None, :, :]
        decay = jnp.exp(jnp.where(tri[None, None, :, :, None], diff, -jnp.inf))
        A = jnp.einsum("bhtk,bhsk,bhtsk->bhts", qt, kt, decay)
        intra = jnp.einsum("bhts,bhsv->bhtv", A, vt)
        G_last = G[:, :, -1:, :]
        new_state = jnp.exp(G_last[:, :, 0, :])[..., None] * state + jnp.einsum(
            "bhsk,bhsv->bhkv", kt * jnp.exp(G_last - G), vt)
        return new_state, inter + intra

    state0 = jnp.zeros((B, REC_HEADS, REC_K, REC_V), jnp.float32)
    _, o = lax.scan(step, state0, (qc, kc, vc, gc))
    o = o.transpose(1, 0, 3, 2, 4).reshape(B, S, REC_HEADS, REC_V)
    o = rmsnorm(o, g_norm).reshape(B, S, D_MODEL) * jax.nn.silu(g.astype(jnp.float32))
    return o.astype(h.dtype) @ w_out

def conv_ffn(h, w_in, conv_w, conv_b, w_out):
    S = h.shape[1]
    u = h @ w_in
    up = jnp.pad(u, ((0, 0), (CONV_W - 1, 0), (0, 0)))
    u = sum(up[:, j:j + S] * conv_w[j] for j in range(CONV_W)) + conv_b
    a, b = u[..., :D_FF], u[..., D_FF:]
    return (jax.nn.silu(a) * b) @ w_out

def setup_inputs(seed: int = 0) -> dict:
    key = jax.random.key(seed)
    ks = jax.random.split(key, 20)

    def nrm(k, shape, scale):
        return jax.random.normal(k, shape, jnp.float32) * scale

    offset = jax.random.randint(ks[2], (BATCH, 1), 0, 4096)
    positions = (offset + jnp.arange(SEQ)[None, :]).astype(jnp.int32)
    return {
        "x": nrm(ks[0], (BATCH, SEQ, D_MODEL), 1.0),
        "c": nrm(ks[1], (BATCH, D_MODEL), 1.0),
        "positions": positions,
        "ada_w": nrm(ks[3], (DEPTH, D_MODEL, 6 * D_MODEL), 0.5 * D_MODEL ** -0.5),
        "ada_b": nrm(ks[4], (DEPTH, 6 * D_MODEL), 0.02),
        "norm1_w": 1.0 + nrm(ks[5], (DEPTH, D_MODEL), 0.02),
        "norm2_w": 1.0 + nrm(ks[6], (DEPTH, D_MODEL), 0.02),
        "final_norm_w": 1.0 + nrm(ks[7], (D_MODEL,), 0.02),
        "attn_w_in": nrm(ks[8], (N_ATTN_LAYERS, D_MODEL, ATTN_IN_DIM), D_MODEL ** -0.5),
        "attn_w_out": nrm(ks[9], (N_ATTN_LAYERS, ATTN_Q_DIM, D_MODEL), ATTN_Q_DIM ** -0.5),
        "attn_sinks": nrm(ks[10], (N_ATTN_LAYERS, ATTN_Q_HEADS), 1.0),
        "rec_w_in": nrm(ks[11], (N_REC_LAYERS, D_MODEL, REC_IN_DIM), D_MODEL ** -0.5),
        "rec_lb_logits": nrm(ks[12], (N_REC_LAYERS, REC_F_DIM), 1.0),
        "rec_g_norm": 1.0 + nrm(ks[13], (N_REC_LAYERS, REC_V), 0.02),
        "rec_w_out": nrm(ks[14], (N_REC_LAYERS, D_MODEL, D_MODEL), D_MODEL ** -0.5),
        "ffn_w_in": nrm(ks[15], (DEPTH, D_MODEL, 2 * D_FF), D_MODEL ** -0.5),
        "ffn_conv_w": nrm(ks[16], (DEPTH, CONV_W, 2 * D_FF), CONV_W ** -0.5),
        "ffn_conv_b": nrm(ks[17], (DEPTH, 2 * D_FF), 0.02),
        "ffn_w_out": nrm(ks[18], (DEPTH, D_FF, D_MODEL), D_FF ** -0.5),
    }

def reference(x, c, positions, ada_w, ada_b, norm1_w, norm2_w, final_norm_w,
              attn_w_in, attn_w_out, attn_sinks, rec_w_in, rec_lb_logits,
              rec_g_norm, rec_w_out, ffn_w_in, ffn_conv_w, ffn_conv_b, ffn_w_out):
    lb_p = jax.nn.softmax(rec_lb_logits.astype(jnp.float32), axis=0)
    lower_bounds = jnp.cumsum(lb_p, axis=0) - lb_p[0:1]
    c_act = jax.nn.silu(c)
    for i in range(DEPTH):
        mod = c_act @ ada_w[i] + ada_b[i]
        sh1, sc1, g1, sh2, sc2, g2 = [m[:, None, :] for m in jnp.split(mod, 6, axis=-1)]
        h = rmsnorm(x, norm1_w[i]) * (1.0 + sc1) + sh1
        j = i // N_MIXERS
        if i % N_MIXERS == 0:
            y = sliding_window_attention(h, positions, attn_w_in[j], attn_w_out[j], attn_sinks[j])
        else:
            y = hgrn2(h, rec_w_in[j], rec_w_out[j], rec_g_norm[j], lower_bounds[j])
        x = x + g1 * y
        h = rmsnorm(x, norm2_w[i]) * (1.0 + sc2) + sh2
        x = x + g2 * conv_ffn(h, ffn_w_in[i], ffn_conv_w[i], ffn_conv_b[i], ffn_w_out[i])
    return rmsnorm(x, final_norm_w)


_drawn_inputs = setup_inputs


def setup_inputs(seed=0):
    import zlib

    import numpy as np

    out = dict(_drawn_inputs(seed))
    spreads = {}
    factors = {'norm1_w': 8.0,
     'norm2_w': 6.357,
     'final_norm_w': 2.862,
     'attn_sinks': 8.0,
     'rec_g_norm': 8.0,
     'ffn_conv_b': 6.95}
    for name, (base, spread) in spreads.items():
        noise = np.random.default_rng([zlib.crc32(name.encode()), seed]).standard_normal(out[name].shape)
        drawn = base * np.exp(spread * noise) if base else spread * noise
        out[name] = __import__('jax').numpy.asarray(drawn.astype(out[name].dtype))
    for name, factor in factors.items():
        out[name] = (out[name] * factor).astype(out[name].dtype)
    return out
```

```python
from contextlib import ExitStack

import numpy as np

import concourse.bass as bass
from concourse import mybir

F32 = mybir.dt.float32
F32R = mybir.dt.float32r
I32 = mybir.dt.int32
U8 = mybir.dt.uint8
ACT = mybir.ActivationFunctionType
ALU = mybir.AluOpType
AX = mybir.AxisListType

P = 128
S = 1024
D = 1024
KT = D // P
HALF = S // 2
DEPTH = 2
CHUNK = 64
N_CHUNKS = S // CHUNK
HEAD = 64
N_HEADS = D // HEAD
ROPE = HEAD // 4
ROPE_THETA = 500000.0
REC_HEADS = 8
TT = S // P
LEVELS = 7
FF = 2816
FT = FF // P
GROUPS = FT // 2
EPS = 1e-6

C_COND = 0
C_ADA_B = C_COND + KT
C_NORM1 = C_ADA_B + DEPTH * 6 * KT
C_NORM2 = C_NORM1 + DEPTH * KT
C_FINAL = C_NORM2 + DEPTH * KT
C_LB = C_FINAL + KT
C_GNORM = C_LB + REC_HEADS
C_SINK = C_GNORM + 1
C_FREQ = C_SINK + N_HEADS // 2
C_SIGN = C_FREQ + 1
C_CONV_W = C_SIGN + 1
C_CONV_B = C_CONV_W + DEPTH * 3 * 2 * FT
N_VEC = C_CONV_B + DEPTH * 2 * FT

N_QKV = D // P + 2
N_OUT = D // P
N_FFN = 3 * FT
N_REC = 4 * REC_HEADS
W_QKV = 0
W_AO = W_QKV + N_QKV
W_FFN0 = W_AO + N_OUT
W_REC = W_FFN0 + N_FFN
W_RO = W_REC + N_REC
W_FFN1 = W_RO + N_OUT
N_WTILES = W_FFN1 + N_FFN

RAW_RING = 2
W_RING = 4


def at(it, per, k):
    return k if it is None else it * per + k


class Steps:

    def __init__(self, eng, sem):
        self.eng, self.sem, self.n, self.it, self.per = eng, sem, 0, None, 0

    def add(self, ins):
        ins.then_inc(self.sem, 1)
        self.n += 1

    def now(self):
        return at(self.it, self.per, self.n)

    def wait(self):
        self.eng.wait_ge(self.sem, self.now())

    def link(self, ins):
        self.add(ins)
        self.wait()

    def enter(self, it, per):
        self.it, self.per, self.start = it, per, self.n

    def leave(self, trips):
        assert self.n - self.start == self.per, (self.n - self.start, self.per)
        self.n = self.start + self.per * trips
        self.it, self.per = None, 0


def two_pi_parts():
    whole = 2 * np.pi
    c1 = np.floor(whole * 32) / 32
    c2 = np.floor((whole - c1) * 2.0 ** 17) / 2.0 ** 17
    return float(c1), float(c2), float(np.float32(whole - c1 - c2))


def trunk_kernel(nc, xT, positions, vec_in, ada_tiles, w_tiles, ident_in, masks_in, outT, x_spill):
    ctx = ExitStack()
    with ctx:
        def sem(name):
            return ctx.enter_context(nc.semaphore(name))

        def alloc(stack, name, shape, dt=F32):
            return stack.enter_context(nc.sbuf_tensor(name, shape, dt))

        vec = alloc(ctx, "vec", [P, N_VEC])
        ident = alloc(ctx, "ident", [P, P])
        ones = alloc(ctx, "ones", [P, P])
        cond = alloc(ctx, "cond_silu", [P, KT])
        mod = alloc(ctx, "mod", [P, DEPTH * 6 * KT])
        gain = alloc(ctx, "gain", [P, DEPTH * 2 * KT])
        eps_col = alloc(ctx, "eps_col", [P, 1])
        rstd = alloc(ctx, "rstd", [P, S])
        w_raw = [alloc(ctx, f"w_raw{i}", [P, KT, P]) for i in range(RAW_RING)]
        w_hi = [alloc(ctx, f"w_hi{i}", [P, KT, P], F32R) for i in range(W_RING)]
        w_lo = [alloc(ctx, f"w_lo{i}", [P, KT, P], F32R) for i in range(W_RING)]
        in_hi = alloc(ctx, "in_hi", [P, KT, S], F32R)
        in_lo = alloc(ctx, "in_lo", [P, KT, S], F32R)
        tail = ExitStack()
        with tail:
            x = alloc(tail, "x", [P, KT, S])
            attn = ExitStack()
            with attn:
                q_raw = alloc(attn, "q_raw", [P, KT, S])
                kv_raw = alloc(attn, "kv_raw", [P, 2, S])
                rope_cos = alloc(attn, "rope_cos", [P, S])
                rope_sin = alloc(attn, "rope_sin", [P, S])
                tmp = [alloc(attn, f"tmp{i}", [P, S]) for i in range(2)]
            ffn = ExitStack()
            with ffn:
                g_hi = alloc(ffn, "g_hi", [P, 4, S], F32R)
                g_lo = alloc(ffn, "g_lo", [P, 4, S], F32R)
                ua = [alloc(ffn, f"ua{i}", [P, S]) for i in range(2)]
                ub = [alloc(ffn, f"ub{i}", [P, S]) for i in range(2)]
        rec = ExitStack()
        with rec:
            sig = [alloc(rec, f"sig{i}", [P, S]) for i in range(3)]
            qh = alloc(rec, "qh", [P, S])
            kh = alloc(rec, "kh", [P, S])
            G = alloc(rec, "G", [P, S])
            vn = alloc(rec, "vn", [P, TT, P])
            AT = alloc(rec, "AT", [P, TT, P])
            oT = alloc(rec, "oT", [P, REC_HEADS, S])
            mask = alloc(rec, "mask", [P, LEVELS, P], U8)
            restart = alloc(rec, "restart", [P, S], U8)
            lb = alloc(rec, "lb", [P, REC_HEADS])
            one_minus_lb = alloc(rec, "one_minus_lb", [P, REC_HEADS])
            X = [alloc(rec, f"X{i}", [P, S]) for i in range(2)]
            q_decay = alloc(rec, "q_decay", [P, S])
            state = alloc(rec, "state", [P, TT, P])
            g_last = alloc(rec, "g_last", [P, TT])

        psum = [ctx.enter_context(nc.psum_tensor(f"ps{i}", [P, S], F32)) for i in range(4)]

        def mod_col(layer, which, tile=0, n=1):
            c = layer * 6 * KT + which * KT + tile
            return mod[:, c:c + n]

        class WeightStream:

            def __init__(self, name, base, first=0, gap=0):
                self.base, self.first, self.gap = base, first, gap
                self.raw_ready = [sem(f"{name}_raw_ready{i}") for i in range(RAW_RING)]
                self.hi_ready = sem(f"{name}_w_hi_ready")
                self.lo_ready = sem(f"{name}_w_lo_ready")

            def nth(self, n):
                return n - self.gap if self.gap and n >= self.first else n

            def load(self, sp, n, it=None, per=0):
                r = self.nth(n)
                sp.wait_ge(self.lo_ready, at(it, per, r + 1))
                if it is None:
                    src = w_tiles[self.base + r, :, :]
                else:
                    src = w_tiles[bass.ds(it * per + (self.base + r), 1), :, :]\
                        .rearrange("a p n -> (a p) n")
                sp.dma_start(w_raw[n % RAW_RING][:].rearrange("p k n -> p (k n)"), src)\
                    .then_inc(self.raw_ready[n % RAW_RING], 16)

            def split_hi(self, act, n, released, value, it=None, per=0):
                act.wait_ge(self.raw_ready[n % RAW_RING],
                            at(it, 16 * per // RAW_RING, 16 * (self.nth(n) // RAW_RING + 1)))
                if value is not None:
                    act.wait_ge(released, value)
                act.activation(w_hi[n % W_RING][:], w_raw[n % RAW_RING][:], ACT.Copy)\
                    .then_inc(self.hi_ready, 1)

            def credit(self, dve):
                dve.sem_inc(self.lo_ready, RAW_RING)

            def split_lo(self, dve, n, it=None, per=0):
                dve.wait_ge(self.hi_ready, at(it, per, self.nth(n) + 1))
                dve.tensor_tensor(w_lo[n % W_RING][:], w_raw[n % RAW_RING][:],
                                  w_hi[n % W_RING][:].bitcast(F32), ALU.subtract)\
                    .then_inc(self.lo_ready, 1)

            def wait(self, pe, n, it=None, per=0):
                pe.wait_ge(self.lo_ready, at(it, per, self.nth(n) + 1 + RAW_RING))

        def product(pe, out, parts):
            last = len(parts) - 1
            for k, (wh, wl, mh, ml) in enumerate(parts):
                for j, (w, m) in enumerate(((wh, mh), (wh, ml), (wl, mh))):
                    for h in range(2):
                        cut = slice(h * HALF, (h + 1) * HALF)
                        ins = pe.matmul(out[:, cut], w, m[:, cut], start=(k == 0 and j == 0),
                                        stop=(k == last and j == 2))
            return ins

        def full_parts(n):
            s = n % W_RING
            return [(w_hi[s][:, k], w_lo[s][:, k], in_hi[:, k], in_lo[:, k]) for k in range(KT)]

        class Norm:

            def __init__(self, name, sq, scaled):
                self.sq, self.scaled = sq, scaled
                self.sq_ready = sem(f"{name}_sq_ready")
                self.sq_used = sem(f"{name}_sq_used")
                self.log_ready = sem(f"{name}_log_ready")
                self.rstd_ready = sem(f"{name}_rstd_ready")
                self.scaled_ready = sem(f"{name}_scaled_ready")
                self.hi_ready = sem(f"{name}_in_hi_ready")
                self.in_ready = sem(f"{name}_in_ready")

            def act_stats(self, act, ss):
                for k in range(KT):
                    if k >= 2:
                        act.wait_ge(self.sq_used, k - 1)
                    act.activation(self.sq[k % 2], x[:, k], ACT.Square).then_inc(self.sq_ready, 1)
                act.wait_ge(self.sq_used, KT)
                act.activation(rstd[:], ss[:], ACT.Ln, bias=eps_col[:, 0:1], scale=1.0 / D)\
                    .then_inc(self.log_ready, 1)
                act.wait_ge(self.log_ready, 1)
                act.activation(rstd[:], rstd[:], ACT.Exp, scale=-0.5).then_inc(self.rstd_ready, 1)

            def pe_stats(self, pe, ss):
                for k in range(KT):
                    pe.wait_ge(self.sq_ready, k + 1)
                    for h in range(2):
                        cut = slice(h * HALF, (h + 1) * HALF)
                        ins = pe.matmul(ss[:, cut], ones[:], self.sq[k % 2][:, cut],
                                        start=(k == 0), stop=(k == KT - 1))
                    ins.then_inc(self.sq_used, 1)

            def act_apply(self, act, shift):
                for k in range(KT):
                    act.wait_ge(self.scaled_ready, k + 1)
                    act.activation(in_hi[:, k], self.scaled[k % 2], ACT.Identity,
                                   bias=shift[:, k:k + 1]).then_inc(self.hi_ready, 1)

            def dve_apply(self, dve, g, shift):
                dve.wait_ge(self.rstd_ready, 1)
                for k in range(KT):
                    if k >= 2:
                        dve.wait_ge(self.in_ready, k - 1)
                    dve.scalar_tensor_tensor(self.scaled[k % 2], x[:, k], g[:, k:k + 1], rstd[:],
                                             ALU.mult, ALU.mult).then_inc(self.scaled_ready, 1)
                    if k >= 1:
                        self.dve_rest(dve, k - 1, shift)
                self.dve_rest(dve, KT - 1, shift)

            def dve_rest(self, dve, k, shift):
                dve.wait_ge(self.hi_ready, k + 1)
                dve.scalar_tensor_tensor(in_lo[:, k], self.scaled[k % 2], shift[:, k:k + 1],
                                         in_hi[:, k].bitcast(F32), ALU.add, ALU.subtract)\
                    .then_inc(self.in_ready, 1)

        class Ada:

            TILES = 6 * KT

            def __init__(self, name, layer, raw, acc, cols):
                self.layer, self.raw, self.acc, self.cols = layer, raw, acc, cols
                self.landed = [sem(f"{name}_ada_landed{i}") for i in range(2)]
                self.acc_ready = sem(f"{name}_ada_acc_ready")
                self.step_sem = sem(f"{name}_ada_step")
                self.col_ready = sem(f"{name}_ada_col_ready")
                self.col_taken = sem(f"{name}_ada_col_taken")
                self.mod_ready = sem(f"{name}_mod_ready")

            def load(self, sp, pair):
                for i in range(2):
                    if isinstance(pair, int):
                        src = ada_tiles[self.layer * self.TILES + 2 * pair + i, :, :]
                    else:
                        sp.wait_ge(self.acc_ready, pair * 2 + (i + 1 - 2))
                        src = ada_tiles[bass.ds(pair * 2 + (self.layer * self.TILES + i), 1), :, :]
                        src = src.rearrange("a p n -> (a p) n")
                    sp.dma_start(self.raw[i], src).then_inc(self.landed[i], 16)

            def sync(self, sp):
                self.load(sp, 0)
                with sp.Fori(1, self.TILES // 2) as pair:
                    self.load(sp, pair)

            def sum_tiles(self, dve, steps, it):
                for i in range(2):
                    dve.wait_ge(self.landed[i], at(it, 16, 16))
                    w = self.raw[i].rearrange("p (k n) -> p k n", k=KT)
                    steps.link(dve.tensor_scalar(self.acc[i], w[:, 0], cond[:, 0:1], None, ALU.mult))
                    for k in range(1, KT):
                        ins = dve.scalar_tensor_tensor(self.acc[i], w[:, k], cond[:, k:k + 1],
                                                       self.acc[i], ALU.mult, ALU.add)
                        if k < KT - 1:
                            steps.link(ins)
                        else:
                            ins.then_inc(self.acc_ready, 1)

            def tensor(self, pe):
                with pe.Fori(0, self.TILES // 2) as it:
                    for i in range(2):
                        pe.wait_ge(self.acc_ready, it * 2 + (i + 1))
                        pe.matmul(self.cols[:, i * HALF:i * HALF + 1], self.acc[i], ones[:, 0:1],
                                  start=True, stop=True).then_inc(self.col_ready, 1)

            def vector(self, dve):
                steps = Steps(dve, self.step_sem)
                base = self.layer * self.TILES
                with dve.Fori(0, self.TILES // 2) as it:
                    steps.enter(it, 2 * (KT - 1))
                    self.sum_tiles(dve, steps, it)
                    for i in range(2):
                        dve.wait_ge(self.col_ready, it * 2 + (i + 1))
                        dve.tensor_copy(mod[:, bass.ds(it * 2 + (base + i), 1)],
                                        self.cols[:, i * HALF:i * HALF + 1]).then_inc(self.col_taken, 1)
                    steps.leave(self.TILES // 2)
                dve.wait_ge(self.col_taken, self.TILES)
                m = mod[:, base:base + self.TILES]
                dve.tensor_tensor(m, m, vec[:, C_ADA_B + base:C_ADA_B + base + self.TILES], ALU.add)\
                    .then_inc(self.mod_ready, 1)
                dve.wait_ge(self.mod_ready, 1)
                for which, col in ((0, C_NORM1), (1, C_NORM2)):
                    g = gain[:, (2 * self.layer + which) * KT:(2 * self.layer + which + 1) * KT]
                    dve.scalar_tensor_tensor(
                        g, mod_col(self.layer, 3 * which + 1, 0, KT), 1.0,
                        vec[:, col + self.layer * KT:col + (self.layer + 1) * KT], ALU.add, ALU.mult)\
                        .then_inc(self.mod_ready, 1)
                dve.wait_ge(self.mod_ready, 3)

        def setup_phase():
            s_const = sem("const_landed")
            s_x = sem("x_landed")
            s_cond = sem("cond_ready")
            s_ones = sem("ones_ready")
            s_pos = sem("pos_step")
            s_ang = sem("angle_ready")
            s_rope = sem("rope_ready")
            norm = Norm("n0", [t[:] for t in tmp], [t[:] for t in tmp])
            ada = [Ada(f"s{layer}", layer, [q_raw[:, 4 * layer], q_raw[:, 4 * layer + 1]],
                       [q_raw[:, 4 * layer + 2, 0:P], q_raw[:, 4 * layer + 3, 0:P]], psum[1 + layer])
                   for layer in range(DEPTH)]
            pos_i = kv_raw[:, 0].bitcast(I32)
            ang, turns = kv_raw[:, 1], rstd
            with nc.Block() as block:
                @block.sync
                def _(sp):
                    sp.dma_start(vec[:], vec_in).then_inc(s_const, 16)
                    sp.dma_start(ident[:], ident_in).then_inc(s_const, 16)
                    sp.dma_start(pos_i, positions.partition_broadcast(P)).then_inc(s_const, 16)
                    sp.dma_start(x[:], xT).then_inc(s_x, 16)
                    for a in ada:
                        a.sync(sp)

                @block.gpsimd
                def _(pool):
                    pool.memset(ones[:], 1.0).then_inc(s_ones, 1)
                    pool.memset(eps_col[:], EPS).then_inc(s_ones, 1)

                @block.scalar
                def _(act):
                    act.wait_ge(s_const, 48)
                    act.activation(cond[:], vec[:, C_COND:C_COND + KT], ACT.Silu).then_inc(s_cond, 1)
                    act.wait_ge(s_ang, 1)
                    act.activation(rope_sin[:], rope_sin[:], ACT.Sin).then_inc(s_rope, 1)
                    act.wait_ge(s_ang, 2)
                    act.activation(rope_cos[:], rope_cos[:], ACT.Sin).then_inc(s_rope, 1)
                    act.wait_ge(s_x, 16)
                    act.wait_ge(s_ones, 2)
                    norm.act_stats(act, psum[0])
                    norm.act_apply(act, mod_col(0, 0, 0, KT))

                @block.tensor
                def _(pe):
                    pe.wait_ge(s_ones, 2)
                    norm.pe_stats(pe, psum[0])
                    for a in ada:
                        a.tensor(pe)

                @block.vector
                def _(dve):
                    pos = Steps(dve, s_pos)
                    dve.wait_ge(s_const, 48)
                    pos.link(dve.tensor_copy(ang, pos_i))
                    pos.link(dve.tensor_scalar(ang, ang, vec[:, C_FREQ:C_FREQ + 1], None, ALU.mult))
                    magic = 1.5 * 2.0 ** 23
                    parts = two_pi_parts()

                    def reduce_angle(dst, src, unit, shift):
                        pos.link(dve.tensor_scalar(turns[:], src, 1.0 / (2 * np.pi * unit), shift,
                                                   ALU.mult, ALU.add))
                        pos.link(dve.tensor_scalar(turns[:], turns[:], magic, None, ALU.add))
                        pos.link(dve.tensor_scalar(turns[:], turns[:], magic, None, ALU.subtract))
                        for c in parts:
                            pos.link(dve.scalar_tensor_tensor(dst, turns[:], -c * unit, src,
                                                              ALU.mult, ALU.add))
                            src = dst

                    pi32 = 3.1415925
                    reduce_angle(ang, ang, 4096.0, 0.0)
                    reduce_angle(rope_sin[:], ang, 1.0, 0.0)
                    dve.tensor_scalar(rope_sin[:], rope_sin[:], pi32, -pi32, ALU.min, ALU.max)\
                        .then_inc(s_ang, 1)
                    reduce_angle(rope_cos[:], ang, 1.0, 0.25)
                    pos.link(dve.tensor_scalar(rope_cos[:], rope_cos[:], float(np.pi / 2), None, ALU.add))
                    dve.tensor_scalar(rope_cos[:], rope_cos[:], pi32, -pi32, ALU.min, ALU.max)\
                        .then_inc(s_ang, 1)
                    dve.wait_ge(s_cond, 1)
                    for a in ada:
                        a.vector(dve)
                    dve.wait_ge(s_rope, 1)
                    pos.link(dve.tensor_scalar(rope_sin[:], rope_sin[:], vec[:, C_SIGN:C_SIGN + 1],
                                                 None, ALU.mult))
                    norm.dve_apply(dve, gain[:, 0:KT], mod_col(0, 0, 0, KT))

        def qkv_phase():
            ws = WeightStream("qkv", W_QKV)
            done, evac = sem("qkv_done"), sem("qkv_evac")
            with nc.Block() as block:
                @block.sync
                def _(sp):
                    for n in range(N_QKV):
                        ws.load(sp, n)

                @block.vector
                def _(dve):
                    ws.credit(dve)
                    for n in range(N_QKV):
                        ws.split_lo(dve, n)

                @block.tensor
                def _(pe):
                    for n in range(N_QKV):
                        ws.wait(pe, n)
                        if n >= 4:
                            pe.wait_ge(evac, n - 3)
                        product(pe, psum[n % 4], full_parts(n)).then_inc(done, 1)

                @block.scalar
                def _(act):
                    def take(n):
                        act.wait_ge(done, n + 1)
                        dst = q_raw[:, n] if n < KT else kv_raw[:, n - KT]
                        act.activation(dst, psum[n % 4][:], ACT.Copy).then_inc(evac, 1)

                    for n in range(N_QKV):
                        ws.split_hi(act, n, done, n - W_RING + 1 if n >= W_RING else None)
                        if n >= 2:
                            take(n - 2)
                    take(N_QKV - 2)
                    take(N_QKV - 1)

        def out_proj_phase(name, base, gate, prepare=None):
            ws = WeightStream(name, base)
            done, evac = sem(f"{name}_done"), sem(f"{name}_evac")
            with nc.Block() as block:
                @block.sync
                def _(sp):
                    if prepare:
                        prepare["sync"](sp)
                    for n in range(N_OUT):
                        ws.load(sp, n)

                @block.scalar
                def _(act):
                    if prepare:
                        prepare["scalar"](act)
                    for n in range(N_OUT):
                        ws.split_hi(act, n, done, n - W_RING + 1 if n >= W_RING else None)

                @block.vector
                def _(dve):
                    ws.credit(dve)
                    if prepare:
                        prepare["vector"](dve)

                    def take(n):
                        dve.wait_ge(done, n + 1)
                        dve.scalar_tensor_tensor(x[:, n], psum[n % 4][:], gate[:, n:n + 1], x[:, n],
                                                 ALU.mult, ALU.add).then_inc(evac, 1)

                    for n in range(N_OUT):
                        ws.split_lo(dve, n)
                        if n >= 2:
                            take(n - 2)
                    take(N_OUT - 2)
                    take(N_OUT - 1)

                @block.tensor
                def _(pe):
                    if prepare:
                        prepare["tensor"](pe)
                    for n in range(N_OUT):
                        ws.wait(pe, n)
                        if n >= 4:
                            pe.wait_ge(evac, n - 3)
                        product(pe, psum[n % 4], full_parts(n)).then_inc(done, 1)

        AT_TURN = 4
        AT_TURNS = (N_CHUNKS - 1) // AT_TURN
        NB = N_HEADS // 2
        at_ctx = ExitStack()
        with at_ctx:
            for n, w in (("at_x", KT), ("at_q", KT), ("at_kv", 2), ("at_cos", 1), ("at_sin", 1)):
                alloc(at_ctx, n, [P, w, S])
            q_rot = alloc(at_ctx, "q_rot", [P, KT, CHUNK])
            q_swap = alloc(at_ctx, "q_swap", [P, KT, CHUNK])
            k_rot = alloc(at_ctx, "k_rot", [P, AT_TURN, CHUNK])
            k_swap = alloc(at_ctx, "k_swap", [P, CHUNK])
            v_keys = alloc(at_ctx, "v_keys", [P, 2, CHUNK])
            v_win = alloc(at_ctx, "v_win", [P, P])
            probsT = alloc(at_ctx, "probsT", [P, S])
            row_max, sink_exp, neg_max, row_sum, inv_den = (
                alloc(at_ctx, n, [P, NB]) for n in ("row_max", "sink_exp", "neg_max", "row_sum", "inv_den"))

        def attention_phase():
            s_rot = sem("at_rope_step")
            s_in = sem("at_chunk_rotated")
            s_qk = sem("at_scores_ready")
            s_mx = sem("at_max_step")
            s_bias = sem("at_bias_ready")
            s_exp = sem("at_exp_ready")
            s_esink = sem("at_sink_exp_ready")
            s_probs = sem("at_probs_ready")
            s_pT = sem("at_probs_transposed")
            s_pc = sem("at_probsT_copied")
            s_vT = sem("at_v_transposed")
            s_v = sem("at_v_copied")
            s_o = sem("at_out_ready")
            s_ohi = sem("at_out_hi")
            s_olo = sem("at_out_lo")
            sink = vec[:, C_SINK:C_SINK + NB]
            probs = w_raw[0][:]
            scores = [psum[i][:].rearrange("p (b k) -> p b k", b=NB) for i in range(2)]
            v_ps, out_ps = psum[2][:, 0:P], psum[2][:, HALF:]
            pT_ps = psum[3]
            scale = HEAD ** -0.5
            swap = [i + ROPE // 2 if i < ROPE // 2 else i - ROPE // 2 if i < ROPE else i for i in range(32)]

            def chunks(eng, body, steps=()):
                body(0, None)
                with eng.Fori(0, AT_TURNS) as it:
                    for s, k in steps:
                        s.enter(it, AT_TURN * k)
                    for c in range(AT_TURN):
                        body(1 + c, it)
                    for s, k in steps:
                        s.leave(AT_TURNS)
                for n in range(1 + AT_TURN * AT_TURNS, N_CHUNKS):
                    body(n, None)

            def keys(n):
                if n == 0:
                    return slice(0, 1), CHUNK
                lo, hi = sorted(((n - 1) % AT_TURN, n % AT_TURN))
                return slice(lo, hi + 1, hi - lo), 2 * CHUNK

            def tokens(n, it):
                return slice(n * CHUNK, (n + 1) * CHUNK) if it is None else \
                    bass.ds(it * (AT_TURN * CHUNK) + n * CHUNK, CHUNK)

            def count(n, it, k):
                return at(it, AT_TURN, n + k)

            with nc.Block() as block:
                @block.vector
                def _(dve):
                    rot, mx = Steps(dve, s_rot), Steps(dve, s_mx)

                    def rotate(n, it):
                        cut, slot = tokens(n, it), n % AT_TURN
                        cos = rope_cos[:, cut].unsqueeze(1).to_broadcast([P, KT, CHUNK])
                        sin = rope_sin[:, cut].unsqueeze(1).to_broadcast([P, KT, CHUNK])
                        if n > 0:
                            dve.wait_ge(s_qk, count(n, it, 0))
                        rot.add(dve.tensor_tensor(q_swap[:], q_raw[:, :, cut], sin, ALU.mult))
                        rot.add(dve.tensor_tensor(k_swap[:], kv_raw[:, 0, cut], rope_sin[:, cut], ALU.mult))
                        rot.add(dve.tensor_tensor(q_rot[:], q_raw[:, :, cut], cos, ALU.mult))
                        rot.add(dve.tensor_tensor(k_rot[:, slot], kv_raw[:, 0, cut], rope_cos[:, cut],
                                                  ALU.mult))
                        rot.wait()
                        if n > 0:
                            dve.wait_ge(s_vT, count(n, it, 0))
                        rot.add(dve.tensor_copy(v_keys[:, min(slot, 1)], kv_raw[:, 1, cut]))
                        if n > 0:
                            rot.add(dve.tensor_copy(v_keys[:, 1 - min(slot, 1)],
                                                    kv_raw[:, 1, tokens(n - 1, it)]))
                        rot.add(dve.stream_shuffle(q_swap[:], q_swap[:], swap))
                        rot.add(dve.stream_shuffle(k_swap[:], k_swap[:], swap))
                        rot.wait()
                        rot.add(dve.tensor_tensor(k_rot[:, slot], k_rot[:, slot], k_swap[:], ALU.add))
                        rot.wait()
                        dve.tensor_tensor(q_rot[:], q_rot[:], q_swap[:], ALU.add).then_inc(s_in, 1)

                    def body(n, it):
                        w = keys(n)[1]
                        rotate(n, it)
                        dve.wait_ge(s_qk, count(n, it, 1))
                        mx.link(dve.tensor_reduce(row_max[:], scores[n % 2][:, :, 0:w], AX.X, ALU.max))
                        mx.link(dve.scalar_tensor_tensor(row_max[:], row_max[:], scale, sink,
                                                         ALU.mult, ALU.max))
                        mx.link(dve.tensor_tensor(sink_exp[:], sink, row_max[:], ALU.subtract))
                        if n > 0:
                            dve.wait_ge(s_pT, count(n, it, 0))
                        dve.tensor_scalar(neg_max[:], row_max[:], -1.0, None, ALU.mult).then_inc(s_bias, 1)
                        dve.wait_ge(s_esink, count(n, it, 1))
                        mx.link(dve.tensor_tensor(inv_den[:], row_sum[:], sink_exp[:], ALU.add))
                        mx.link(dve.reciprocal(inv_den[:], inv_den[:]))
                        pr = probs[:, :, 0:w]
                        dve.tensor_tensor(pr, pr, inv_den[:].unsqueeze(2).to_broadcast([P, NB, w]),
                                          ALU.mult).then_inc(s_probs, 1)
                        dve.wait_ge(s_ohi, count(n, it, 1))
                        cut = tokens(n, it)
                        dve.tensor_tensor(in_lo[:, :, cut], out_ps.rearrange("p (t q) -> p t q", t=KT),
                                          in_hi[:, :, cut].bitcast(F32), ALU.subtract).then_inc(s_olo, 1)

                    chunks(dve, body, ((rot, 9), (mx, 5)))

                @block.tensor
                def _(pe):
                    def body(n, it):
                        slots, w = keys(n)
                        sc = scores[n % 2]
                        pe.wait_ge(s_in, count(n, it, 1))
                        if n > 1:
                            pe.wait_ge(s_exp, count(n, it, -1))
                        elif n == 1 and it is not None:
                            pe.wait_ge(s_exp, count(n, it, 0))
                        for b in range(NB):
                            rows = slice(HEAD * (b // 4), HEAD * (b // 4) + HEAD)
                            t = 2 * (b % 4)
                            ins = pe.matmul(sc[:, b, 0:w], q_rot[rows, t:t + 2], k_rot[rows, slots],
                                            start=True, stop=True)
                        ins.then_inc(s_qk, 1)
                        if n > 0:
                            pe.wait_ge(s_v, count(n, it, 0))
                        pe.transpose(v_ps[0:w], v_keys[:].rearrange("p a b -> p (a b)")[:, 0:w], ident[:])\
                            .then_inc(s_vT, 1)
                        pe.wait_ge(s_probs, count(n, it, 1))
                        if n > 0:
                            pe.wait_ge(s_pc, count(n, it, 0))
                        for b in range(NB):
                            ins = pe.transpose(pT_ps[0:w, b * P:(b + 1) * P], probs[:, b, 0:w], ident[:])
                        ins.then_inc(s_pT, 1)
                        pe.wait_ge(s_pc, count(n, it, 1))
                        pe.wait_ge(s_v, count(n, it, 1))
                        if n > 0:
                            pe.wait_ge(s_olo, count(n, it, 0))
                        for kv in range(2):
                            rows = slice(HEAD * kv, HEAD * kv + HEAD)
                            ins = pe.matmul(out_ps[rows, :], v_win[0:w, rows],
                                            probsT[0:w, kv * HALF:(kv + 1) * HALF], start=True, stop=True)
                        ins.then_inc(s_o, 1)

                    chunks(pe, body)

                @block.scalar
                def _(act):
                    def body(n, it):
                        w = keys(n)[1]
                        if n > 0:
                            act.wait_ge(s_o, count(n, it, 0))
                        act.wait_ge(s_vT, count(n, it, 1))
                        act.activation(v_win[0:w, :], v_ps[0:w], ACT.Copy).then_inc(s_v, 1)
                        act.wait_ge(s_bias, count(n, it, 1))
                        for b in range(NB):
                            ins = act.activation(probs[:, b, 0:w], scores[n % 2][:, b, 0:w], ACT.Exp,
                                                 bias=neg_max[:, b:b + 1], scale=scale,
                                                 accum_out=row_sum[:, b:b + 1])
                        ins.then_inc(s_exp, 1)
                        act.activation(sink_exp[:], sink_exp[:], ACT.Exp).then_inc(s_esink, 1)
                        act.wait_ge(s_pT, count(n, it, 1))
                        act.activation(probsT[0:w, :], pT_ps[0:w, :], ACT.Copy).then_inc(s_pc, 1)
                        act.wait_ge(s_o, count(n, it, 1))
                        act.activation(in_hi[:, :, tokens(n, it)],
                                       out_ps.rearrange("p (t q) -> p t q", t=KT),
                                       ACT.Copy).then_inc(s_ohi, 1)

                    chunks(act, body)

        def ffn_phase(layer, base):
            name = f"f{layer}"
            norm = Norm(name, [ua[0][:], ub[0][:]], [ua[1][:], ub[1][:]])
            done = sem(f"{name}_job_done")
            taken = sem(f"{name}_job_taken")
            s_tap = sem(f"{name}_tap_ready")
            s_cs = sem(f"{name}_conv_step")
            s_silu = sem(f"{name}_silu_ready")
            s_gate = sem(f"{name}_gated_ready")
            s_ghi = sem(f"{name}_g_hi_ready")
            s_glo = sem(f"{name}_g_lo_ready")
            gate2 = mod_col(layer, 5, 0, KT)
            cw = C_CONV_W + layer * 6 * FT
            cb = C_CONV_B + layer * 2 * FT
            GW, GJ = 6, 4 + KT
            GAP = 2
            PW, PJ, PH = 2 * GW, 2 * GJ, 4
            ws = WeightStream(name, base, first=4, gap=GAP)
            STEPS = 2 * 2 * 2

            def groups(eng, hidden, output, skip=None, steps=()):
                hidden(0, 0, 0, None)
                if skip:
                    skip()
                with eng.Fori(0, (GROUPS - 1) // 2) as it:
                    for s, k in steps:
                        s.enter(it, k)
                    for g in (1, 2):
                        hidden(g, GW * g, GJ * g, it)
                        output(g - 1, GW * g + 4, GJ * g + 4, it)
                    for s, k in steps:
                        s.leave((GROUPS - 1) // 2)
                output(GROUPS - 1, GW * GROUPS, GJ * GROUPS, None)

            def released(n, it):
                g, i = divmod(n, GW)
                if n < W_RING:
                    return None
                if n == GW * GROUPS or n == GW * GROUPS + 1:
                    return GJ * (GROUPS - 1) + 3 + i
                return at(it, PJ, (GJ * (g - 1) + 3, GJ * (g - 1) + 4, GJ * g, GJ * g,
                                   GJ * g + 1, GJ * g + 2)[i])

            def col(start, f, it):
                return vec[:, start + f:start + f + 1] if it is None else \
                    vec[:, bass.ds(it * PH + (start + f), 1)]

            RING = len(psum)

            with nc.Block() as block:
                @block.sync
                def _(sp):
                    def load(k):
                        return lambda g, n, j, it: [ws.load(sp, n + i, it, PW) for i in range(k)]
                    groups(sp, load(4), load(2))

                @block.tensor
                def _(pe):
                    norm.pe_stats(pe, psum[3])
                    pe.wait_ge(norm.in_ready, KT)

                    def job(j, it, parts):
                        if j >= RING:
                            pe.wait_ge(taken, at(it, PJ, j - RING + 1))
                        product(pe, psum[j % RING], parts).then_inc(done, 1)

                    def hidden(g, n, j, it):
                        for i in range(4):
                            ws.wait(pe, n + i, it, PW)
                            job(j + i, it, full_parts(n + i))

                    def output(g, n, j, it):
                        ws.wait(pe, n, it, PW)
                        ws.wait(pe, n + 1, it, PW)
                        pe.wait_ge(s_glo, at(it, PH, 2 * g + 2))
                        for d in range(KT):
                            job(j + d, it, [(w_hi[(n + i) % W_RING][:, d], w_lo[(n + i) % W_RING][:, d],
                                             g_hi[:, (2 * g + i) % 4], g_lo[:, (2 * g + i) % 4])
                                            for i in range(2)])

                    groups(pe, hidden, output, lambda: pe.drain().then_inc(done, KT))

                @block.scalar
                def _(act):
                    def split(n, it):
                        ws.split_hi(act, n, done, released(n, it), it, PW)

                    split(0, None)
                    split(1, None)
                    norm.act_stats(act, psum[3])
                    norm.act_apply(act, mod_col(layer, 3, 0, KT))

                    def tap(side, f, j, it):
                        act.wait_ge(done, at(it, PJ, j + 1))
                        if f >= 2:
                            act.wait_ge(s_glo, at(it, PH, f - 1))
                        act.activation((ua, ub)[side][f % 2][:], psum[j % RING][:], ACT.Identity,
                                       bias=col(cb + side * FT, f, it),
                                       scale=col(cw + (2 * 2 + side) * FT, f, it)).then_inc(s_tap, 1)

                    def silu(f, j, it):
                        act.wait_ge(taken, at(it, PJ, j + 1))
                        act.activation(ua[f % 2][:], ua[f % 2][:], ACT.Silu).then_inc(s_silu, 1)

                    def gated_hi(f, it):
                        act.wait_ge(s_gate, at(it, PH, f + 1))
                        act.activation(g_hi[:, f % 4], ua[f % 2][:], ACT.Copy).then_inc(s_ghi, 1)

                    def hidden(g, n, j, it):
                        f = 2 * g
                        split(n + 2, it)
                        split(n + 3, it)
                        tap(0, f, j, it)
                        if g > 0:
                            split(n + 4, it)
                        tap(1, f, j + 1, it)
                        silu(f, j, it)
                        if g > 0:
                            split(n + 5, it)
                        gated_hi(f, it)
                        tap(0, f + 1, j + 2, it)
                        tap(1, f + 1, j + 3, it)
                        silu(f + 1, j + 2, it)

                    def output(g, n, j, it):
                        gated_hi(2 * g + 3, it)
                        split(n + 2, it)
                        split(n + 3, it)

                    groups(act, hidden, lambda g, n, j, it: output(g, n, j, it) if it is not None else None,
                           lambda: output(-1, GW - 2, 0, None))

                @block.vector
                def _(dve):
                    ws.credit(dve)
                    ws.split_lo(dve, 0)
                    ws.split_lo(dve, 1)
                    norm.dve_apply(dve, gain[:, (2 * layer + 1) * KT:(2 * layer + 2) * KT],
                                   mod_col(layer, 3, 0, KT))
                    cs = Steps(dve, s_cs)

                    def earlier_taps(side, f, j, it):
                        ps, dst = psum[j % RING], (ua, ub)[side][f % 2]
                        dve.wait_ge(s_tap, at(it, 2 * PH, 2 * f + side + 1))
                        cs.link(dve.scalar_tensor_tensor(
                            dst[:, 1:], ps[:, :S - 1], col(cw + (2 * 1 + side) * FT, f, it),
                            dst[:, 1:], ALU.mult, ALU.add))
                        dve.scalar_tensor_tensor(
                            dst[:, 2:], ps[:, :S - 2], col(cw + side * FT, f, it),
                            dst[:, 2:], ALU.mult, ALU.add).then_inc(taken, 1)

                    def gated(f, j, it):
                        dve.wait_ge(s_silu, at(it, PH, f + 1))
                        dve.wait_ge(taken, at(it, PJ, j + 1))
                        dve.tensor_tensor(ua[f % 2][:], ua[f % 2][:], ub[f % 2][:], ALU.mult)\
                            .then_inc(s_gate, 1)

                    def gated_lo(f, it):
                        dve.wait_ge(s_ghi, at(it, PH, f + 1))
                        dve.tensor_tensor(g_lo[:, f % 4], ua[f % 2][:], g_hi[:, f % 4].bitcast(F32),
                                          ALU.subtract).then_inc(s_glo, 1)

                    def hidden(g, n, j, it):
                        f = 2 * g
                        ws.split_lo(dve, n + 2, it, PW)
                        ws.split_lo(dve, n + 3, it, PW)
                        earlier_taps(0, f, j, it)
                        if g > 0:
                            ws.split_lo(dve, n + 4, it, PW)
                        earlier_taps(1, f, j + 1, it)
                        gated(f, j + 1, it)
                        if g > 0:
                            ws.split_lo(dve, n + 5, it, PW)
                        gated_lo(f, it)
                        earlier_taps(0, f + 1, j + 2, it)
                        earlier_taps(1, f + 1, j + 3, it)

                    def output(g, n, j, it):
                        between = {0: lambda: gated(2 * g + 3, j - 1, it),
                                   1: lambda: gated_lo(2 * g + 3, it),
                                   2: lambda: ws.split_lo(dve, n + 2, it, PW),
                                   3: lambda: ws.split_lo(dve, n + 3, it, PW)}
                        for d in range(KT):
                            if g >= 0:
                                dve.wait_ge(done, at(it, PJ, j + d + 1))
                                dve.scalar_tensor_tensor(x[:, d], psum[(j + d) % RING][:],
                                                         gate2[:, d:d + 1], x[:, d],
                                                         ALU.mult, ALU.add).then_inc(taken, 1)
                            if d in between and g < GROUPS - 1:
                                between[d]()

                    def skip():
                        output(-1, GW - 2, 4, None)
                        dve.drain().then_inc(taken, KT)

                    groups(dve, hidden, output, skip, ((cs, STEPS),))

        def rec_norm_phase():
            norm = Norm("rn", [ua[0][:], ub[0][:]], [ua[1][:], ub[1][:]])
            s_spill = sem("x_spilled")
            with nc.Block() as block:
                @block.sync
                def _(sp):
                    sp.dma_start(x_spill, x[:]).then_inc(s_spill, 16)
                    sp.wait_ge(s_spill, 16)

                @block.scalar
                def _(act):
                    norm.act_stats(act, psum[3])
                    norm.act_apply(act, mod_col(1, 0, 0, KT))

                @block.tensor
                def _(pe):
                    norm.pe_stats(pe, psum[3])

                @block.vector
                def _(dve):
                    norm.dve_apply(dve, gain[:, 2 * KT:3 * KT], mod_col(1, 0, 0, KT))

        def rec_phase():
            ws = WeightStream("rec", W_REC)
            N_W = 4
            (J_GATE, J_Q, J_F, J_V, J_VT, J_L0) = range(6)
            J_KT = J_L0 + LEVELS + 1
            J_UPD, J_OUT, J_SS, N_J = J_KT + 1, J_KT + 2, J_KT + 3, J_KT + 4
            LEVEL_SLOT = (1, 2, 3, 1, 2, 3, 1, 2)
            done = sem("rec_result_done")
            free = [sem(f"rec_psum{i}_free") for i in range(4)]
            s_masks = sem("rec_masks_landed")
            s_const = sem("rec_const_ready")
            s_sig = sem("rec_sigmoid_ready")
            s_vraw = sem("rec_vT_ready")
            s_v = sem("rec_v_ready")
            s_f = sem("rec_f_ready")
            s_ln = sem("rec_ln_ready")
            s_G = sem("rec_G_ready")
            s_eg = sem("rec_exp_G_ready")
            s_d = sem("rec_exponent_ready")
            s_e = sem("rec_decay_ready")
            s_x = sem("rec_level_operand_ready")
            s_kn = sem("rec_k_natural_ready")
            s_sq = sem("rec_squares_ready")
            s_ms = sem("rec_mean_square_read")
            s_rms = sem("rec_rstd_ready")
            s_step = sem("rec_dve_step")
            s_out = sem("rec_out_ready")
            LN2 = float(np.log(2.0))
            vT = state[:].rearrange("p c n -> p (c n)")
            kn = sig[2][:].rearrange("p (c n) -> p c n", c=TT)

            def tiles(t):
                return t[:].rearrange("p (c n) -> p c n", c=TT)

            def head(t, it):
                return t[:, bass.ds(it, 1), :].rearrange("p a s -> p (a s)")

            with nc.Block() as block:
                @block.sync
                def _(sp):
                    sp.dma_start(AT[:, 0:LEVELS], masks_in).then_inc(s_masks, 16)
                    with sp.Fori(0, REC_HEADS) as it:
                        for n in range(N_W):
                            ws.load(sp, n, it, N_W)

                @block.gpsimd
                def _(pool):
                    pool.memset(restart[:], 1).then_inc(s_const, 1)
                    pool.wait_ge(s_const, 1)
                    pool.memset(restart[:].rearrange("p (c n) -> p c n", c=TT)[:, :, 0:1], 0)\
                        .then_inc(s_const, 1)

                @block.tensor
                def _(pe):
                    for i in range(4):
                        pe.sem_inc(free[i], 1)
                    pe.sem_inc(s_ms, 1)
                    with pe.Fori(0, REC_HEADS) as it:
                        def projection(n, slot):
                            ws.wait(pe, n, it, N_W)
                            product(pe, psum[slot], full_parts(n)).then_inc(done, 1)

                        pe.wait_ge(free[0], it * 2 + 1)
                        projection(J_GATE, 0)
                        pe.wait_ge(s_ms, it + 1)
                        projection(J_Q, 1)
                        pe.wait_ge(free[2], it * 3 + 1)
                        projection(J_F, 2)
                        pe.wait_ge(free[3], it * 3 + 1)
                        projection(J_V, 3)

                        def per_tile(slot, op):
                            for c in range(TT):
                                ins = op(c, psum[slot][:, c * P:(c + 1) * P])
                            ins.then_inc(done, 1)

                        pe.wait_ge(free[0], it * 2 + 2)
                        pe.wait_ge(s_vraw, it + 1)
                        per_tile(0, lambda c, o: pe.transpose(o, vT[:, c * P:(c + 1) * P], ident[:]))
                        pe.wait_ge(s_f, it + 1)
                        pe.wait_ge(free[1], it * 4 + 2)
                        per_tile(1, lambda c, o: pe.matmul(o, tiles(kh)[:, c], tiles(qh)[:, c],
                                                           start=True, stop=True))
                        for l in range(1, LEVELS + 1):
                            slot = LEVEL_SLOT[l]
                            pe.wait_ge(s_x, it * (LEVELS + 1) + l)
                            if l >= 3:
                                pe.wait_ge(free[slot], it * (4 if slot == 1 else 3) +
                                           {3: 3, 4: 2, 5: 2, 6: 4, 7: 3}[l])
                            xl = tiles(X[l % 2])
                            per_tile(slot, lambda c, o: pe.matmul(o, xl[:, c], xl[:, c],
                                                                  start=True, stop=True))
                        pe.wait_ge(s_x, it * (LEVELS + 1) + LEVELS + 1)
                        pe.wait_ge(s_v, it + 1)
                        xl = tiles(X[(LEVELS + 1) % 2])
                        per_tile(0, lambda c, o: pe.transpose(o, xl[:, c], ident[:]))
                        pe.wait_ge(s_kn, it + 1)
                        pe.wait_ge(free[3], it * 3 + 3)
                        per_tile(3, lambda c, o: pe.matmul(o, kn[:, c], vn[:, c], start=True, stop=True))
                        pe.wait_ge(free[2], it * 3 + 4)
                        pe.wait_ge(free[3], it * 3 + 4)

                        def output(c, o):
                            ins = pe.matmul(o, vn[:, c], AT[:, c], start=True, stop=(c == 0))
                            if c > 0:
                                ins = pe.matmul(o, state[:, c], tiles(q_decay)[:, c], start=False, stop=True)
                            return ins
                        per_tile(0, output)
                        pe.wait_ge(s_sq, it + 1)
                        pe.wait_ge(free[1], it * 4 + 5)
                        for h in range(2):
                            cut = slice(h * HALF, (h + 1) * HALF)
                            ins = pe.matmul(psum[1][:, cut], ones[:], sig[1][:, cut], start=True, stop=True)
                        ins.then_inc(done, 1)

                @block.scalar
                def _(act):
                    act.wait_ge(s_const, 3)
                    act.activation(lb[:], lb[:], ACT.Exp).then_inc(s_const, 1)
                    with act.Fori(0, REC_HEADS) as it:
                        def result(j):
                            act.wait_ge(done, it * N_J + (j + 1))

                        for n in range(N_W):
                            ws.split_hi(act, n, s_ms, it + 1, it, N_W)
                        for j in (J_GATE, J_Q, J_F):
                            result(j)
                            act.activation(sig[j][:], psum[j][:], ACT.Sigmoid).then_inc(s_sig, 1)
                        result(J_V)
                        act.activation(vT, psum[3][:], ACT.Copy).then_inc(s_vraw, 1)
                        result(J_VT)
                        act.activation(vn[:], tiles(psum[0]), ACT.Copy).then_inc(s_v, 1)
                        act.wait_ge(s_f, it + 1)
                        act.activation(X[1][:], sig[2][:], ACT.Ln, scale=2.0 ** 63).then_inc(s_ln, 1)
                        act.activation(X[0][:], X[0][:], ACT.Ln).then_inc(s_ln, 1)
                        act.wait_ge(s_G, it + 1)
                        act.activation(q_decay[:], G[:], ACT.Exp).then_inc(s_eg, 1)
                        act.activation(g_last[:], tiles(G)[:, :, P - 1], ACT.Exp).then_inc(s_eg, 1)
                        for l in range(1, LEVELS + 2):
                            act.wait_ge(s_d, it * (LEVELS + 1) + l)
                            if l <= LEVELS:
                                b = X[l % 2][:].rearrange("p (b n) -> p b n", n=2 ** l)
                                half = 2 ** (l - 1)
                                act.activation(b[:, :, half:], b[:, :, half:], ACT.Exp)
                                act.activation(b[:, :, :half], b[:, :, :half], ACT.Exp, scale=-1.0)\
                                    .then_inc(s_e, 1)
                            else:
                                act.activation(X[l % 2][:], X[l % 2][:], ACT.Exp, scale=-1.0)\
                                    .then_inc(s_e, 1)
                        result(J_KT)
                        act.activation(kn, tiles(psum[0]), ACT.Copy).then_inc(s_kn, 1)
                        result(J_OUT)
                        act.activation(sig[1][:], psum[0][:], ACT.Square).then_inc(s_sq, 1)
                        result(J_SS)
                        act.activation(sig[1][:], psum[1][:], ACT.Ln, bias=eps_col[:, 0:1], scale=1.0 / P)\
                            .then_inc(s_ms, 1)
                        act.wait_ge(s_ms, it + 2)
                        act.activation(sig[1][:], sig[1][:], ACT.Exp, scale=-0.5).then_inc(s_rms, 1)

                @block.vector
                def _(dve):
                    ws.credit(dve)
                    st = Steps(dve, s_step)
                    logits = vec[:, C_LB:C_LB + REC_HEADS]
                    dve.wait_ge(s_const, 2)
                    dve.tensor_tensor(lb[:], logits, logits, ALU.subtract).then_inc(s_const, 1)
                    dve.wait_ge(s_const, 4)
                    st.link(dve.reciprocal(one_minus_lb[:], lb[:]))
                    st.link(dve.tensor_tensor(lb[:], lb[:], one_minus_lb[:], ALU.mult))
                    st.link(dve.tensor_tensor(lb[:], lb[:], lb[:], ALU.subtract))
                    st.link(dve.tensor_scalar(one_minus_lb[:], lb[:], -1.0, 1.0, ALU.mult, ALU.add))
                    dve.wait_ge(s_masks, 16)
                    st.link(dve.tensor_copy(mask[:], AT[:, 0:LEVELS]))
                    with dve.Fori(0, REC_HEADS) as it:
                        st.enter(it, 11)

                        def result(j):
                            dve.wait_ge(done, it * N_J + (j + 1))

                        for n in range(N_W):
                            ws.split_lo(dve, n, it, N_W)
                        dve.wait_ge(s_sig, it * 3 + 1)
                        dve.tensor_tensor(head(oT, it), psum[0][:], sig[0][:], ALU.mult).then_inc(free[0], 1)
                        dve.wait_ge(s_sig, it * 3 + 2)
                        dve.tensor_tensor(qh[:], psum[1][:], sig[1][:], ALU.mult).then_inc(free[1], 1)
                        dve.wait_ge(s_sig, it * 3 + 3)
                        st.link(dve.tensor_scalar(sig[2][:], sig[2][:], one_minus_lb[:, bass.ds(it, 1)],
                                                  lb[:, bass.ds(it, 1)], ALU.mult, ALU.add))
                        st.add(dve.tensor_scalar(kh[:], sig[2][:], -1.0, 1.0, ALU.mult, ALU.add))
                        dve.tensor_scalar(X[0][:], sig[2][:], 2.0 ** -60, None, ALU.max).then_inc(s_f, 1)
                        dve.wait_ge(s_ln, it * 2 + 1)
                        st.link(dve.tensor_scalar(X[1][:], X[1][:], -3.0 * LN2, 0.0, ALU.add, ALU.min))
                        dve.wait_ge(s_ln, it * 2 + 2)
                        st.link(dve.tensor_tensor(X[0][:], X[0][:], X[1][:], ALU.add))
                        dve.tensor_tensor_scan(G[:], restart[:], X[0][:], 0.0, ALU.mult, ALU.add)\
                            .then_inc(s_G, 1)
                        dve.wait_ge(s_G, it + 1)

                        def exponent(l):
                            if l <= LEVELS:
                                n, ref = 2 ** l, 2 ** (l - 1) - 1
                            else:
                                n, ref = P, P - 1
                            if l >= 3:
                                result(J_L0 + l - 2)
                            g = G[:].rearrange("p (b n) -> p b n", n=n)
                            r = g[:, :, ref:ref + 1].to_broadcast([P, S // n, n])
                            dve.tensor_tensor(X[l % 2][:].rearrange("p (b n) -> p b n", n=n), g, r,
                                              ALU.subtract).then_inc(s_d, 1)

                        def operand(l):
                            dve.wait_ge(s_e, it * (LEVELS + 1) + l)
                            if l <= LEVELS:
                                n, half = 2 ** l, 2 ** (l - 1)
                                b, q, k = (t[:].rearrange("p (b n) -> p b n", n=n) for t in (X[l % 2], qh, kh))
                                dve.tensor_tensor(b[:, :, half:], b[:, :, half:], q[:, :, half:], ALU.mult)
                                dve.tensor_tensor(b[:, :, :half], b[:, :, :half], k[:, :, :half], ALU.mult)\
                                    .then_inc(s_x, 1)
                            else:
                                dve.tensor_tensor(X[l % 2][:], X[l % 2][:], kh[:], ALU.mult).then_inc(s_x, 1)

                        def collect_waits(l):
                            result(J_L0 + l)
                            if l >= 1:
                                slot = LEVEL_SLOT[l - 1]
                                dve.wait_ge(free[slot], it * (4 if slot == 1 else 3) +
                                            (3, 2, 2, 4, 3, 3, 5, 4)[l - 1])

                        def collect(l):
                            ps = psum[LEVEL_SLOT[l]]
                            if l == 0:
                                diag = ident[:].unsqueeze(1).to_broadcast([P, TT, P])
                                ins = dve.tensor_tensor(AT[:], tiles(ps), diag, ALU.mult)
                            else:
                                m = mask[:, l - 1, :].unsqueeze(1).to_broadcast([P, TT, P])
                                ins = dve.copy_predicated(AT[:], m, tiles(ps))
                            ins.then_inc(free[LEVEL_SLOT[l]], 1)

                        exponent(1)
                        for l in range(1, LEVELS + 2):
                            if l <= LEVELS:
                                exponent(l + 1)
                            if l >= 2:
                                collect_waits(l - 2)
                            operand(l)
                            if l == 1:
                                dve.wait_ge(s_eg, it * 2 + 2)
                                st.link(dve.tensor_tensor(q_decay[:], q_decay[:], qh[:], ALU.mult))
                            else:
                                collect(l - 2)
                        collect_waits(LEVELS)
                        result(J_UPD)
                        u = tiles(psum[3])
                        st.add(dve.tensor_copy(state[:, 1], u[:, 0]))
                        collect(LEVELS)
                        st.wait()
                        for c in range(1, TT - 1):
                            ins = dve.scalar_tensor_tensor(state[:, c + 1], state[:, c], g_last[:, c:c + 1],
                                                           u[:, c], ALU.mult, ALU.add)
                            if c < TT - 2:
                                st.link(ins)
                            else:
                                ins.then_inc(free[3], 1)
                        dve.wait_ge(s_rms, it + 1)
                        dve.scalar_tensor_tensor(sig[0][:], psum[0][:], vec[:, C_GNORM:C_GNORM + 1],
                                                 sig[1][:], ALU.mult, ALU.mult).then_inc(free[0], 1)
                        dve.wait_ge(free[0], it * 2 + 3)
                        dve.tensor_tensor(head(oT, it), sig[0][:], head(oT, it), ALU.mult).then_inc(s_out, 1)
                        st.leave(REC_HEADS)

        def rec_prepare():
            s_back = sem("x_back")
            s_hi = sem("ro_hi")
            s_lo = sem("ro_lo")

            def sync(sp):
                sp.dma_start(x[:], x_spill).then_inc(s_back, 16)

            def scalar(act):
                for k in range(KT):
                    act.activation(in_hi[:, k], oT[:, k], ACT.Copy).then_inc(s_hi, 1)

            def vector(dve):
                for k in range(KT):
                    dve.wait_ge(s_hi, k + 1)
                    dve.tensor_tensor(in_lo[:, k], oT[:, k], in_hi[:, k].bitcast(F32), ALU.subtract)\
                        .then_inc(s_lo, 1)
                dve.wait_ge(s_back, 16)

            return dict(sync=sync, scalar=scalar, vector=vector, tensor=lambda pe: pe.wait_ge(s_lo, KT))

        def final_phase():
            norm = Norm("fin", [ua[0][:], ub[0][:]], [ua[1][:], ub[1][:]])
            s_y = sem("y_ready")
            s_store = sem("y_stored")
            with nc.Block() as block:
                @block.scalar
                def _(act):
                    norm.act_stats(act, psum[3])

                @block.tensor
                def _(pe):
                    norm.pe_stats(pe, psum[3])

                @block.vector
                def _(dve):
                    dve.wait_ge(norm.rstd_ready, 1)
                    for k in range(KT):
                        dve.scalar_tensor_tensor(x[:, k], x[:, k], vec[:, C_FINAL + k:C_FINAL + k + 1],
                                                 rstd[:], ALU.mult, ALU.mult).then_inc(s_y, 1)

                @block.sync
                def _(sp):
                    for k in range(KT):
                        sp.wait_ge(s_y, k + 1)
                        sp.dma_start(outT[:, k, :], x[:, k]).then_inc(s_store, 16)
                    sp.wait_ge(s_store, 16 * KT)

        setup_phase()
        qkv_phase()
        attention_phase()
        out_proj_phase("ao", W_AO, mod_col(0, 2, 0, KT))
        ffn_phase(0, W_FFN0)
        rec_norm_phase()
        rec_phase()
        out_proj_phase("ro", W_RO, mod_col(1, 2, 0, KT), rec_prepare())
        ffn_phase(1, W_FFN1)
        final_phase()


def per_column(v):
    return np.reshape(v, (-1, P)).T


def kernel(x, c, positions, ada_w, ada_b, norm1_w, norm2_w, final_norm_w, attn_w_in, attn_w_out,
           attn_sinks, rec_w_in, rec_lb_logits, rec_g_norm, rec_w_out, ffn_w_in, ffn_conv_w,
           ffn_conv_b, ffn_w_out):
    import concourse.bacc as bacc
    from concourse.bass_utils import run_bass_kernel_spmd

    def arr(a):
        return np.asarray(a)

    sinks = arr(attn_sinks)[0]
    sink_cols = np.repeat(sinks.reshape(N_HEADS // 2, 2).T, CHUNK, axis=0)
    row = np.arange(P) % HEAD
    inv_freq = np.float32(ROPE_THETA) ** (-np.arange(0, ROPE, 2, dtype=np.float32) / np.float32(ROPE))
    freq = np.where(row < ROPE, inv_freq.astype(np.float32)[row % (ROPE // 2)], np.float32(0))[:, None]
    sign = np.where(row < ROPE // 2, 1.0, np.where(row < ROPE, -1.0, 0.0)).astype(np.float32)[:, None]
    conv_w = arr(ffn_conv_w)
    vec = np.concatenate(
        [per_column(arr(c)), per_column(arr(ada_b)), per_column(arr(norm1_w)), per_column(arr(norm2_w)),
         per_column(arr(final_norm_w)), per_column(arr(rec_lb_logits)), per_column(arr(rec_g_norm)),
         sink_cols, freq.astype(np.float32), sign, per_column(conv_w), per_column(arr(ffn_conv_b))], axis=1)
    assert vec.shape == (P, N_VEC), vec.shape

    def column_tiles(w):
        return w.reshape(KT, P, -1, P).transpose(2, 1, 0, 3)

    def row_tiles(w):
        return w.reshape(-1, P, KT, P)

    q_order = np.arange(D).reshape(2, KT, HEAD).transpose(1, 0, 2).reshape(-1)
    w_in = arr(attn_w_in)[0]
    qkv = column_tiles(np.concatenate([w_in[:, q_order], w_in[:, D:]], axis=1))
    attn_out = column_tiles(arr(attn_w_out)[0][q_order])

    def ffn_tiles(layer):
        up, down = column_tiles(arr(ffn_w_in)[layer]), row_tiles(arr(ffn_w_out)[layer])
        order = []
        for g in range(GROUPS + 1):
            if g < GROUPS:
                order += [up[2 * g], up[FT + 2 * g], up[2 * g + 1], up[FT + 2 * g + 1]]
            if g > 0:
                order += [down[2 * g - 2], down[2 * g - 1]]
        return np.stack(order)

    rec = column_tiles(arr(rec_w_in)[0]).reshape(4, REC_HEADS, P, KT, P)[[3, 0, 1, 2]]
    rec = rec.transpose(1, 0, 2, 3, 4).reshape(-1, P, KT, P)
    rec_out = column_tiles(arr(rec_w_out)[0])
    w_tiles = np.concatenate([qkv, attn_out, ffn_tiles(0), rec, rec_out, ffn_tiles(1)])
    assert w_tiles.shape[0] == N_WTILES
    ada = np.concatenate([column_tiles(arr(ada_w)[i]) for i in range(DEPTH)])

    s_, t_ = np.arange(P)[:, None], np.arange(P)[None, :]
    masks = np.stack([(s_ >> l == t_ >> l) & (s_ >> (l - 1) & 1 == 0) & (t_ >> (l - 1) & 1 == 1)
                      for l in range(1, LEVELS + 1)], axis=1).astype(np.float32)

    ins = {
        "xT": np.ascontiguousarray(arr(x)[0].T.reshape(KT, P, S).transpose(1, 0, 2)),
        "positions": np.ascontiguousarray(arr(positions)[0]),
        "vec": np.ascontiguousarray(vec),
        "ada_tiles": np.ascontiguousarray(ada.reshape(-1, P, KT * P)),
        "w_tiles": np.ascontiguousarray(w_tiles.reshape(-1, P, KT * P)),
        "ident": np.eye(P, dtype=np.float32),
        "masks": np.ascontiguousarray(masks),
    }
    nc = bacc.Bacc("TRN2", target_bir_lowering=False, num_devices=1)
    aps = [nc.dram_tensor(f"in_{n}", a.shape, mybir.dt.from_np(a.dtype), kind="ExternalInput").ap()
           for n, a in ins.items()]
    out = nc.dram_tensor("out", (P, KT, S), F32, kind="ExternalOutput").ap()
    spill = nc.dram_tensor("x_spill", (P, KT, S), F32, kind="Internal").ap()
    trunk_kernel(nc, *aps, out, spill)
    r = run_bass_kernel_spmd(nc, [{f"in_{n}": a for n, a in ins.items()}], core_ids=[0])
    yT = r.results[0]["out"]
    return np.ascontiguousarray(yT.transpose(1, 0, 2).reshape(D, S).T)[None]
```

```python
from contextlib import ExitStack

import numpy as np

import concourse.bass as bass
from concourse import mybir

F32 = mybir.dt.float32
F32R = mybir.dt.float32r
I32 = mybir.dt.int32
U8 = mybir.dt.uint8
ACT = mybir.ActivationFunctionType
ALU = mybir.AluOpType
AX = mybir.AxisListType

P = 128
S = 1024
D = 1024
KT = D // P
HALF = S // 2
DEPTH = 2
CHUNK = 64
N_CHUNKS = S // CHUNK
HEAD = 64
N_HEADS = D // HEAD
ROPE = HEAD // 4
ROPE_THETA = 500000.0
REC_HEADS = 8
TT = S // P
LEVELS = 7
FF = 2816
FT = FF // P
GROUPS = FT // 2
EPS = 1e-6

C_COND = 0
C_ADA_B = C_COND + KT
C_NORM1 = C_ADA_B + DEPTH * 6 * KT
C_NORM2 = C_NORM1 + DEPTH * KT
C_FINAL = C_NORM2 + DEPTH * KT
C_LB = C_FINAL + KT
C_GNORM = C_LB + REC_HEADS
C_SINK = C_GNORM + 1
C_FREQ = C_SINK + N_HEADS // 2
C_SIGN = C_FREQ + 1
C_CONV_W = C_SIGN + 1
C_CONV_B = C_CONV_W + DEPTH * 3 * 2 * FT
N_VEC = C_CONV_B + DEPTH * 2 * FT

N_QKV = D // P + 2
N_OUT = D // P
N_FFN = 3 * FT
N_REC = 4 * REC_HEADS
W_QKV = 0
W_AO = W_QKV + N_QKV
W_FFN0 = W_AO + N_OUT
W_REC = W_FFN0 + N_FFN
W_RO = W_REC + N_REC
W_FFN1 = W_RO + N_OUT
N_WTILES = W_FFN1 + N_FFN

RAW_RING = 2
W_RING = 4


def at(it, per, k):
    return k if it is None else it * per + k


class Steps:

    def __init__(self, eng, sem):
        self.eng, self.sem, self.n, self.it, self.per = eng, sem, 0, None, 0

    def add(self, ins):
        ins.then_inc(self.sem, 1)
        self.n += 1

    def now(self):
        return at(self.it, self.per, self.n)

    def wait(self):
        self.eng.wait_ge(self.sem, self.now())

    def link(self, ins):
        self.add(ins)
        self.wait()

    def enter(self, it, per):
        self.it, self.per, self.start = it, per, self.n

    def leave(self, trips):
        assert self.n - self.start == self.per, (self.n - self.start, self.per)
        self.n = self.start + self.per * trips
        self.it, self.per = None, 0


def two_pi_parts():
    whole = 2 * np.pi
    c1 = np.floor(whole * 32) / 32
    c2 = np.floor((whole - c1) * 2.0 ** 17) / 2.0 ** 17
    return float(c1), float(c2), float(np.float32(whole - c1 - c2))


def trunk_kernel(nc, xT, positions, vec_in, ada_tiles, w_tiles, ident_in, masks_in, outT, x_spill):
    ctx = ExitStack()
    with ctx:
        def sem(name):
            return ctx.enter_context(nc.semaphore(name))

        def alloc(stack, name, shape, dt=F32):
            return stack.enter_context(nc.sbuf_tensor(name, shape, dt))

        vec = alloc(ctx, "vec", [P, N_VEC])
        ident = alloc(ctx, "ident", [P, P])
        ones = alloc(ctx, "ones", [P, P])
        cond = alloc(ctx, "cond_silu", [P, KT])
        mod = alloc(ctx, "mod", [P, DEPTH * 6 * KT])
        gain = alloc(ctx, "gain", [P, DEPTH * 2 * KT])
        eps_col = alloc(ctx, "eps_col", [P, 1])
        w_raw = [alloc(ctx, f"w_raw{i}", [P, KT, P]) for i in range(RAW_RING)]
        w_hi = [alloc(ctx, f"w_hi{i}", [P, KT, P], F32R) for i in range(W_RING)]
        w_lo = [alloc(ctx, f"w_lo{i}", [P, KT, P], F32R) for i in range(W_RING)]
        in_hi = alloc(ctx, "in_hi", [P, KT, S], F32R)
        in_lo = alloc(ctx, "in_lo", [P, KT, S], F32R)
        tail = ExitStack()
        with tail:
            x = alloc(tail, "x", [P, KT, S])
            attn = ExitStack()
            with attn:
                q_raw = alloc(attn, "q_raw", [P, KT, S])
                kv_raw = alloc(attn, "kv_raw", [P, 2, S])
                rope_cos = alloc(attn, "rope_cos", [P, S])
                rope_sin = alloc(attn, "rope_sin", [P, S])
                ada_raw = alloc(attn, "ada_raw", [P, 4, S])
                ada_acc = alloc(attn, "ada_acc", [P, 4, P])
            ffn = ExitStack()
            with ffn:
                g_hi = alloc(ffn, "g_hi", [P, 4, S], F32R)
                g_lo = alloc(ffn, "g_lo", [P, 4, S], F32R)
                ua = [alloc(ffn, f"ua{i}", [P, S]) for i in range(2)]
                ub = [alloc(ffn, f"ub{i}", [P, S]) for i in range(2)]
                rstd = alloc(ffn, "rstd", [P, S])
                ffn_ada_raw = alloc(ffn, "ffn_ada_raw", [P, 2, S])
                ffn_ada_acc = alloc(ffn, "ffn_ada_acc", [P, 8, P])
        rec = ExitStack()
        with rec:
            sig = [alloc(rec, f"sig{i}", [P, S]) for i in range(3)]
            qh = alloc(rec, "qh", [P, S])
            kh = alloc(rec, "kh", [P, S])
            G = alloc(rec, "G", [P, S])
            vn = alloc(rec, "vn", [P, TT, P])
            AT = alloc(rec, "AT", [P, TT, P])
            oT = alloc(rec, "oT", [P, REC_HEADS, S])
            mask = alloc(rec, "mask", [P, LEVELS, P], U8)
            restart = alloc(rec, "restart", [P, S], U8)
            lb = alloc(rec, "lb", [P, REC_HEADS])
            one_minus_lb = alloc(rec, "one_minus_lb", [P, REC_HEADS])
            X = [alloc(rec, f"X{i}", [P, S]) for i in range(2)]
            q_decay = alloc(rec, "q_decay", [P, S])
            state = alloc(rec, "state", [P, TT, P])
            g_last = alloc(rec, "g_last", [P, TT])

        psum = [ctx.enter_context(nc.psum_tensor(f"ps{i}", [P, S], F32)) for i in range(4)]

        def mod_col(layer, which, tile=0, n=1):
            c = layer * 6 * KT + which * KT + tile
            return mod[:, c:c + n]

        class WeightStream:

            def __init__(self, name, base, first=0, gap=0):
                self.base, self.first, self.gap = base, first, gap
                self.raw_ready = [sem(f"{name}_raw_ready{i}") for i in range(RAW_RING)]
                self.hi_ready = sem(f"{name}_w_hi_ready")
                self.lo_ready = sem(f"{name}_w_lo_ready")

            def nth(self, n):
                return n - self.gap if self.gap and n >= self.first else n

            def load(self, sp, n, it=None, per=0):
                r = self.nth(n)
                sp.wait_ge(self.lo_ready, at(it, per, r + 1))
                if it is None:
                    src = w_tiles[self.base + r, :, :]
                else:
                    src = w_tiles[bass.ds(it * per + (self.base + r), 1), :, :]\
                        .rearrange("a p n -> (a p) n")
                sp.dma_start(w_raw[n % RAW_RING][:].rearrange("p k n -> p (k n)"), src)\
                    .then_inc(self.raw_ready[n % RAW_RING], 16)

            def split_hi(self, act, n, released, value, it=None, per=0):
                act.wait_ge(self.raw_ready[n % RAW_RING],
                            at(it, 16 * per // RAW_RING, 16 * (self.nth(n) // RAW_RING + 1)))
                if value is not None:
                    act.wait_ge(released, value)
                act.activation(w_hi[n % W_RING][:], w_raw[n % RAW_RING][:], ACT.Copy)\
                    .then_inc(self.hi_ready, 1)

            def credit(self, dve):
                dve.sem_inc(self.lo_ready, RAW_RING)

            def split_lo(self, dve, n, it=None, per=0):
                dve.wait_ge(self.hi_ready, at(it, per, self.nth(n) + 1))
                dve.tensor_tensor(w_lo[n % W_RING][:], w_raw[n % RAW_RING][:],
                                  w_hi[n % W_RING][:].bitcast(F32), ALU.subtract)\
                    .then_inc(self.lo_ready, 1)

            def wait(self, pe, n, it=None, per=0):
                pe.wait_ge(self.lo_ready, at(it, per, self.nth(n) + 1 + RAW_RING))

        def product(pe, out, parts, ready=None):
            last = len(parts) - 1
            for k, (wh, wl, mh, ml) in enumerate(parts):
                if ready is not None:
                    pe.wait_ge(ready, k + 1)
                for j, (w, m) in enumerate(((wh, mh), (wh, ml), (wl, mh))):
                    for h in range(2):
                        cut = slice(h * HALF, (h + 1) * HALF)
                        ins = pe.matmul(out[:, cut], w, m[:, cut], start=(k == 0 and j == 0),
                                        stop=(k == last and j == 2))
            return ins

        def full_parts(n):
            s = n % W_RING
            return [(w_hi[s][:, k], w_lo[s][:, k], in_hi[:, k], in_lo[:, k]) for k in range(KT)]

        class Norm:

            def __init__(self, name, sq, scaled, rstd):
                self.sq, self.scaled, self.rstd = sq, scaled, rstd
                self.sq_ready = sem(f"{name}_sq_ready")
                self.sq_used = sem(f"{name}_sq_used")
                self.rstd_ready = sem(f"{name}_rstd_ready")
                if scaled is not None:
                    self.scaled_ready = sem(f"{name}_scaled_ready")
                    self.hi_ready = sem(f"{name}_in_hi_ready")
                    self.in_ready = sem(f"{name}_in_ready")

            def act_stats(self, act, ss, landed=None):
                for k in range(KT):
                    if landed is not None:
                        act.wait_ge(landed[k], 16)
                    if k >= 2:
                        act.wait_ge(self.sq_used, k - 1)
                    act.activation(self.sq[k % 2], x[:, k], ACT.Square).then_inc(self.sq_ready, 1)
                act.wait_ge(self.sq_used, KT)
                act.activation(self.rstd, ss[:], ACT.Ln, bias=eps_col[:, 0:1], scale=1.0 / D)\
                    .then_inc(self.rstd_ready, 1)
                act.wait_ge(self.rstd_ready, 1)
                act.activation(self.rstd, self.rstd, ACT.Exp, scale=-0.5).then_inc(self.rstd_ready, 1)

            def pe_stats(self, pe, ss):
                for k in range(KT):
                    pe.wait_ge(self.sq_ready, k + 1)
                    for h in range(2):
                        cut = slice(h * HALF, (h + 1) * HALF)
                        ins = pe.matmul(ss[:, cut], ones[:], self.sq[k % 2][:, cut],
                                        start=(k == 0), stop=(k == KT - 1))
                    ins.then_inc(self.sq_used, 1)

            def act_apply(self, act, shift):
                for k in range(KT):
                    act.wait_ge(self.scaled_ready, k + 1)
                    act.activation(in_hi[:, k], self.scaled[k % 2], ACT.Identity,
                                   bias=shift[:, k:k + 1]).then_inc(self.hi_ready, 1)

            def dve_apply(self, dve, g, shift):
                dve.wait_ge(self.rstd_ready, 2)
                for k in range(KT):
                    if k >= 2:
                        dve.wait_ge(self.in_ready, k - 1)
                    dve.scalar_tensor_tensor(self.scaled[k % 2], x[:, k], g[:, k:k + 1], self.rstd,
                                             ALU.mult, ALU.mult).then_inc(self.scaled_ready, 1)
                    if k >= 1:
                        self.dve_rest(dve, k - 1, shift)
                self.dve_rest(dve, KT - 1, shift)

            def dve_rest(self, dve, k, shift):
                dve.wait_ge(self.hi_ready, k + 1)
                dve.scalar_tensor_tensor(in_lo[:, k], self.scaled[k % 2], shift[:, k:k + 1],
                                         in_hi[:, k].bitcast(F32), ALU.add, ALU.subtract)\
                    .then_inc(self.in_ready, 1)

        class Ada:

            def __init__(self, name, first, width, raw, acc, cols):
                self.first, self.width, self.raw, self.acc, self.cols = first, width, raw, acc, cols
                self.landed = [sem(f"{name}_ada_landed{i}") for i in range(len(raw))]
                self.acc_ready = sem(f"{name}_ada_acc_ready")
                self.step_sem = sem(f"{name}_ada_step")
                self.col_ready = sem(f"{name}_ada_col_ready")
                self.col_taken = sem(f"{name}_ada_col_taken")
                self.mod_ready = sem(f"{name}_mod_ready")

            def load(self, sp, b, it=None, per=0):
                sp.wait_ge(self.acc_ready, at(it, per, b + 1))
                first = self.first + b * self.width
                if it is None:
                    src = ada_tiles[first:first + self.width]
                else:
                    src = ada_tiles[bass.ds(it * (per * self.width) + first, self.width)]
                slot = b % len(self.raw)
                sp.dma_start(self.raw[slot], src.rearrange("a p n -> p a n")).then_inc(self.landed[slot], 16)

            def credit(self, dve):
                dve.sem_inc(self.acc_ready, len(self.raw))

            def sum_tiles(self, dve, steps, b, it=None, per=0):
                slot, acc = b % len(self.raw), self.acc[b % len(self.acc)]
                dve.wait_ge(self.landed[slot], at(it, 16 * per // len(self.raw), 16 * (b // len(self.raw) + 1)))
                dve.wait_ge(self.col_ready, at(it, per, b + 1))
                w = self.raw[slot].rearrange("p a (k n) -> p a k n", k=KT)
                steps.link(dve.tensor_scalar(acc, w[:, :, 0], cond[:, 0:1], None, ALU.mult))
                for k in range(1, KT):
                    ins = dve.scalar_tensor_tensor(acc, w[:, :, k], cond[:, k:k + 1], acc,
                                                   ALU.mult, ALU.add)
                    if k < KT - 1:
                        steps.link(ins)
                    else:
                        ins.then_inc(self.acc_ready, 1)

            def pe_credit(self, pe):
                pe.sem_inc(self.col_ready, len(self.acc))
                pe.sem_inc(self.col_taken, 1)

            def columns(self, pe, b, col, taken=None, it=None, per=0):
                pe.wait_ge(self.acc_ready, at(it, per, b + 1 + len(self.raw)))
                if taken is not None:
                    pe.wait_ge(self.col_taken, taken)
                for i in range(self.width):
                    ins = pe.matmul(self.cols[:, col + i:col + i + 1], self.acc[b % len(self.acc)][:, i],
                                    ones[:, 0:1], start=True, stop=True)
                ins.then_inc(self.col_ready, 1)

            def take(self, act, b, n, it=None, per=0):
                act.wait_ge(self.col_ready, at(it, per, b + 1 + len(self.acc)))
                first = self.first + (b + 1 - n) * self.width
                dst = mod[:, first:first + n * self.width] if it is None else \
                    mod[:, bass.ds(it * (per * self.width) + first, n * self.width)]
                act.activation(dst, self.cols[:, 0:n * self.width], ACT.Copy).then_inc(self.col_taken, 1)

            def finish(self, dve, takes, end, norms):
                dve.wait_ge(self.col_taken, takes + 1)
                m = mod[:, self.first:end]
                dve.tensor_tensor(m, m, vec[:, C_ADA_B + self.first:C_ADA_B + end], ALU.add)\
                    .then_inc(self.mod_ready, 1)
                dve.wait_ge(self.mod_ready, 1)
                for layer, which in norms:
                    g = gain[:, (2 * layer + which) * KT:(2 * layer + which + 1) * KT]
                    col = (C_NORM1, C_NORM2)[which] + layer * KT
                    dve.scalar_tensor_tensor(g, mod_col(layer, 3 * which + 1, 0, KT), 1.0,
                                             vec[:, col:col + KT], ALU.add, ALU.mult)\
                        .then_inc(self.mod_ready, 1)
                dve.wait_ge(self.mod_ready, 1 + len(norms))

        SETUP_ADA = 2 * KT

        def setup_phase():
            s_vec = sem("vectors_landed")
            s_ident = sem("identity_landed")
            s_x = [sem(f"x_tile{k}_landed") for k in range(KT)]
            s_cond = sem("cond_ready")
            s_ones = sem("ones_ready")
            norm = Norm("n0", [ada_raw[:, i] for i in range(2)], [ada_raw[:, 2 + i] for i in range(2)],
                        kv_raw[:, 0])
            quads = SETUP_ADA // 4
            ada = Ada("s", 0, 4, [q_raw[:, 0:4], q_raw[:, 4:8]],
                      [kv_raw[:, 1, i * HALF:(i + 1) * HALF].rearrange("p (a n) -> p a n", a=4)
                       for i in range(2)], psum[1])
            with nc.Block() as block:
                @block.sync
                def _(sp):
                    sp.dma_start(vec[:], vec_in).then_inc(s_vec, 16)
                    ada.load(sp, 0)
                    for k in range(KT):
                        sp.dma_start(x[:, k], xT[:, k]).then_inc(s_x[k], 16)
                    for b in range(1, quads):
                        ada.load(sp, b)
                    sp.dma_start(ident[:], ident_in).then_inc(s_ident, 16)
                    sp.wait_ge(s_ident, 16)

                @block.gpsimd
                def _(pool):
                    pool.memset(ones[:], 1.0).then_inc(s_ones, 1)
                    pool.memset(eps_col[:], EPS).then_inc(s_ones, 1)

                @block.scalar
                def _(act):
                    act.wait_ge(s_vec, 16)
                    act.activation(cond[:], vec[:, C_COND:C_COND + KT], ACT.Silu).then_inc(s_cond, 1)
                    act.wait_ge(s_ones, 2)
                    norm.act_stats(act, psum[0], s_x)
                    ada.take(act, quads - 1, quads)
                    norm.act_apply(act, mod_col(0, 0, 0, KT))

                @block.tensor
                def _(pe):
                    ada.pe_credit(pe)
                    pe.wait_ge(s_ones, 2)
                    norm.pe_stats(pe, psum[0])
                    for b in range(quads):
                        ada.columns(pe, b, 4 * b)

                @block.vector
                def _(dve):
                    ada.credit(dve)
                    steps = Steps(dve, ada.step_sem)
                    dve.wait_ge(s_cond, 1)
                    for b in range(quads):
                        ada.sum_tiles(dve, steps, b)
                    ada.finish(dve, 1, SETUP_ADA, [(0, 0)])
                    norm.dve_apply(dve, gain[:, 0:KT], mod_col(0, 0, 0, KT))

        def qkv_phase():
            TURN = 4
            TURNS = N_QKV // TURN
            RING = 2
            PAIRS = 2
            PT = TURN * PAIRS
            ws = WeightStream("qkv", W_QKV)
            done, evac = sem("qkv_done"), sem("qkv_evac")
            s_pos = sem("positions_landed")
            s_step = sem("angle_step")
            s_ang = sem("angle_ready")
            s_rope = sem("rope_ready")
            ada = Ada("q", SETUP_ADA, 2, [ada_raw[:, 0:2], ada_raw[:, 2:4]],
                      [ada_acc[:, 0:2], ada_acc[:, 2:4]], psum[3])
            ang, turns = ada_raw[:, 0], ada_raw[:, 1]
            pos_i = ada_raw[:, 2].bitcast(I32)

            def tiles(eng, body, steps=()):
                with eng.Fori(0, TURNS) as it:
                    for s, k in steps:
                        s.enter(it, k)
                    for n in range(TURN):
                        body(n, it)
                    for s, k in steps:
                        s.leave(TURNS)
                for n in range(TURNS * TURN, N_QKV):
                    body(n, None)

            def ada_batches(n, it):
                return [] if it is None else [n * PAIRS + i for i in range(PAIRS)]

            with nc.Block() as block:
                @block.sync
                def _(sp):
                    def body(n, it):
                        ws.load(sp, n, it, TURN)
                        for b in ada_batches(n, it):
                            ada.load(sp, b, it, PT)
                    tiles(sp, body)
                    sp.wait_ge(ada.acc_ready, TURNS * PT + len(ada.raw))
                    sp.dma_start(pos_i, positions.partition_broadcast(P)).then_inc(s_pos, 16)

                @block.vector
                def _(dve):
                    ws.credit(dve)
                    ada.credit(dve)
                    steps = Steps(dve, ada.step_sem)

                    def body(n, it):
                        for b in ada_batches(n, it):
                            ada.sum_tiles(dve, steps, b, it, PT)
                        ws.split_lo(dve, n, it, TURN)
                    tiles(dve, body, ((steps, PT * (KT - 1)),))
                    ada.finish(dve, TURNS, 6 * KT, [(0, 1)])
                    pos = Steps(dve, s_step)
                    dve.wait_ge(s_pos, 16)
                    pos.link(dve.tensor_copy(ang, pos_i))
                    pos.link(dve.tensor_scalar(ang, ang, vec[:, C_FREQ:C_FREQ + 1], None, ALU.mult))
                    magic = 1.5 * 2.0 ** 23
                    parts = two_pi_parts()

                    def reduce_angle(dst, src, unit, shift):
                        pos.link(dve.tensor_scalar(turns, src, 1.0 / (2 * np.pi * unit), shift,
                                                   ALU.mult, ALU.add))
                        pos.link(dve.tensor_scalar(turns, turns, magic, None, ALU.add))
                        pos.link(dve.tensor_scalar(turns, turns, magic, None, ALU.subtract))
                        for c in parts:
                            pos.link(dve.scalar_tensor_tensor(dst, turns, -c * unit, src,
                                                              ALU.mult, ALU.add))
                            src = dst

                    pi32 = 3.1415925
                    reduce_angle(ang, ang, 4096.0, 0.0)
                    reduce_angle(rope_sin[:], ang, 1.0, 0.0)
                    dve.tensor_scalar(rope_sin[:], rope_sin[:], pi32, -pi32, ALU.min, ALU.max)\
                        .then_inc(s_ang, 1)
                    reduce_angle(rope_cos[:], ang, 1.0, 0.25)
                    pos.link(dve.tensor_scalar(rope_cos[:], rope_cos[:], float(np.pi / 2), None, ALU.add))
                    dve.tensor_scalar(rope_cos[:], rope_cos[:], pi32, -pi32, ALU.min, ALU.max)\
                        .then_inc(s_ang, 1)
                    dve.wait_ge(s_rope, 1)
                    dve.tensor_scalar(rope_sin[:], rope_sin[:], vec[:, C_SIGN:C_SIGN + 1], None, ALU.mult)

                @block.tensor
                def _(pe):
                    ada.pe_credit(pe)
                    pe.sem_inc(evac, RING)

                    def body(n, it):
                        for b in ada_batches(n, it):
                            ada.columns(pe, b, 2 * b, at(it, 1, 1) if b == 0 else None, it, PT)
                        ws.wait(pe, n, it, TURN)
                        pe.wait_ge(evac, at(it, TURN, n + 1))
                        product(pe, psum[n % RING], full_parts(n)).then_inc(done, 1)
                    tiles(pe, body)

                @block.scalar
                def _(act):
                    def take(n, it):
                        act.wait_ge(done, at(it, TURN, n + 1))
                        if it is None:
                            dst = kv_raw[:, n - KT]
                        else:
                            dst = q_raw[:, bass.ds(it * TURN + n, 1)].rearrange("p a s -> p (a s)")
                        act.activation(dst, psum[n % RING][:], ACT.Copy).then_inc(evac, 1)

                    ws.split_hi(act, 0, None, None)
                    ws.split_hi(act, 1, None, None)

                    def body(n, it):
                        if it is not None and n == TURN - 1:
                            ada.take(act, PT - 1, PT, it, PT)
                        take(n, it)
                        if it is not None:
                            ws.split_hi(act, n + 2, None, None, it, TURN)

                    tiles(act, body)
                    act.wait_ge(s_ang, 1)
                    act.activation(rope_sin[:], rope_sin[:], ACT.Sin).then_inc(s_rope, 1)
                    act.wait_ge(s_ang, 2)
                    act.activation(rope_cos[:], rope_cos[:], ACT.Sin).then_inc(s_rope, 1)

        def out_proj_phase(name, base, gate, prepare=None):
            ws = WeightStream(name, base)
            done, evac = sem(f"{name}_done"), sem(f"{name}_evac")
            with nc.Block() as block:
                @block.sync
                def _(sp):
                    if prepare:
                        prepare["sync"](sp)
                    for n in range(N_OUT):
                        ws.load(sp, n)

                @block.scalar
                def _(act):
                    if prepare:
                        prepare["scalar"](act)
                    for n in range(N_OUT):
                        ws.split_hi(act, n, done, n - W_RING + 1 if n >= W_RING else None)

                @block.vector
                def _(dve):
                    ws.credit(dve)
                    if prepare:
                        prepare["vector"](dve)

                    def take(n):
                        dve.wait_ge(done, n + 1)
                        dve.scalar_tensor_tensor(x[:, n], psum[n % 4][:], gate[:, n:n + 1], x[:, n],
                                                 ALU.mult, ALU.add).then_inc(evac, 1)

                    for n in range(N_OUT):
                        ws.split_lo(dve, n)
                        if n >= 2:
                            take(n - 2)
                    take(N_OUT - 2)
                    take(N_OUT - 1)

                @block.tensor
                def _(pe):
                    if prepare:
                        prepare["tensor"](pe)
                    for n in range(N_OUT):
                        ws.wait(pe, n)
                        if n >= 4:
                            pe.wait_ge(evac, n - 3)
                        product(pe, psum[n % 4], full_parts(n)).then_inc(done, 1)

        AT_TURN = 4
        AT_TURNS = (N_CHUNKS - 1) // AT_TURN
        NB = N_HEADS // 2
        at_ctx = ExitStack()
        with at_ctx:
            for n, w in (("at_x", KT), ("at_q", KT), ("at_kv", 2), ("at_cos", 1), ("at_sin", 1)):
                alloc(at_ctx, n, [P, w, S])
            q_rot = alloc(at_ctx, "q_rot", [P, KT, CHUNK])
            q_swap = alloc(at_ctx, "q_swap", [P, KT, CHUNK])
            k_rot = alloc(at_ctx, "k_rot", [P, AT_TURN, CHUNK])
            k_swap = alloc(at_ctx, "k_swap", [P, CHUNK])
            v_keys = alloc(at_ctx, "v_keys", [P, 2, CHUNK])
            v_win = alloc(at_ctx, "v_win", [P, P])
            probsT = alloc(at_ctx, "probsT", [P, S])
            row_max, sink_exp, neg_max, row_sum, inv_den = (
                alloc(at_ctx, n, [P, NB]) for n in ("row_max", "sink_exp", "neg_max", "row_sum", "inv_den"))

        def attention_phase():
            s_rot = sem("at_rope_step")
            s_in = sem("at_chunk_rotated")
            s_qk = sem("at_scores_ready")
            s_mx = sem("at_max_step")
            s_bias = sem("at_bias_ready")
            s_exp = sem("at_exp_ready")
            s_esink = sem("at_sink_exp_ready")
            s_probs = sem("at_probs_ready")
            s_pT = sem("at_probs_transposed")
            s_pc = sem("at_probsT_copied")
            s_vT = sem("at_v_transposed")
            s_v = sem("at_v_copied")
            s_o = sem("at_out_ready")
            s_ohi = sem("at_out_hi")
            s_olo = sem("at_out_lo")
            sink = vec[:, C_SINK:C_SINK + NB]
            probs = w_raw[0][:]
            scores = [psum[i][:].rearrange("p (b k) -> p b k", b=NB) for i in range(2)]
            v_ps, out_ps = psum[2][:, 0:P], psum[2][:, HALF:]
            pT_ps = psum[3]
            scale = HEAD ** -0.5
            swap = [i + ROPE // 2 if i < ROPE // 2 else i - ROPE // 2 if i < ROPE else i for i in range(32)]

            def chunks(eng, body, steps=()):
                body(0, None)
                with eng.Fori(0, AT_TURNS) as it:
                    for s, k in steps:
                        s.enter(it, AT_TURN * k)
                    for c in range(AT_TURN):
                        body(1 + c, it)
                    for s, k in steps:
                        s.leave(AT_TURNS)
                for n in range(1 + AT_TURN * AT_TURNS, N_CHUNKS):
                    body(n, None)

            def keys(n):
                if n == 0:
                    return slice(0, 1), CHUNK
                lo, hi = sorted(((n - 1) % AT_TURN, n % AT_TURN))
                return slice(lo, hi + 1, hi - lo), 2 * CHUNK

            def tokens(n, it):
                return slice(n * CHUNK, (n + 1) * CHUNK) if it is None else \
                    bass.ds(it * (AT_TURN * CHUNK) + n * CHUNK, CHUNK)

            def count(n, it, k):
                return at(it, AT_TURN, n + k)

            with nc.Block() as block:
                @block.vector
                def _(dve):
                    rot, mx = Steps(dve, s_rot), Steps(dve, s_mx)

                    def rotate(n, it):
                        cut, slot = tokens(n, it), n % AT_TURN
                        cos = rope_cos[:, cut].unsqueeze(1).to_broadcast([P, KT, CHUNK])
                        sin = rope_sin[:, cut].unsqueeze(1).to_broadcast([P, KT, CHUNK])
                        if n > 0:
                            dve.wait_ge(s_qk, count(n, it, 0))
                        rot.add(dve.tensor_tensor(q_swap[:], q_raw[:, :, cut], sin, ALU.mult))
                        rot.add(dve.tensor_tensor(k_swap[:], kv_raw[:, 0, cut], rope_sin[:, cut], ALU.mult))
                        rot.add(dve.tensor_tensor(q_rot[:], q_raw[:, :, cut], cos, ALU.mult))
                        rot.add(dve.tensor_tensor(k_rot[:, slot], kv_raw[:, 0, cut], rope_cos[:, cut],
                                                  ALU.mult))
                        rot.wait()
                        if n > 0:
                            dve.wait_ge(s_vT, count(n, it, 0))
                        rot.add(dve.tensor_copy(v_keys[:, min(slot, 1)], kv_raw[:, 1, cut]))
                        if n > 0:
                            rot.add(dve.tensor_copy(v_keys[:, 1 - min(slot, 1)],
                                                    kv_raw[:, 1, tokens(n - 1, it)]))
                        rot.add(dve.stream_shuffle(q_swap[:], q_swap[:], swap))
                        rot.add(dve.stream_shuffle(k_swap[:], k_swap[:], swap))
                        rot.wait()
                        rot.add(dve.tensor_tensor(k_rot[:, slot], k_rot[:, slot], k_swap[:], ALU.add))
                        rot.wait()
                        dve.tensor_tensor(q_rot[:], q_rot[:], q_swap[:], ALU.add).then_inc(s_in, 1)

                    def body(n, it):
                        w = keys(n)[1]
                        rotate(n, it)
                        dve.wait_ge(s_qk, count(n, it, 1))
                        mx.link(dve.tensor_reduce(row_max[:], scores[n % 2][:, :, 0:w], AX.X, ALU.max))
                        mx.link(dve.scalar_tensor_tensor(row_max[:], row_max[:], scale, sink,
                                                         ALU.mult, ALU.max))
                        mx.link(dve.tensor_tensor(sink_exp[:], sink, row_max[:], ALU.subtract))
                        if n > 0:
                            dve.wait_ge(s_pT, count(n, it, 0))
                        dve.tensor_scalar(neg_max[:], row_max[:], -1.0, None, ALU.mult).then_inc(s_bias, 1)
                        dve.wait_ge(s_esink, count(n, it, 1))
                        mx.link(dve.tensor_tensor(inv_den[:], row_sum[:], sink_exp[:], ALU.add))
                        mx.link(dve.reciprocal(inv_den[:], inv_den[:]))
                        pr = probs[:, :, 0:w]
                        dve.tensor_tensor(pr, pr, inv_den[:].unsqueeze(2).to_broadcast([P, NB, w]),
                                          ALU.mult).then_inc(s_probs, 1)
                        dve.wait_ge(s_ohi, count(n, it, 1))
                        cut = tokens(n, it)
                        dve.tensor_tensor(in_lo[:, :, cut], out_ps.rearrange("p (t q) -> p t q", t=KT),
                                          in_hi[:, :, cut].bitcast(F32), ALU.subtract).then_inc(s_olo, 1)

                    chunks(dve, body, ((rot, 9), (mx, 5)))

                @block.tensor
                def _(pe):
                    def body(n, it):
                        slots, w = keys(n)
                        sc = scores[n % 2]
                        pe.wait_ge(s_in, count(n, it, 1))
                        if n > 1:
                            pe.wait_ge(s_exp, count(n, it, -1))
                        elif n == 1 and it is not None:
                            pe.wait_ge(s_exp, count(n, it, 0))
                        for b in range(NB):
                            rows = slice(HEAD * (b // 4), HEAD * (b // 4) + HEAD)
                            t = 2 * (b % 4)
                            ins = pe.matmul(sc[:, b, 0:w], q_rot[rows, t:t + 2], k_rot[rows, slots],
                                            start=True, stop=True)
                        ins.then_inc(s_qk, 1)
                        if n > 0:
                            pe.wait_ge(s_v, count(n, it, 0))
                        pe.transpose(v_ps[0:w], v_keys[:].rearrange("p a b -> p (a b)")[:, 0:w], ident[:])\
                            .then_inc(s_vT, 1)
                        pe.wait_ge(s_probs, count(n, it, 1))
                        if n > 0:
                            pe.wait_ge(s_pc, count(n, it, 0))
                        for b in range(NB):
                            ins = pe.transpose(pT_ps[0:w, b * P:(b + 1) * P], probs[:, b, 0:w], ident[:])
                        ins.then_inc(s_pT, 1)
                        pe.wait_ge(s_pc, count(n, it, 1))
                        pe.wait_ge(s_v, count(n, it, 1))
                        if n > 0:
                            pe.wait_ge(s_olo, count(n, it, 0))
                        for kv in range(2):
                            rows = slice(HEAD * kv, HEAD * kv + HEAD)
                            ins = pe.matmul(out_ps[rows, :], v_win[0:w, rows],
                                            probsT[0:w, kv * HALF:(kv + 1) * HALF], start=True, stop=True)
                        ins.then_inc(s_o, 1)

                    chunks(pe, body)

                @block.scalar
                def _(act):
                    def body(n, it):
                        w = keys(n)[1]
                        if n > 0:
                            act.wait_ge(s_o, count(n, it, 0))
                        act.wait_ge(s_vT, count(n, it, 1))
                        act.activation(v_win[0:w, :], v_ps[0:w], ACT.Copy).then_inc(s_v, 1)
                        act.wait_ge(s_bias, count(n, it, 1))
                        for b in range(NB):
                            ins = act.activation(probs[:, b, 0:w], scores[n % 2][:, b, 0:w], ACT.Exp,
                                                 bias=neg_max[:, b:b + 1], scale=scale,
                                                 accum_out=row_sum[:, b:b + 1])
                        ins.then_inc(s_exp, 1)
                        act.activation(sink_exp[:], sink_exp[:], ACT.Exp).then_inc(s_esink, 1)
                        act.wait_ge(s_pT, count(n, it, 1))
                        act.activation(probsT[0:w, :], pT_ps[0:w, :], ACT.Copy).then_inc(s_pc, 1)
                        act.wait_ge(s_o, count(n, it, 1))
                        act.activation(in_hi[:, :, tokens(n, it)],
                                       out_ps.rearrange("p (t q) -> p t q", t=KT),
                                       ACT.Copy).then_inc(s_ohi, 1)

                    chunks(act, body)

        def ffn_phase(layer, base, next_ada=None):
            name = f"f{layer}"
            norm = Norm(name, [ua[0][:], ub[0][:]], [ua[1][:], ub[1][:]], rstd[:])
            done = sem(f"{name}_job_done")
            taken = sem(f"{name}_job_taken")
            s_tap = sem(f"{name}_tap_ready")
            s_cs = sem(f"{name}_conv_step")
            s_silu = sem(f"{name}_silu_ready")
            s_gate = sem(f"{name}_gated_ready")
            s_ghi = sem(f"{name}_g_hi_ready")
            s_glo = sem(f"{name}_g_lo_ready")
            gate2 = mod_col(layer, 5, 0, KT)
            cw = C_CONV_W + layer * 6 * FT
            cb = C_CONV_B + layer * 2 * FT
            GW, GJ = 6, 4 + KT
            GAP = 2
            PW, PJ, PH = 2 * GW, 2 * GJ, 4
            ws = WeightStream(name, base, first=4, gap=GAP)
            STEPS = 2 * 2 * 2

            def groups(eng, hidden, output, skip=None, steps=()):
                hidden(0, 0, 0, None)
                if skip:
                    skip()
                with eng.Fori(0, (GROUPS - 1) // 2) as it:
                    for s, k in steps:
                        s.enter(it, k)
                    for g in (1, 2):
                        hidden(g, GW * g, GJ * g, it)
                        output(g - 1, GW * g + 4, GJ * g + 4, it)
                    for s, k in steps:
                        s.leave((GROUPS - 1) // 2)
                output(GROUPS - 1, GW * GROUPS, GJ * GROUPS, None)

            def released(n, it):
                g, i = divmod(n, GW)
                if n < W_RING:
                    return None
                if n == GW * GROUPS or n == GW * GROUPS + 1:
                    return GJ * (GROUPS - 1) + 3 + i
                return at(it, PJ, (GJ * (g - 1) + 3, GJ * (g - 1) + 4, GJ * g, GJ * g,
                                   GJ * g + 1, GJ * g + 2)[i])

            def col(start, f, it):
                return vec[:, start + f:start + f + 1] if it is None else \
                    vec[:, bass.ds(it * PH + (start + f), 1)]

            RING = 3 if next_ada is not None else 4
            if next_ada is not None:
                AB, PB = 2, 4
                ada = Ada(name, next_ada, 2, [ffn_ada_raw[:]],
                          [ffn_ada_acc[:, 2 * i:2 * i + 2] for i in range(PB)], psum[3])

            def ada_batches(g, i):
                if next_ada is None:
                    return []
                return [2 * i, 2 * i + 1] if g == 0 else [PB + 2 * (g - 1) + i]

            with nc.Block() as block:
                @block.sync
                def _(sp):
                    def load(n, k, it):
                        for i in range(k):
                            ws.load(sp, n + i, it, PW)

                    def hidden(g, n, j, it):
                        load(n, 4, it)
                        for b in ada_batches(g, 0) + (ada_batches(g, 1) if g == 0 else []):
                            ada.load(sp, b, it, PB)

                    def output(g, n, j, it):
                        load(n, 2, it)
                        if g < GROUPS - 1:
                            for b in ada_batches(g + 1, 1):
                                ada.load(sp, b, it, PB)

                    groups(sp, hidden, output)

                @block.tensor
                def _(pe):
                    if next_ada is not None:
                        ada.pe_credit(pe)
                    norm.pe_stats(pe, psum[3])

                    def job(j, it, parts):
                        if j >= RING:
                            pe.wait_ge(taken, at(it, PJ, j - RING + 1))
                        product(pe, psum[j % RING], parts, norm.in_ready if it is None and j == 0 else None)\
                            .then_inc(done, 1)

                    def columns(g, it):
                        if next_ada is not None:
                            for i in range(2):
                                ada.columns(pe, 2 * g + i, 2 * i, at(it, 2, g + 1), it, PB)

                    def hidden(g, n, j, it):
                        if g > 0:
                            columns(g, it)
                        for i in range(4):
                            ws.wait(pe, n + i, it, PW)
                            job(j + i, it, full_parts(n + i))

                    def output(g, n, j, it):
                        if g == GROUPS - 1:
                            columns(GROUPS, None)
                        ws.wait(pe, n, it, PW)
                        ws.wait(pe, n + 1, it, PW)
                        pe.wait_ge(s_glo, at(it, PH, 2 * g + 2))
                        for d in range(KT):
                            job(j + d, it, [(w_hi[(n + i) % W_RING][:, d], w_lo[(n + i) % W_RING][:, d],
                                             g_hi[:, (2 * g + i) % 4], g_lo[:, (2 * g + i) % 4])
                                            for i in range(2)])

                    def skip():
                        pe.drain().then_inc(done, KT)
                        columns(0, None)

                    groups(pe, hidden, output, skip)

                @block.scalar
                def _(act):
                    def split(n, it):
                        ws.split_hi(act, n, done, released(n, it), it, PW)

                    split(0, None)
                    split(1, None)
                    norm.act_stats(act, psum[3])
                    norm.act_apply(act, mod_col(layer, 3, 0, KT))

                    def tap(side, f, j, it):
                        act.wait_ge(done, at(it, PJ, j + 1))
                        if f >= 2:
                            act.wait_ge(s_glo, at(it, PH, f - 1))
                        act.activation((ua, ub)[side][f % 2][:], psum[j % RING][:], ACT.Identity,
                                       bias=col(cb + side * FT, f, it),
                                       scale=col(cw + (2 * 2 + side) * FT, f, it)).then_inc(s_tap, 1)

                    def silu(f, j, it):
                        act.wait_ge(taken, at(it, PJ, j + 1))
                        act.activation(ua[f % 2][:], ua[f % 2][:], ACT.Silu).then_inc(s_silu, 1)

                    def take_columns(g, it):
                        if next_ada is not None:
                            ada.take(act, 2 * g + 1, 2, it, PB)

                    def gated_hi(f, it):
                        act.wait_ge(s_gate, at(it, PH, f + 1))
                        act.activation(g_hi[:, f % 4], ua[f % 2][:], ACT.Copy).then_inc(s_ghi, 1)

                    def hidden(g, n, j, it):
                        f = 2 * g
                        split(n + 2, it)
                        split(n + 3, it)
                        tap(0, f, j, it)
                        if g > 0:
                            take_columns(g, it)
                            split(n + 4, it)
                        tap(1, f, j + 1, it)
                        silu(f, j, it)
                        if g > 0:
                            split(n + 5, it)
                        gated_hi(f, it)
                        tap(0, f + 1, j + 2, it)
                        tap(1, f + 1, j + 3, it)
                        silu(f + 1, j + 2, it)

                    def output(g, n, j, it):
                        gated_hi(2 * g + 3, it)
                        split(n + 2, it)
                        split(n + 3, it)

                    def skip():
                        output(-1, GW - 2, 0, None)
                        take_columns(0, None)

                    groups(act, hidden, lambda g, n, j, it: output(g, n, j, it) if it is not None
                           else take_columns(GROUPS, None), skip)

                @block.vector
                def _(dve):
                    ws.credit(dve)
                    ws.split_lo(dve, 0)
                    ws.split_lo(dve, 1)
                    norm.dve_apply(dve, gain[:, (2 * layer + 1) * KT:(2 * layer + 2) * KT],
                                   mod_col(layer, 3, 0, KT))
                    cs = Steps(dve, s_cs)
                    if next_ada is not None:
                        ada.credit(dve)
                        ada_steps = Steps(dve, ada.step_sem)

                    def earlier_taps(side, f, j, it):
                        ps, dst = psum[j % RING], (ua, ub)[side][f % 2]
                        dve.wait_ge(s_tap, at(it, 2 * PH, 2 * f + side + 1))
                        cs.link(dve.scalar_tensor_tensor(
                            dst[:, 1:], ps[:, :S - 1], col(cw + (2 * 1 + side) * FT, f, it),
                            dst[:, 1:], ALU.mult, ALU.add))
                        dve.scalar_tensor_tensor(
                            dst[:, 2:], ps[:, :S - 2], col(cw + side * FT, f, it),
                            dst[:, 2:], ALU.mult, ALU.add).then_inc(taken, 1)

                    def gated(f, j, it):
                        dve.wait_ge(s_silu, at(it, PH, f + 1))
                        dve.wait_ge(taken, at(it, PJ, j + 1))
                        dve.tensor_tensor(ua[f % 2][:], ua[f % 2][:], ub[f % 2][:], ALU.mult)\
                            .then_inc(s_gate, 1)

                    def gated_lo(f, it):
                        dve.wait_ge(s_ghi, at(it, PH, f + 1))
                        dve.tensor_tensor(g_lo[:, f % 4], ua[f % 2][:], g_hi[:, f % 4].bitcast(F32),
                                          ALU.subtract).then_inc(s_glo, 1)

                    def sum_tiles(g, i, it):
                        for b in ada_batches(g, i):
                            ada.sum_tiles(dve, ada_steps, b, it, PB)

                    def hidden(g, n, j, it):
                        f = 2 * g
                        ws.split_lo(dve, n + 2, it, PW)
                        ws.split_lo(dve, n + 3, it, PW)
                        earlier_taps(0, f, j, it)
                        if g > 0:
                            ws.split_lo(dve, n + 4, it, PW)
                        sum_tiles(g, 0, it)
                        earlier_taps(1, f, j + 1, it)
                        gated(f, j + 1, it)
                        if g > 0:
                            ws.split_lo(dve, n + 5, it, PW)
                        gated_lo(f, it)
                        earlier_taps(0, f + 1, j + 2, it)
                        sum_tiles(g, 1, it)
                        earlier_taps(1, f + 1, j + 3, it)

                    def output(g, n, j, it):
                        between = {0: lambda: gated(2 * g + 3, j - 1, it),
                                   1: lambda: gated_lo(2 * g + 3, it),
                                   2: lambda: ws.split_lo(dve, n + 2, it, PW),
                                   3: lambda: ws.split_lo(dve, n + 3, it, PW)}
                        for d in range(KT):
                            if g >= 0:
                                dve.wait_ge(done, at(it, PJ, j + d + 1))
                                dve.scalar_tensor_tensor(x[:, d], psum[(j + d) % RING][:],
                                                         gate2[:, d:d + 1], x[:, d],
                                                         ALU.mult, ALU.add).then_inc(taken, 1)
                            if d in between and g < GROUPS - 1:
                                between[d]()

                    def skip():
                        output(-1, GW - 2, 4, None)
                        dve.drain().then_inc(taken, KT)

                    loop_steps = [(cs, STEPS)]
                    if next_ada is not None:
                        loop_steps.append((ada_steps, PB * (KT - 1)))
                    groups(dve, hidden, output, skip, loop_steps)
                    if next_ada is not None:
                        ada.finish(dve, GROUPS + 1, 12 * KT, [(1, 0), (1, 1)])

        def rec_norm_phase():
            norm = Norm("rn", [ua[0][:], ub[0][:]], [ua[1][:], ub[1][:]], rstd[:])
            s_spill = sem("x_spilled")
            with nc.Block() as block:
                @block.sync
                def _(sp):
                    sp.dma_start(x_spill, x[:]).then_inc(s_spill, 16)
                    sp.wait_ge(s_spill, 16)

                @block.scalar
                def _(act):
                    norm.act_stats(act, psum[3])
                    norm.act_apply(act, mod_col(1, 0, 0, KT))

                @block.tensor
                def _(pe):
                    norm.pe_stats(pe, psum[3])

                @block.vector
                def _(dve):
                    norm.dve_apply(dve, gain[:, 2 * KT:3 * KT], mod_col(1, 0, 0, KT))

        def rec_phase():
            ws = WeightStream("rec", W_REC)
            N_W = 4
            (J_GATE, J_Q, J_F, J_V, J_VT, J_L0) = range(6)
            J_KT = J_L0 + LEVELS + 1
            J_UPD, J_OUT, J_SS, N_J = J_KT + 1, J_KT + 2, J_KT + 3, J_KT + 4
            LEVEL_SLOT = (1, 2, 3, 1, 2, 3, 1, 2)
            done = sem("rec_result_done")
            free = [sem(f"rec_psum{i}_free") for i in range(4)]
            s_masks = sem("rec_masks_landed")
            s_const = sem("rec_const_ready")
            s_sig = sem("rec_sigmoid_ready")
            s_vraw = sem("rec_vT_ready")
            s_v = sem("rec_v_ready")
            s_f = sem("rec_f_ready")
            s_ln = sem("rec_ln_ready")
            s_G = sem("rec_G_ready")
            s_eg = sem("rec_exp_G_ready")
            s_d = sem("rec_exponent_ready")
            s_e = sem("rec_decay_ready")
            s_x = sem("rec_level_operand_ready")
            s_kn = sem("rec_k_natural_ready")
            s_sq = sem("rec_squares_ready")
            s_ms = sem("rec_mean_square_read")
            s_rms = sem("rec_rstd_ready")
            s_step = sem("rec_dve_step")
            s_out = sem("rec_out_ready")
            LN2 = float(np.log(2.0))
            vT = state[:].rearrange("p c n -> p (c n)")
            kn = sig[2][:].rearrange("p (c n) -> p c n", c=TT)

            def tiles(t):
                return t[:].rearrange("p (c n) -> p c n", c=TT)

            def head(t, it):
                return t[:, bass.ds(it, 1), :].rearrange("p a s -> p (a s)")

            with nc.Block() as block:
                @block.sync
                def _(sp):
                    sp.dma_start(AT[:, 0:LEVELS], masks_in).then_inc(s_masks, 16)
                    with sp.Fori(0, REC_HEADS) as it:
                        for n in range(N_W):
                            ws.load(sp, n, it, N_W)

                @block.gpsimd
                def _(pool):
                    pool.memset(restart[:], 1).then_inc(s_const, 1)
                    pool.wait_ge(s_const, 1)
                    pool.memset(restart[:].rearrange("p (c n) -> p c n", c=TT)[:, :, 0:1], 0)\
                        .then_inc(s_const, 1)

                @block.tensor
                def _(pe):
                    for i in range(4):
                        pe.sem_inc(free[i], 1)
                    pe.sem_inc(s_ms, 1)
                    with pe.Fori(0, REC_HEADS) as it:
                        def projection(n, slot):
                            ws.wait(pe, n, it, N_W)
                            product(pe, psum[slot], full_parts(n)).then_inc(done, 1)

                        pe.wait_ge(free[0], it * 2 + 1)
                        projection(J_GATE, 0)
                        pe.wait_ge(s_ms, it + 1)
                        projection(J_Q, 1)
                        pe.wait_ge(free[2], it * 3 + 1)
                        projection(J_F, 2)
                        pe.wait_ge(free[3], it * 3 + 1)
                        projection(J_V, 3)

                        def per_tile(slot, op):
                            for c in range(TT):
                                ins = op(c, psum[slot][:, c * P:(c + 1) * P])
                            ins.then_inc(done, 1)

                        pe.wait_ge(free[0], it * 2 + 2)
                        pe.wait_ge(s_vraw, it + 1)
                        per_tile(0, lambda c, o: pe.transpose(o, vT[:, c * P:(c + 1) * P], ident[:]))
                        pe.wait_ge(s_f, it + 1)
                        pe.wait_ge(free[1], it * 4 + 2)
                        per_tile(1, lambda c, o: pe.matmul(o, tiles(kh)[:, c], tiles(qh)[:, c],
                                                           start=True, stop=True))
                        for l in range(1, LEVELS + 1):
                            slot = LEVEL_SLOT[l]
                            pe.wait_ge(s_x, it * (LEVELS + 1) + l)
                            if l >= 3:
                                pe.wait_ge(free[slot], it * (4 if slot == 1 else 3) +
                                           {3: 3, 4: 2, 5: 2, 6: 4, 7: 3}[l])
                            xl = tiles(X[l % 2])
                            per_tile(slot, lambda c, o: pe.matmul(o, xl[:, c], xl[:, c],
                                                                  start=True, stop=True))
                        pe.wait_ge(s_x, it * (LEVELS + 1) + LEVELS + 1)
                        pe.wait_ge(s_v, it + 1)
                        xl = tiles(X[(LEVELS + 1) % 2])
                        per_tile(0, lambda c, o: pe.transpose(o, xl[:, c], ident[:]))
                        pe.wait_ge(s_kn, it + 1)
                        pe.wait_ge(free[3], it * 3 + 3)
                        per_tile(3, lambda c, o: pe.matmul(o, kn[:, c], vn[:, c], start=True, stop=True))
                        pe.wait_ge(free[2], it * 3 + 4)
                        pe.wait_ge(free[3], it * 3 + 4)

                        def output(c, o):
                            ins = pe.matmul(o, vn[:, c], AT[:, c], start=True, stop=(c == 0))
                            if c > 0:
                                ins = pe.matmul(o, state[:, c], tiles(q_decay)[:, c], start=False, stop=True)
                            return ins
                        per_tile(0, output)
                        pe.wait_ge(s_sq, it + 1)
                        pe.wait_ge(free[1], it * 4 + 5)
                        for h in range(2):
                            cut = slice(h * HALF, (h + 1) * HALF)
                            ins = pe.matmul(psum[1][:, cut], ones[:], sig[1][:, cut], start=True, stop=True)
                        ins.then_inc(done, 1)

                @block.scalar
                def _(act):
                    act.wait_ge(s_const, 3)
                    act.activation(lb[:], lb[:], ACT.Exp).then_inc(s_const, 1)
                    with act.Fori(0, REC_HEADS) as it:
                        def result(j):
                            act.wait_ge(done, it * N_J + (j + 1))

                        for n in range(N_W):
                            ws.split_hi(act, n, s_ms, it + 1, it, N_W)
                        for j in (J_GATE, J_Q, J_F):
                            result(j)
                            act.activation(sig[j][:], psum[j][:], ACT.Sigmoid).then_inc(s_sig, 1)
                        result(J_V)
                        act.activation(vT, psum[3][:], ACT.Copy).then_inc(s_vraw, 1)
                        result(J_VT)
                        act.activation(vn[:], tiles(psum[0]), ACT.Copy).then_inc(s_v, 1)
                        act.wait_ge(s_f, it + 1)
                        act.activation(X[1][:], sig[2][:], ACT.Ln, scale=2.0 ** 63).then_inc(s_ln, 1)
                        act.activation(X[0][:], X[0][:], ACT.Ln).then_inc(s_ln, 1)
                        act.wait_ge(s_G, it + 1)
                        act.activation(q_decay[:], G[:], ACT.Exp).then_inc(s_eg, 1)
                        act.activation(g_last[:], tiles(G)[:, :, P - 1], ACT.Exp).then_inc(s_eg, 1)
                        for l in range(1, LEVELS + 2):
                            act.wait_ge(s_d, it * (LEVELS + 1) + l)
                            if l <= LEVELS:
                                b = X[l % 2][:].rearrange("p (b n) -> p b n", n=2 ** l)
                                half = 2 ** (l - 1)
                                act.activation(b[:, :, half:], b[:, :, half:], ACT.Exp)
                                act.activation(b[:, :, :half], b[:, :, :half], ACT.Exp, scale=-1.0)\
                                    .then_inc(s_e, 1)
                            else:
                                act.activation(X[l % 2][:], X[l % 2][:], ACT.Exp, scale=-1.0)\
                                    .then_inc(s_e, 1)
                        result(J_KT)
                        act.activation(kn, tiles(psum[0]), ACT.Copy).then_inc(s_kn, 1)
                        result(J_OUT)
                        act.activation(sig[1][:], psum[0][:], ACT.Square).then_inc(s_sq, 1)
                        result(J_SS)
                        act.activation(sig[1][:], psum[1][:], ACT.Ln, bias=eps_col[:, 0:1], scale=1.0 / P)\
                            .then_inc(s_ms, 1)
                        act.wait_ge(s_ms, it + 2)
                        act.activation(sig[1][:], sig[1][:], ACT.Exp, scale=-0.5).then_inc(s_rms, 1)

                @block.vector
                def _(dve):
                    ws.credit(dve)
                    st = Steps(dve, s_step)
                    logits = vec[:, C_LB:C_LB + REC_HEADS]
                    dve.wait_ge(s_const, 2)
                    dve.tensor_tensor(lb[:], logits, logits, ALU.subtract).then_inc(s_const, 1)
                    dve.wait_ge(s_const, 4)
                    st.link(dve.reciprocal(one_minus_lb[:], lb[:]))
                    st.link(dve.tensor_tensor(lb[:], lb[:], one_minus_lb[:], ALU.mult))
                    st.link(dve.tensor_tensor(lb[:], lb[:], lb[:], ALU.subtract))
                    st.link(dve.tensor_scalar(one_minus_lb[:], lb[:], -1.0, 1.0, ALU.mult, ALU.add))
                    dve.wait_ge(s_masks, 16)
                    st.link(dve.tensor_copy(mask[:], AT[:, 0:LEVELS]))
                    with dve.Fori(0, REC_HEADS) as it:
                        st.enter(it, 11)

                        def result(j):
                            dve.wait_ge(done, it * N_J + (j + 1))

                        for n in range(N_W):
                            ws.split_lo(dve, n, it, N_W)
                        dve.wait_ge(s_sig, it * 3 + 1)
                        dve.tensor_tensor(head(oT, it), psum[0][:], sig[0][:], ALU.mult).then_inc(free[0], 1)
                        dve.wait_ge(s_sig, it * 3 + 2)
                        dve.tensor_tensor(qh[:], psum[1][:], sig[1][:], ALU.mult).then_inc(free[1], 1)
                        dve.wait_ge(s_sig, it * 3 + 3)
                        st.link(dve.tensor_scalar(sig[2][:], sig[2][:], one_minus_lb[:, bass.ds(it, 1)],
                                                  lb[:, bass.ds(it, 1)], ALU.mult, ALU.add))
                        st.add(dve.tensor_scalar(kh[:], sig[2][:], -1.0, 1.0, ALU.mult, ALU.add))
                        dve.tensor_scalar(X[0][:], sig[2][:], 2.0 ** -60, None, ALU.max).then_inc(s_f, 1)
                        dve.wait_ge(s_ln, it * 2 + 1)
                        st.link(dve.tensor_scalar(X[1][:], X[1][:], -3.0 * LN2, 0.0, ALU.add, ALU.min))
                        dve.wait_ge(s_ln, it * 2 + 2)
                        st.link(dve.tensor_tensor(X[0][:], X[0][:], X[1][:], ALU.add))
                        dve.tensor_tensor_scan(G[:], restart[:], X[0][:], 0.0, ALU.mult, ALU.add)\
                            .then_inc(s_G, 1)
                        dve.wait_ge(s_G, it + 1)

                        def exponent(l):
                            if l <= LEVELS:
                                n, ref = 2 ** l, 2 ** (l - 1) - 1
                            else:
                                n, ref = P, P - 1
                            if l >= 3:
                                result(J_L0 + l - 2)
                            g = G[:].rearrange("p (b n) -> p b n", n=n)
                            r = g[:, :, ref:ref + 1].to_broadcast([P, S // n, n])
                            dve.tensor_tensor(X[l % 2][:].rearrange("p (b n) -> p b n", n=n), g, r,
                                              ALU.subtract).then_inc(s_d, 1)

                        def operand(l):
                            dve.wait_ge(s_e, it * (LEVELS + 1) + l)
                            if l <= LEVELS:
                                n, half = 2 ** l, 2 ** (l - 1)
                                b, q, k = (t[:].rearrange("p (b n) -> p b n", n=n) for t in (X[l % 2], qh, kh))
                                dve.tensor_tensor(b[:, :, half:], b[:, :, half:], q[:, :, half:], ALU.mult)
                                dve.tensor_tensor(b[:, :, :half], b[:, :, :half], k[:, :, :half], ALU.mult)\
                                    .then_inc(s_x, 1)
                            else:
                                dve.tensor_tensor(X[l % 2][:], X[l % 2][:], kh[:], ALU.mult).then_inc(s_x, 1)

                        def collect_waits(l):
                            result(J_L0 + l)
                            if l >= 1:
                                slot = LEVEL_SLOT[l - 1]
                                dve.wait_ge(free[slot], it * (4 if slot == 1 else 3) +
                                            (3, 2, 2, 4, 3, 3, 5, 4)[l - 1])

                        def collect(l):
                            ps = psum[LEVEL_SLOT[l]]
                            if l == 0:
                                diag = ident[:].unsqueeze(1).to_broadcast([P, TT, P])
                                ins = dve.tensor_tensor(AT[:], tiles(ps), diag, ALU.mult)
                            else:
                                m = mask[:, l - 1, :].unsqueeze(1).to_broadcast([P, TT, P])
                                ins = dve.copy_predicated(AT[:], m, tiles(ps))
                            ins.then_inc(free[LEVEL_SLOT[l]], 1)

                        exponent(1)
                        for l in range(1, LEVELS + 2):
                            if l <= LEVELS:
                                exponent(l + 1)
                            if l >= 2:
                                collect_waits(l - 2)
                            operand(l)
                            if l == 1:
                                dve.wait_ge(s_eg, it * 2 + 2)
                                st.link(dve.tensor_tensor(q_decay[:], q_decay[:], qh[:], ALU.mult))
                            else:
                                collect(l - 2)
                        collect_waits(LEVELS)
                        result(J_UPD)
                        u = tiles(psum[3])
                        st.add(dve.tensor_copy(state[:, 1], u[:, 0]))
                        collect(LEVELS)
                        st.wait()
                        for c in range(1, TT - 1):
                            ins = dve.scalar_tensor_tensor(state[:, c + 1], state[:, c], g_last[:, c:c + 1],
                                                           u[:, c], ALU.mult, ALU.add)
                            if c < TT - 2:
                                st.link(ins)
                            else:
                                ins.then_inc(free[3], 1)
                        dve.wait_ge(s_rms, it + 1)
                        dve.scalar_tensor_tensor(sig[0][:], psum[0][:], vec[:, C_GNORM:C_GNORM + 1],
                                                 sig[1][:], ALU.mult, ALU.mult).then_inc(free[0], 1)
                        dve.wait_ge(free[0], it * 2 + 3)
                        dve.tensor_tensor(head(oT, it), sig[0][:], head(oT, it), ALU.mult).then_inc(s_out, 1)
                        st.leave(REC_HEADS)

        def rec_prepare():
            s_back = sem("x_back")
            s_hi = sem("ro_hi")
            s_lo = sem("ro_lo")

            def sync(sp):
                sp.dma_start(x[:], x_spill).then_inc(s_back, 16)

            def scalar(act):
                for k in range(KT):
                    act.activation(in_hi[:, k], oT[:, k], ACT.Copy).then_inc(s_hi, 1)

            def vector(dve):
                for k in range(KT):
                    dve.wait_ge(s_hi, k + 1)
                    dve.tensor_tensor(in_lo[:, k], oT[:, k], in_hi[:, k].bitcast(F32), ALU.subtract)\
                        .then_inc(s_lo, 1)
                dve.wait_ge(s_back, 16)

            return dict(sync=sync, scalar=scalar, vector=vector, tensor=lambda pe: pe.wait_ge(s_lo, KT))

        def final_phase():
            norm = Norm("fin", [ua[0][:], ub[0][:]], None, rstd[:])
            s_y = sem("y_ready")
            s_store = sem("y_stored")
            with nc.Block() as block:
                @block.scalar
                def _(act):
                    norm.act_stats(act, psum[3])

                @block.tensor
                def _(pe):
                    norm.pe_stats(pe, psum[3])

                @block.vector
                def _(dve):
                    dve.wait_ge(norm.rstd_ready, 2)
                    for k in range(KT):
                        dve.scalar_tensor_tensor(x[:, k], x[:, k], vec[:, C_FINAL + k:C_FINAL + k + 1],
                                                 norm.rstd, ALU.mult, ALU.mult).then_inc(s_y, 1)

                @block.sync
                def _(sp):
                    for k in range(KT):
                        sp.wait_ge(s_y, k + 1)
                        sp.dma_start(outT[:, k, :], x[:, k]).then_inc(s_store, 16)
                    sp.wait_ge(s_store, 16 * KT)

        setup_phase()
        qkv_phase()
        attention_phase()
        out_proj_phase("ao", W_AO, mod_col(0, 2, 0, KT))
        ffn_phase(0, W_FFN0, 6 * KT)
        rec_norm_phase()
        rec_phase()
        out_proj_phase("ro", W_RO, mod_col(1, 2, 0, KT), rec_prepare())
        ffn_phase(1, W_FFN1)
        final_phase()


def per_column(v):
    return np.reshape(v, (-1, P)).T


def kernel(x, c, positions, ada_w, ada_b, norm1_w, norm2_w, final_norm_w, attn_w_in, attn_w_out,
           attn_sinks, rec_w_in, rec_lb_logits, rec_g_norm, rec_w_out, ffn_w_in, ffn_conv_w,
           ffn_conv_b, ffn_w_out):
    import concourse.bacc as bacc
    from concourse.bass_utils import run_bass_kernel_spmd

    def arr(a):
        return np.asarray(a)

    sinks = arr(attn_sinks)[0]
    sink_cols = np.repeat(sinks.reshape(N_HEADS // 2, 2).T, CHUNK, axis=0)
    row = np.arange(P) % HEAD
    inv_freq = np.float32(ROPE_THETA) ** (-np.arange(0, ROPE, 2, dtype=np.float32) / np.float32(ROPE))
    freq = np.where(row < ROPE, inv_freq.astype(np.float32)[row % (ROPE // 2)], np.float32(0))[:, None]
    sign = np.where(row < ROPE // 2, 1.0, np.where(row < ROPE, -1.0, 0.0)).astype(np.float32)[:, None]
    conv_w = arr(ffn_conv_w)
    vec = np.concatenate(
        [per_column(arr(c)), per_column(arr(ada_b)), per_column(arr(norm1_w)), per_column(arr(norm2_w)),
         per_column(arr(final_norm_w)), per_column(arr(rec_lb_logits)), per_column(arr(rec_g_norm)),
         sink_cols, freq.astype(np.float32), sign, per_column(conv_w), per_column(arr(ffn_conv_b))], axis=1)
    assert vec.shape == (P, N_VEC), vec.shape

    def column_tiles(w):
        return w.reshape(KT, P, -1, P).transpose(2, 1, 0, 3)

    def row_tiles(w):
        return w.reshape(-1, P, KT, P)

    q_order = np.arange(D).reshape(2, KT, HEAD).transpose(1, 0, 2).reshape(-1)
    w_in = arr(attn_w_in)[0]
    qkv = column_tiles(np.concatenate([w_in[:, q_order], w_in[:, D:]], axis=1))
    attn_out = column_tiles(arr(attn_w_out)[0][q_order])

    def ffn_tiles(layer):
        up, down = column_tiles(arr(ffn_w_in)[layer]), row_tiles(arr(ffn_w_out)[layer])
        order = []
        for g in range(GROUPS + 1):
            if g < GROUPS:
                order += [up[2 * g], up[FT + 2 * g], up[2 * g + 1], up[FT + 2 * g + 1]]
            if g > 0:
                order += [down[2 * g - 2], down[2 * g - 1]]
        return np.stack(order)

    rec = column_tiles(arr(rec_w_in)[0]).reshape(4, REC_HEADS, P, KT, P)[[3, 0, 1, 2]]
    rec = rec.transpose(1, 0, 2, 3, 4).reshape(-1, P, KT, P)
    rec_out = column_tiles(arr(rec_w_out)[0])
    w_tiles = np.concatenate([qkv, attn_out, ffn_tiles(0), rec, rec_out, ffn_tiles(1)])
    assert w_tiles.shape[0] == N_WTILES
    ada = np.concatenate([column_tiles(arr(ada_w)[i]) for i in range(DEPTH)])

    s_, t_ = np.arange(P)[:, None], np.arange(P)[None, :]
    masks = np.stack([(s_ >> l == t_ >> l) & (s_ >> (l - 1) & 1 == 0) & (t_ >> (l - 1) & 1 == 1)
                      for l in range(1, LEVELS + 1)], axis=1).astype(np.float32)

    ins = {
        "xT": np.ascontiguousarray(arr(x)[0].T.reshape(KT, P, S).transpose(1, 0, 2)),
        "positions": np.ascontiguousarray(arr(positions)[0]),
        "vec": np.ascontiguousarray(vec),
        "ada_tiles": np.ascontiguousarray(ada.reshape(-1, P, KT * P)),
        "w_tiles": np.ascontiguousarray(w_tiles.reshape(-1, P, KT * P)),
        "ident": np.eye(P, dtype=np.float32),
        "masks": np.ascontiguousarray(masks),
    }
    nc = bacc.Bacc("TRN2", target_bir_lowering=False, num_devices=1)
    aps = [nc.dram_tensor(f"in_{n}", a.shape, mybir.dt.from_np(a.dtype), kind="ExternalInput").ap()
           for n, a in ins.items()]
    out = nc.dram_tensor("out", (P, KT, S), F32, kind="ExternalOutput").ap()
    spill = nc.dram_tensor("x_spill", (P, KT, S), F32, kind="Internal").ap()
    trunk_kernel(nc, *aps, out, spill)
    r = run_bass_kernel_spmd(nc, [{f"in_{n}": a for n, a in ins.items()}], core_ids=[0])
    yT = r.results[0]["out"]
    return np.ascontiguousarray(yT.transpose(1, 0, 2).reshape(D, S).T)[None]
```

```python
from contextlib import ExitStack

import numpy as np

import concourse.bass as bass
from concourse import mybir

F32 = mybir.dt.float32
F32R = mybir.dt.float32r
I32 = mybir.dt.int32
U8 = mybir.dt.uint8
ACT = mybir.ActivationFunctionType
ALU = mybir.AluOpType
AX = mybir.AxisListType

P = 128
S = 1024
D = 1024
KT = D // P
HALF = S // 2
DEPTH = 2
CHUNK = 64
N_CHUNKS = S // CHUNK
HEAD = 64
N_HEADS = D // HEAD
ROPE = HEAD // 4
ROPE_THETA = 500000.0
REC_HEADS = 8
TT = S // P
LEVELS = 7
FF = 2816
FT = FF // P
GROUPS = FT // 2
EPS = 1e-6

C_COND = 0
C_ADA_B = C_COND + KT
C_NORM1 = C_ADA_B + DEPTH * 6 * KT
C_NORM2 = C_NORM1 + DEPTH * KT
C_FINAL = C_NORM2 + DEPTH * KT
C_LB = C_FINAL + KT
C_GNORM = C_LB + REC_HEADS
C_SINK = C_GNORM + 1
C_FREQ = C_SINK + N_HEADS // 2
C_SIGN = C_FREQ + 1
C_CONV_W = C_SIGN + 1
C_CONV_B = C_CONV_W + DEPTH * 3 * 2 * FT
N_VEC = C_CONV_B + DEPTH * 2 * FT

N_QKV = D // P + 2
N_OUT = D // P
N_FFN = 3 * FT
N_REC = 4 * REC_HEADS
W_QKV = 0
W_AO = W_QKV + N_QKV
W_FFN0 = W_AO + N_OUT
W_REC = W_FFN0 + N_FFN
W_RO = W_REC + N_REC
W_FFN1 = W_RO + N_OUT
N_WTILES = W_FFN1 + N_FFN

RAW_RING = 2
W_RING = 4


def at(it, per, k):
    return k if it is None else it * per + k


class Steps:

    def __init__(self, eng, sem):
        self.eng, self.sem, self.n, self.it, self.per = eng, sem, 0, None, 0

    def add(self, ins):
        ins.then_inc(self.sem, 1)
        self.n += 1

    def now(self):
        return at(self.it, self.per, self.n)

    def wait(self):
        self.eng.wait_ge(self.sem, self.now())

    def link(self, ins):
        self.add(ins)
        self.wait()

    def enter(self, it, per):
        self.it, self.per, self.start = it, per, self.n

    def leave(self, trips):
        assert self.n - self.start == self.per, (self.n - self.start, self.per)
        self.n = self.start + self.per * trips
        self.it, self.per = None, 0


def two_pi_parts():
    whole = 2 * np.pi
    c1 = np.floor(whole * 32) / 32
    c2 = np.floor((whole - c1) * 2.0 ** 17) / 2.0 ** 17
    return float(c1), float(c2), float(np.float32(whole - c1 - c2))


def trunk_kernel(nc, xT, positions, vec_in, ada_tiles, w_tiles, ident_in, masks_in, outT, x_spill):
    ctx = ExitStack()
    with ctx:
        def sem(name):
            return ctx.enter_context(nc.semaphore(name))

        def alloc(stack, name, shape, dt=F32):
            return stack.enter_context(nc.sbuf_tensor(name, shape, dt))

        vec = alloc(ctx, "vec", [P, N_VEC])
        ident = alloc(ctx, "ident", [P, P])
        ones = alloc(ctx, "ones", [P, P])
        cond = alloc(ctx, "cond_silu", [P, KT])
        mod = alloc(ctx, "mod", [P, DEPTH * 6 * KT])
        gain = alloc(ctx, "gain", [P, DEPTH * 2 * KT])
        eps_col = alloc(ctx, "eps_col", [P, 1])
        w_raw = [alloc(ctx, f"w_raw{i}", [P, KT, P]) for i in range(RAW_RING)]
        w_hi = [alloc(ctx, f"w_hi{i}", [P, KT, P], F32R) for i in range(W_RING)]
        w_lo = [alloc(ctx, f"w_lo{i}", [P, KT, P], F32R) for i in range(W_RING)]
        in_hi = alloc(ctx, "in_hi", [P, KT, S], F32R)
        in_lo = alloc(ctx, "in_lo", [P, KT, S], F32R)
        outer = ExitStack()
        with outer:
            x = alloc(outer, "x", [P, KT, S])
            attn = ExitStack()
            with attn:
                q_raw = alloc(attn, "q_raw", [P, KT, S])
                kv_raw = alloc(attn, "kv_raw", [P, 2, S])
                rope_cos = alloc(attn, "rope_cos", [P, S])
                rope_sin = alloc(attn, "rope_sin", [P, S])
                ada_raw = alloc(attn, "ada_raw", [P, 4, S])
                ada_acc = alloc(attn, "ada_acc", [P, 4, P])
            ffn = ExitStack()
            with ffn:
                g_hi = alloc(ffn, "g_hi", [P, 4, S], F32R)
                g_lo = alloc(ffn, "g_lo", [P, 4, S], F32R)
                ua = [alloc(ffn, f"ua{i}", [P, S]) for i in range(2)]
                ub = [alloc(ffn, f"ub{i}", [P, S]) for i in range(2)]
                rstd = alloc(ffn, "rstd", [P, S])
                ffn_ada_raw = alloc(ffn, "ffn_ada_raw", [P, 2, S])
                ffn_ada_acc = alloc(ffn, "ffn_ada_acc", [P, 8, P])
        rec = ExitStack()
        with rec:
            sig = alloc(rec, "sig", [P, S])
            q_next, f_next, ln_next, vT_next = (
                alloc(rec, n, [P, S]) for n in ("q_next", "f_next", "ln_next", "vT_next"))
            qh = alloc(rec, "qh", [P, S])
            kh = alloc(rec, "kh", [P, S])
            G = alloc(rec, "G", [P, S])
            vn = alloc(rec, "vn", [P, TT, P])
            AT = alloc(rec, "AT", [P, TT, P])
            X = [alloc(rec, f"X{i}", [P, S]) for i in range(2)]
            q_decay = alloc(rec, "q_decay", [P, S])
            state = alloc(rec, "state", [P, TT, P])
            g_last = alloc(rec, "g_last", [P, TT])
            oT = alloc(rec, "oT", [P, REC_HEADS, S])
            mask = alloc(rec, "mask", [P, LEVELS, P], U8)
            restart = alloc(rec, "restart", [P, S], U8)
            lb = alloc(rec, "lb", [P, REC_HEADS])
            one_minus_lb = alloc(rec, "one_minus_lb", [P, REC_HEADS])

        psum = [ctx.enter_context(nc.psum_tensor(f"ps{i}", [P, S], F32)) for i in range(4)]

        def mod_col(layer, which, tile=0, n=1):
            c = layer * 6 * KT + which * KT + tile
            return mod[:, c:c + n]

        class WeightStream:

            def __init__(self, name, base, first=0, gap=0):
                self.base, self.first, self.gap = base, first, gap
                self.raw_ready = [sem(f"{name}_raw_ready{i}") for i in range(RAW_RING)]
                self.hi_ready = sem(f"{name}_w_hi_ready")
                self.lo_ready = sem(f"{name}_w_lo_ready")

            def nth(self, n):
                return n - self.gap if self.gap and n >= self.first else n

            def load(self, sp, n, it=None, per=0):
                r = self.nth(n)
                sp.wait_ge(self.lo_ready, at(it, per, r + 1))
                if it is None:
                    src = w_tiles[self.base + r, :, :]
                else:
                    src = w_tiles[bass.ds(it * per + (self.base + r), 1), :, :]\
                        .rearrange("a p n -> (a p) n")
                sp.dma_start(w_raw[n % RAW_RING][:].rearrange("p k n -> p (k n)"), src)\
                    .then_inc(self.raw_ready[n % RAW_RING], 16)

            def split_hi(self, act, n, released, value, it=None, per=0):
                act.wait_ge(self.raw_ready[n % RAW_RING],
                            at(it, 16 * per // RAW_RING, 16 * (self.nth(n) // RAW_RING + 1)))
                if value is not None:
                    act.wait_ge(released, value)
                act.activation(w_hi[n % W_RING][:], w_raw[n % RAW_RING][:], ACT.Copy)\
                    .then_inc(self.hi_ready, 1)

            def credit(self, dve):
                dve.sem_inc(self.lo_ready, RAW_RING)

            def split_lo(self, dve, n, it=None, per=0):
                dve.wait_ge(self.hi_ready, at(it, per, self.nth(n) + 1))
                dve.tensor_tensor(w_lo[n % W_RING][:], w_raw[n % RAW_RING][:],
                                  w_hi[n % W_RING][:].bitcast(F32), ALU.subtract)\
                    .then_inc(self.lo_ready, 1)

            FIRST = RAW_RING

            def begin_sync(self, sp, before=None, n=0):
                if before is not None:
                    sp.wait_ge(before.lo_ready, before.nth(n) + 1 + RAW_RING)
                for i in range(self.FIRST):
                    self.load(sp, i)

            def begin_act(self, act):
                for i in range(self.FIRST):
                    self.split_hi(act, i, None, None)

            def begin_dve(self, dve):
                for i in range(self.FIRST):
                    self.split_lo(dve, i)

            def wait(self, pe, n, it=None, per=0):
                pe.wait_ge(self.lo_ready, at(it, per, self.nth(n) + 1 + RAW_RING))

        def product(pe, out, parts, ready=None, ks=None):
            last = len(parts) - 1
            for k in ks or range(len(parts)):
                wh, wl, mh, ml = parts[k]
                if ready is not None:
                    pe.wait_ge(ready, k + 1)
                for j, (w, m) in enumerate(((wh, mh), (wh, ml), (wl, mh))):
                    for h in range(2):
                        cut = slice(h * HALF, (h + 1) * HALF)
                        ins = pe.matmul(out[:, cut], w, m[:, cut], start=(k == 0 and j == 0),
                                        stop=(k == last and j == 2))
            return ins

        def first_two(pe, ws, n, ready, done):
            for i in range(2):
                ws.wait(pe, n + i)
            for k in range(KT):
                for i in range(2):
                    if i == 0:
                        pe.wait_ge(ready, k + 1)
                    ins = product(pe, psum[i], full_parts(n + i), None, [k])
                    if k == KT - 1:
                        ins.then_inc(done, 1)

        def full_parts(n):
            s = n % W_RING
            return [(w_hi[s][:, k], w_lo[s][:, k], in_hi[:, k], in_lo[:, k]) for k in range(KT)]

        class Norm:

            def __init__(self, name, sq, scaled, rstd):
                self.sq, self.scaled, self.rstd = sq, scaled, rstd
                self.sq_ready = sem(f"{name}_sq_ready")
                self.summed = sem(f"{name}_sq_summed")
                self.rstd_ready = sem(f"{name}_rstd_ready")
                if scaled is not None:
                    self.scaled_ready = sem(f"{name}_scaled_ready")
                    self.hi_ready = sem(f"{name}_in_hi_ready")
                    self.in_ready = sem(f"{name}_in_ready")

            def act_square(self, act, k):
                if k >= 3:
                    act.wait_ge(self.summed, k - 2)
                act.activation(self.rstd if k == 0 else self.sq[k % 2], x[:, k], ACT.Square)\
                    .then_inc(self.sq_ready, 1)

            def dve_sum(self, dve, k):
                if k == 0:
                    return
                dve.wait_ge(self.sq_ready, k + 1)
                if k >= 2:
                    dve.wait_ge(self.summed, k - 1)
                dve.tensor_tensor(self.rstd, self.rstd, self.sq[k % 2], ALU.add).then_inc(self.summed, 1)

            def pe_total(self, pe, ss):
                pe.wait_ge(self.summed, KT - 1)
                for h in range(2):
                    cut = slice(h * HALF, (h + 1) * HALF)
                    ins = pe.matmul(ss[:, cut], ones[:], self.rstd[:, cut], start=True, stop=True)
                ins.then_inc(self.rstd_ready, 1)

            def act_rstd(self, act, ss):
                act.wait_ge(self.rstd_ready, 1)
                act.activation(self.rstd, ss[:], ACT.Ln, bias=eps_col[:, 0:1], scale=1.0 / D)\
                    .then_inc(self.rstd_ready, 1)
                act.wait_ge(self.rstd_ready, 2)
                act.activation(self.rstd, self.rstd, ACT.Exp, scale=-0.5).then_inc(self.rstd_ready, 1)

            def act_apply(self, act, shift):
                for k in range(KT):
                    act.wait_ge(self.scaled_ready, k + 1)
                    act.activation(in_hi[:, k], self.scaled[k % 2], ACT.Identity,
                                   bias=shift[:, k:k + 1]).then_inc(self.hi_ready, 1)

            def dve_apply(self, dve, g, shift):
                dve.wait_ge(self.rstd_ready, 3)
                for k in range(KT):
                    if k >= 2:
                        dve.wait_ge(self.in_ready, k - 1)
                    dve.scalar_tensor_tensor(self.scaled[k % 2], x[:, k], g[:, k:k + 1], self.rstd,
                                             ALU.mult, ALU.mult).then_inc(self.scaled_ready, 1)
                    if k >= 1:
                        self.dve_rest(dve, k - 1, shift)
                self.dve_rest(dve, KT - 1, shift)

            def dve_rest(self, dve, k, shift):
                dve.wait_ge(self.hi_ready, k + 1)
                dve.scalar_tensor_tensor(in_lo[:, k], self.scaled[k % 2], shift[:, k:k + 1],
                                         in_hi[:, k].bitcast(F32), ALU.add, ALU.subtract)\
                    .then_inc(self.in_ready, 1)

        class Ada:

            def __init__(self, name, first, width, raw, acc, cols):
                self.first, self.width, self.raw, self.acc, self.cols = first, width, raw, acc, cols
                self.landed = [sem(f"{name}_ada_landed{i}") for i in range(len(raw))]
                self.acc_ready = sem(f"{name}_ada_acc_ready")
                self.step_sem = sem(f"{name}_ada_step")
                self.col_ready = sem(f"{name}_ada_col_ready")
                self.col_taken = sem(f"{name}_ada_col_taken")
                self.mod_ready = sem(f"{name}_mod_ready")

            def load(self, sp, b, it=None, per=0):
                sp.wait_ge(self.acc_ready, at(it, per, b + 1))
                first = self.first + b * self.width
                if it is None:
                    src = ada_tiles[first:first + self.width]
                else:
                    src = ada_tiles[bass.ds(it * (per * self.width) + first, self.width)]
                slot = b % len(self.raw)
                sp.dma_start(self.raw[slot], src.rearrange("a p n -> p a n")).then_inc(self.landed[slot], 16)

            def credit(self, dve):
                dve.sem_inc(self.acc_ready, len(self.raw))

            def sum_tiles(self, dve, steps, b, it=None, per=0):
                slot, acc = b % len(self.raw), self.acc[b % len(self.acc)]
                turns = len(self.raw)
                dve.wait_ge(self.landed[slot], at(it, 16 * per // turns, 16 * (b // turns + 1)))
                dve.wait_ge(self.col_ready, at(it, per, b + 1))
                w = self.raw[slot].rearrange("p a (k n) -> p a k n", k=KT)
                steps.link(dve.tensor_scalar(acc, w[:, :, 0], cond[:, 0:1], None, ALU.mult))
                for k in range(1, KT):
                    ins = dve.scalar_tensor_tensor(acc, w[:, :, k], cond[:, k:k + 1], acc,
                                                   ALU.mult, ALU.add)
                    if k < KT - 1:
                        steps.link(ins)
                    else:
                        ins.then_inc(self.acc_ready, 1)

            def whole(self, pe, b):
                slot = b % len(self.raw)
                pe.wait_ge(self.landed[slot], 16 * (b // len(self.raw) + 1))
                for i in range(self.width):
                    col = b * self.width + i
                    for k in range(KT):
                        ins = pe.matmul(self.cols[:, col:col + 1], self.raw[slot][:, i, k * P:(k + 1) * P],
                                        cond[:, k:k + 1], start=(k == 0), stop=(k == KT - 1))
                ins.then_inc(self.acc_ready, 1)

            def pe_credit(self, pe):
                pe.sem_inc(self.col_ready, len(self.acc))
                pe.sem_inc(self.col_taken, 1)

            def columns(self, pe, b, col, taken=None, it=None, per=0):
                pe.wait_ge(self.acc_ready, at(it, per, b + 1 + len(self.raw)))
                if taken is not None:
                    pe.wait_ge(self.col_taken, taken)
                for i in range(self.width):
                    ins = pe.matmul(self.cols[:, col + i:col + i + 1], self.acc[b % len(self.acc)][:, i],
                                    ones[:, 0:1], start=True, stop=True)
                ins.then_inc(self.col_ready, 1)

            def take(self, act, b, n, it=None, per=0):
                act.wait_ge(self.col_ready, at(it, per, b + 1 + len(self.acc)))
                first = self.first + (b + 1 - n) * self.width
                dst = mod[:, first:first + n * self.width] if it is None else \
                    mod[:, bass.ds(it * (per * self.width) + first, n * self.width)]
                act.activation(dst, self.cols[:, 0:n * self.width], ACT.Copy).then_inc(self.col_taken, 1)

            def finish(self, dve, takes, end, norms):
                dve.wait_ge(self.col_taken, takes + 1)
                m = mod[:, self.first:end]
                dve.tensor_tensor(m, m, vec[:, C_ADA_B + self.first:C_ADA_B + end], ALU.add)\
                    .then_inc(self.mod_ready, 1)
                dve.wait_ge(self.mod_ready, 1)
                for layer, which in norms:
                    g = gain[:, (2 * layer + which) * KT:(2 * layer + which + 1) * KT]
                    col = (C_NORM1, C_NORM2)[which] + layer * KT
                    dve.scalar_tensor_tensor(g, mod_col(layer, 3 * which + 1, 0, KT), 1.0,
                                             vec[:, col:col + KT], ALU.add, ALU.mult)\
                        .then_inc(self.mod_ready, 1)
                dve.wait_ge(self.mod_ready, 1 + len(norms))

        SETUP_ADA = 2 * KT

        def setup_phase(norm, next_ws):
            s_vec = sem("vectors_landed")
            s_ident = sem("identity_landed")
            s_x = [sem(f"x_tile{k}_landed") for k in range(KT)]
            s_cond = sem("cond_ready")
            s_ones = sem("ones_ready")
            s_pos = sem("positions_landed")
            s_step = sem("angle_step")
            s_ang = sem("angle_ready")
            s_rope = sem("rope_ready")
            pos_i = rope_cos[:].bitcast(I32)
            ang, turns = ada_raw[:, 2], ada_raw[:, 3]
            shift = Ada("sh", 0, 4, [q_raw[:, 0:4]], [], psum[1])
            ada = Ada("sc", KT, 4, [q_raw[:, 4:8]],
                      [kv_raw[:, 1, 0:HALF].rearrange("p (a n) -> p a n", a=4)], psum[2])
            with nc.Block() as block:
                @block.sync
                def _(sp):
                    sp.dma_start(vec[:], vec_in).then_inc(s_vec, 16)
                    sp.dma_start(pos_i, positions.partition_broadcast(P)).then_inc(s_pos, 16)
                    shift.load(sp, 0)
                    ada.load(sp, 0)
                    for k in range(KT):
                        sp.dma_start(x[:, k], xT[:, k]).then_inc(s_x[k], 16)
                    shift.load(sp, 1)
                    ada.load(sp, 1)
                    next_ws.begin_sync(sp)
                    sp.dma_start(ident[:], ident_in).then_inc(s_ident, 16)
                    sp.wait_ge(s_ident, 16)

                @block.gpsimd
                def _(pool):
                    pool.memset(ones[:], 1.0).then_inc(s_ones, 1)
                    pool.memset(eps_col[:], EPS).then_inc(s_ones, 1)

                @block.scalar
                def _(act):
                    act.wait_ge(s_vec, 16)
                    act.activation(cond[:], vec[:, C_COND:C_COND + KT], ACT.Silu).then_inc(s_cond, 1)
                    act.wait_ge(s_ones, 2)
                    for k in range(KT):
                        act.wait_ge(s_x[k], 16)
                        norm.act_square(act, k)
                    act.wait_ge(s_ang, 1)
                    act.activation(rope_sin[:], rope_sin[:], ACT.Sin).then_inc(s_rope, 1)
                    act.wait_ge(s_ang, 2)
                    act.activation(rope_cos[:], rope_cos[:], ACT.Sin).then_inc(s_rope, 1)
                    norm.act_rstd(act, psum[0])
                    act.wait_ge(shift.acc_ready, 2 + len(shift.raw))
                    act.activation(mod[:, 0:KT], shift.cols[:, 0:KT], ACT.Copy)\
                        .then_inc(shift.col_taken, 1)
                    ada.take(act, 1, 2)
                    next_ws.begin_act(act)

                @block.tensor
                def _(pe):
                    pe.sem_inc(shift.col_taken, 1)
                    ada.pe_credit(pe)
                    pe.wait_ge(s_cond, 1)
                    shift.whole(pe, 0)
                    pe.wait_ge(s_ones, 2)
                    ada.columns(pe, 0, 0)
                    shift.whole(pe, 1)
                    norm.pe_total(pe, psum[0])
                    ada.columns(pe, 1, 4)

                @block.vector
                def _(dve):
                    next_ws.credit(dve)
                    shift.credit(dve)
                    ada.credit(dve)
                    steps = Steps(dve, ada.step_sem)
                    pos = Steps(dve, s_step)
                    dve.wait_ge(s_vec, 16)
                    dve.wait_ge(s_pos, 16)
                    pos.link(dve.tensor_copy(ang, pos_i))
                    pos.link(dve.tensor_scalar(ang, ang, vec[:, C_FREQ:C_FREQ + 1], None, ALU.mult))
                    magic = 1.5 * 2.0 ** 23
                    parts = two_pi_parts()

                    def reduce_angle(dst, src, unit, shift):
                        pos.link(dve.tensor_scalar(turns, src, 1.0 / (2 * np.pi * unit), shift,
                                                   ALU.mult, ALU.add))
                        pos.link(dve.tensor_scalar(turns, turns, magic, None, ALU.add))
                        pos.link(dve.tensor_scalar(turns, turns, magic, None, ALU.subtract))
                        for c in parts:
                            pos.link(dve.scalar_tensor_tensor(dst, turns, -c * unit, src,
                                                              ALU.mult, ALU.add))
                            src = dst

                    pi32 = 3.1415925

                    def sine():
                        reduce_angle(rope_sin[:], ang, 1.0, 0.0)
                        dve.tensor_scalar(rope_sin[:], rope_sin[:], pi32, -pi32, ALU.min, ALU.max)\
                            .then_inc(s_ang, 1)

                    def cosine():
                        reduce_angle(rope_cos[:], ang, 1.0, 0.25)
                        pos.link(dve.tensor_scalar(rope_cos[:], rope_cos[:], float(np.pi / 2), None, ALU.add))
                        dve.tensor_scalar(rope_cos[:], rope_cos[:], pi32, -pi32, ALU.min, ALU.max)\
                            .then_inc(s_ang, 1)

                    reduce_angle(ang, ang, 4096.0, 0.0)
                    sine()
                    dve.wait_ge(s_cond, 1)
                    ada.sum_tiles(dve, steps, 0)
                    cosine()
                    for k in range(KT):
                        norm.dve_sum(dve, k)
                    ada.sum_tiles(dve, steps, 1)
                    ada.finish(dve, 1, SETUP_ADA, [(0, 0)])
                    shift.finish(dve, 1, KT, [])
                    next_ws.begin_dve(dve)
                    dve.wait_ge(s_rope, 1)
                    dve.tensor_scalar(rope_sin[:], rope_sin[:], vec[:, C_SIGN:C_SIGN + 1], None, ALU.mult)

        def qkv_phase(norm, ws):
            TURN = 4
            TURNS = N_QKV // TURN
            RING = 2
            PAIRS = 2
            PT = TURN * PAIRS
            done, evac = sem("qkv_done"), sem("qkv_evac")
            ada = Ada("q", SETUP_ADA, 2, [ada_raw[:, 0:2], ada_raw[:, 2:4]],
                      [ada_acc[:, 0:2], ada_acc[:, 2:4]], psum[3])

            def tiles(eng, body, steps=()):
                with eng.Fori(0, TURNS) as it:
                    for s, k in steps:
                        s.enter(it, k)
                    for n in range(TURN):
                        body(n, it)
                    for s, k in steps:
                        s.leave(TURNS)
                for n in range(TURNS * TURN, N_QKV):
                    body(n, None)

            def ada_batches(n, it):
                return [] if it is None else [n * PAIRS + i for i in range(PAIRS)]

            with nc.Block() as block:
                @block.sync
                def _(sp):
                    def body(n, it):
                        for b in ada_batches(n, it):
                            ada.load(sp, b, it, PT)
                        if it is not None:
                            ws.load(sp, n + 2, it, TURN)
                    tiles(sp, body)

                @block.vector
                def _(dve):
                    ada.credit(dve)
                    steps = Steps(dve, ada.step_sem)
                    norm.dve_apply(dve, gain[:, 0:KT], mod_col(0, 0, 0, KT))

                    def body(n, it):
                        for b in ada_batches(n, it):
                            ada.sum_tiles(dve, steps, b, it, PT)
                        if it is not None:
                            ws.split_lo(dve, n + 2, it, TURN)
                    tiles(dve, body, ((steps, PT * (KT - 1)),))
                    ada.finish(dve, TURNS, 6 * KT, [(0, 1)])

                @block.tensor
                def _(pe):
                    ada.pe_credit(pe)
                    pe.sem_inc(evac, RING)

                    def job(n, it, ready=None):
                        ws.wait(pe, n, it, TURN)
                        pe.wait_ge(evac, at(it, TURN, n + 1))
                        product(pe, psum[n % RING], full_parts(n), ready).then_inc(done, 1)

                    def body(n, it):
                        job(n, it, norm.in_ready if n == 0 else None)
                        for b in ada_batches(n, it):
                            ada.columns(pe, b, 2 * b, at(it, 1, 1) if b == 0 else None, it, PT)
                    tiles(pe, body)

                @block.scalar
                def _(act):
                    def take(n, it):
                        act.wait_ge(done, at(it, TURN, n + 1))
                        if it is None:
                            dst = kv_raw[:, n - KT]
                        else:
                            dst = q_raw[:, bass.ds(it * TURN + n, 1)].rearrange("p a s -> p (a s)")
                        act.activation(dst, psum[n % RING][:], ACT.Copy).then_inc(evac, 1)

                    norm.act_apply(act, mod_col(0, 0, 0, KT))

                    def body(n, it):
                        take(n, it)
                        if it is not None:
                            ws.split_hi(act, n + 2, None, None, it, TURN)
                            if n == TURN - 1:
                                ada.take(act, PT - 1, PT, it, PT)

                    tiles(act, body)
        def out_proj_phase(name, ws, first, gate, norm, next_ws, prepare=None):
            split = ws.FIRST
            RING = 3
            done, evac = sem(f"{name}_done"), sem(f"{name}_evac")
            with nc.Block() as block:
                @block.sync
                def _(sp):
                    if prepare:
                        prepare["sync"](sp)
                    for n in range(split, N_OUT):
                        ws.load(sp, first + n)
                    next_ws.begin_sync(sp, ws, first + N_OUT - 1)

                @block.scalar
                def _(act):
                    if prepare:
                        prepare["scalar"](act)

                    def square(k):
                        act.wait_ge(evac, k + 1)
                        norm.act_square(act, k)

                    for n in range(N_OUT):
                        if n >= split:
                            ws.split_hi(act, first + n, done, n - W_RING + 1 if n >= W_RING else None)
                        if n >= 2:
                            square(n - 2)
                    square(N_OUT - 2)
                    next_ws.begin_act(act)
                    square(N_OUT - 1)
                    norm.act_rstd(act, psum[3])

                @block.vector
                def _(dve):
                    next_ws.credit(dve)
                    if prepare:
                        prepare["vector"](dve)

                    def take(n):
                        dve.wait_ge(done, n + 1)
                        dve.scalar_tensor_tensor(x[:, n], psum[n % RING][:], gate[:, n:n + 1], x[:, n],
                                                 ALU.mult, ALU.add).then_inc(evac, 1)

                    for n in range(N_OUT):
                        if n >= split:
                            ws.split_lo(dve, first + n)
                        if n >= 2:
                            take(n - 2)
                        if n >= 3:
                            norm.dve_sum(dve, n - 3)
                    take(N_OUT - 2)
                    norm.dve_sum(dve, N_OUT - 3)
                    next_ws.begin_dve(dve)
                    take(N_OUT - 1)
                    norm.dve_sum(dve, N_OUT - 2)
                    norm.dve_sum(dve, N_OUT - 1)

                @block.tensor
                def _(pe):
                    if prepare:
                        first_two(pe, ws, first, prepare["ready"], done)
                    for n in range(2 if prepare else 0, N_OUT):
                        ws.wait(pe, first + n)
                        if n >= RING:
                            pe.wait_ge(evac, n - RING + 1)
                        product(pe, psum[n % RING], full_parts(first + n)).then_inc(done, 1)
                    norm.pe_total(pe, psum[3])

        AT_TURN = 4
        AT_FIRST = 2
        AT_TURNS = (N_CHUNKS - AT_FIRST) // AT_TURN
        NB = N_HEADS // 2
        at_ctx = ExitStack()
        with at_ctx:
            for n, w in (("at_x", KT), ("at_q", KT), ("at_kv", 2), ("at_cos", 1), ("at_sin", 1)):
                alloc(at_ctx, n, [P, w, S])
            q_rot = alloc(at_ctx, "q_rot", [P, 2, KT, CHUNK])
            q_swap = alloc(at_ctx, "q_swap", [P, KT, CHUNK])
            k_rot = alloc(at_ctx, "k_rot", [P, AT_TURN, CHUNK])
            k_swap = alloc(at_ctx, "k_swap", [P, CHUNK])
            v_keys = alloc(at_ctx, "v_keys", [P, 2, CHUNK])
            v_win = alloc(at_ctx, "v_win", [P, P])
            probs_buf = alloc(at_ctx, "probs", [P, N_HEADS // 2, P])
            probsT = alloc(at_ctx, "probsT", [P, S])
            row_max, sink_exp, neg_max, row_sum, inv_den = (
                alloc(at_ctx, n, [P, NB]) for n in ("row_max", "sink_exp", "neg_max", "row_sum", "inv_den"))

        def attention_phase(next_ws):
            s_rot = sem("at_rope_step")
            s_in = sem("at_chunk_rotated")
            s_qk = sem("at_scores_ready")
            s_mx = sem("at_max_step")
            s_bias = sem("at_bias_ready")
            s_exp = sem("at_exp_ready")
            s_esink = sem("at_sink_exp_ready")
            s_probs = sem("at_probs_ready")
            s_pT = sem("at_probs_transposed")
            s_pc = sem("at_probsT_copied")
            s_keys = sem("at_window_ready")
            s_vT = sem("at_v_transposed")
            s_v = sem("at_v_copied")
            s_o = sem("at_out_ready")
            s_ohi = sem("at_out_hi")
            s_olo = sem("at_out_lo")
            sink = vec[:, C_SINK:C_SINK + NB]
            probs = probs_buf[:]
            scores = [psum[i][:].rearrange("p (b k) -> p b k", b=NB) for i in range(2)]
            v_ps, out_ps = psum[2][:, 0:P], psum[2][:, HALF:]
            pT_ps = psum[3]
            scale = HEAD ** -0.5
            swap = [i + ROPE // 2 if i < ROPE // 2 else i - ROPE // 2 if i < ROPE else i for i in range(32)]

            def chunks(eng, body, steps=()):
                for n in range(AT_FIRST):
                    body(n, None)
                with eng.Fori(0, AT_TURNS) as it:
                    for s, k in steps:
                        s.enter(it, AT_TURN * k)
                    for c in range(AT_TURN):
                        body(AT_FIRST + c, it)
                    for s, k in steps:
                        s.leave(AT_TURNS)
                for n in range(AT_FIRST + AT_TURN * AT_TURNS, N_CHUNKS):
                    body(n, None)

            def keys(n):
                if n == 0:
                    return slice(0, 1), CHUNK
                lo, hi = sorted(((n - 1) % AT_TURN, n % AT_TURN))
                return slice(lo, hi + 1, hi - lo), 2 * CHUNK

            def tokens(n, it):
                return slice(n * CHUNK, (n + 1) * CHUNK) if it is None else \
                    bass.ds(it * (AT_TURN * CHUNK) + n * CHUNK, CHUNK)

            def count(n, it, k):
                return at(it, AT_TURN, n + k)

            with nc.Block() as block:
                @block.vector
                def _(dve):
                    rot, mx = Steps(dve, s_rot), Steps(dve, s_mx)

                    def rotate(n, it):
                        cut, slot = tokens(n, it), n % AT_TURN
                        q = q_rot[:, n % 2]
                        cos = rope_cos[:, cut].unsqueeze(1).to_broadcast([P, KT, CHUNK])
                        sin = rope_sin[:, cut].unsqueeze(1).to_broadcast([P, KT, CHUNK])
                        if n >= 1:
                            dve.wait_ge(s_in, count(n, it, 0))
                        if n >= 2:
                            dve.wait_ge(s_qk, count(n, it, -1))
                        rot.add(dve.tensor_tensor(q_swap[:], q_raw[:, :, cut], sin, ALU.mult))
                        rot.add(dve.tensor_tensor(k_swap[:], kv_raw[:, 0, cut], rope_sin[:, cut], ALU.mult))
                        rot.add(dve.tensor_tensor(k_rot[:, slot], kv_raw[:, 0, cut], rope_cos[:, cut],
                                                  ALU.mult))
                        rot.wait()
                        rot.add(dve.tensor_tensor(q, q_raw[:, :, cut], cos, ALU.mult))
                        rot.add(dve.stream_shuffle(q_swap[:], q_swap[:], swap))
                        rot.add(dve.stream_shuffle(k_swap[:], k_swap[:], swap))
                        rot.wait()
                        rot.add(dve.tensor_tensor(k_rot[:, slot], k_rot[:, slot], k_swap[:], ALU.add))
                        rot.wait()
                        dve.tensor_tensor(q, q, q_swap[:], ALU.add).then_inc(s_in, 1)

                    def window(n, it):
                        own = min(n % AT_TURN, 1)
                        if n > 0:
                            dve.tensor_copy(v_keys[:, 1 - own], kv_raw[:, 1, tokens(n - 1, it)])\
                                .then_inc(s_keys, 1)
                        dve.tensor_copy(v_keys[:, own], kv_raw[:, 1, tokens(n, it)]).then_inc(s_keys, 1)

                    def output_lo(n, it):
                        dve.wait_ge(s_ohi, count(n, it, 1))
                        cut = tokens(n, it)
                        dve.tensor_tensor(in_lo[:, :, cut], out_ps.rearrange("p (t q) -> p t q", t=KT),
                                          in_hi[:, :, cut].bitcast(F32), ALU.subtract).then_inc(s_olo, 1)

                    def body(n, it):
                        w = keys(n)[1]
                        dve.wait_ge(s_qk, count(n, it, 1))
                        mx.link(dve.tensor_reduce(row_max[:], scores[n % 2][:, :, 0:w], AX.X, ALU.max))
                        mx.link(dve.scalar_tensor_tensor(row_max[:], row_max[:], scale, sink,
                                                         ALU.mult, ALU.max))
                        mx.link(dve.tensor_tensor(sink_exp[:], sink, row_max[:], ALU.subtract))
                        dve.tensor_scalar(neg_max[:], row_max[:], -1.0, None, ALU.mult).then_inc(s_bias, 1)
                        if n + 2 < N_CHUNKS:
                            rotate(n + 2, it)
                        dve.wait_ge(s_esink, count(n, it, 1))
                        mx.link(dve.tensor_tensor(inv_den[:], row_sum[:], sink_exp[:], ALU.add))
                        mx.link(dve.reciprocal(inv_den[:], inv_den[:]))
                        pr = probs[:, :, 0:w]
                        dve.tensor_tensor(pr, pr, inv_den[:].unsqueeze(2).to_broadcast([P, NB, w]),
                                          ALU.mult).then_inc(s_probs, 1)
                        if n + 1 < N_CHUNKS:
                            dve.wait_ge(s_vT, count(n, it, 1))
                        if n > 0:
                            output_lo(n - 1, it)
                        if n + 1 < N_CHUNKS:
                            window(n + 1, it)

                    next_ws.credit(dve)
                    rotate(0, None)
                    window(0, None)
                    rotate(1, None)
                    next_ws.begin_dve(dve)
                    chunks(dve, body, ((rot, 7), (mx, 5)))
                    output_lo(N_CHUNKS - 1, None)

                @block.tensor
                def _(pe):
                    def score(n, it):
                        slots, w = keys(n)
                        sc = scores[n % 2]
                        pe.wait_ge(s_in, count(n, it, 1))
                        if n >= 2:
                            pe.wait_ge(s_exp, count(n, it, -1))
                        for b in range(NB):
                            rows = slice(HEAD * (b // 4), HEAD * (b // 4) + HEAD)
                            t = 2 * (b % 4)
                            ins = pe.matmul(sc[:, b, 0:w], q_rot[rows, n % 2, t:t + 2], k_rot[rows, slots],
                                            start=True, stop=True)
                        ins.then_inc(s_qk, 1)

                    def output(n, it):
                        w = keys(n)[1]
                        pe.wait_ge(s_pc, count(n, it, 1))
                        pe.wait_ge(s_v, count(n, it, 1))
                        if n > 0:
                            pe.wait_ge(s_olo, count(n, it, 0))
                        for kv in range(2):
                            rows = slice(HEAD * kv, HEAD * kv + HEAD)
                            ins = pe.matmul(out_ps[rows, :], v_win[0:w, rows],
                                            probsT[0:w, kv * HALF:(kv + 1) * HALF], start=True, stop=True)
                        ins.then_inc(s_o, 1)

                    def body(n, it):
                        w = keys(n)[1]
                        if n + 1 < N_CHUNKS:
                            score(n + 1, it)
                        if n > 0:
                            output(n - 1, it)
                            pe.wait_ge(s_v, count(n, it, 0))
                        pe.wait_ge(s_keys, at(it, 2 * AT_TURN, 2 * n + 1))
                        pe.transpose(v_ps[0:w], v_keys[:].rearrange("p a b -> p (a b)")[:, 0:w], ident[:])\
                            .then_inc(s_vT, 1)
                        pe.wait_ge(s_probs, count(n, it, 1))
                        if n > 0:
                            pe.wait_ge(s_pc, count(n, it, 0))
                        for b in range(NB):
                            ins = pe.transpose(pT_ps[0:w, b * P:(b + 1) * P], probs[:, b, 0:w], ident[:])
                        ins.then_inc(s_pT, 1)

                    score(0, None)
                    chunks(pe, body)
                    output(N_CHUNKS - 1, None)

                @block.scalar
                def _(act):
                    def output_hi(n, it):
                        act.wait_ge(s_o, count(n, it, 1))
                        act.activation(in_hi[:, :, tokens(n, it)],
                                       out_ps.rearrange("p (t q) -> p t q", t=KT),
                                       ACT.Copy).then_inc(s_ohi, 1)

                    def body(n, it):
                        w = keys(n)[1]
                        act.wait_ge(s_bias, count(n, it, 1))
                        for b in range(NB):
                            ins = act.activation(probs[:, b, 0:w], scores[n % 2][:, b, 0:w], ACT.Exp,
                                                 bias=neg_max[:, b:b + 1], scale=scale,
                                                 accum_out=row_sum[:, b:b + 1])
                        ins.then_inc(s_exp, 1)
                        act.activation(sink_exp[:], sink_exp[:], ACT.Exp).then_inc(s_esink, 1)
                        if n > 0:
                            output_hi(n - 1, it)
                        act.wait_ge(s_vT, count(n, it, 1))
                        act.activation(v_win[0:w, :], v_ps[0:w], ACT.Copy).then_inc(s_v, 1)
                        act.wait_ge(s_pT, count(n, it, 1))
                        act.activation(probsT[0:w, :], pT_ps[0:w, :], ACT.Copy).then_inc(s_pc, 1)

                    next_ws.begin_act(act)
                    chunks(act, body)
                    output_hi(N_CHUNKS - 1, None)

                @block.sync
                def _(sp):
                    next_ws.begin_sync(sp)

        def ffn_phase(layer, ws, norm, next_norm, next_ws=None, next_ada=None):
            name = f"f{layer}"
            done = sem(f"{name}_job_done")
            taken = sem(f"{name}_job_taken")
            s_tap = sem(f"{name}_tap_ready")
            s_cs = sem(f"{name}_conv_step")
            s_silu = sem(f"{name}_silu_ready")
            s_gate = sem(f"{name}_gated_ready")
            s_ghi = sem(f"{name}_g_hi_ready")
            s_glo = sem(f"{name}_g_lo_ready")
            gate2 = mod_col(layer, 5, 0, KT)
            cw = C_CONV_W + layer * 6 * FT
            cb = C_CONV_B + layer * 2 * FT
            GW, GJ = 6, 4 + KT
            PW, PJ, PH = 2 * GW, 2 * GJ, 4
            STEPS = 2 * 2 * 2

            def groups(eng, hidden, output, skip=None, steps=()):
                hidden(0, 0, 0, None)
                if skip:
                    skip()
                with eng.Fori(0, (GROUPS - 1) // 2) as it:
                    for s, k in steps:
                        s.enter(it, k)
                    for g in (1, 2):
                        hidden(g, GW * g, GJ * g, it)
                        output(g - 1, GW * g + 4, GJ * g + 4, it)
                    for s, k in steps:
                        s.leave((GROUPS - 1) // 2)
                output(GROUPS - 1, GW * GROUPS, GJ * GROUPS, None)

            def released(n, it):
                g, i = divmod(n, GW)
                if n < W_RING:
                    return None
                if n == GW * GROUPS or n == GW * GROUPS + 1:
                    return GJ * (GROUPS - 1) + 3 + i
                return at(it, PJ, (GJ * (g - 1) + 3, GJ * (g - 1) + 4, GJ * g, GJ * g,
                                   GJ * g + 1, GJ * g + 2)[i])

            def col(start, f, it):
                return vec[:, start + f:start + f + 1] if it is None else \
                    vec[:, bass.ds(it * PH + (start + f), 1)]

            RING = 3
            if next_ada is not None:
                AB, PB = 2, 4
                ada = Ada(name, next_ada, 2, [ffn_ada_raw[:]],
                          [ffn_ada_acc[:, 2 * i:2 * i + 2] for i in range(PB)], psum[3])

            def ada_batches(g, i):
                if next_ada is None:
                    return []
                return [3 * i, 3 * i + 1, 3 * i + 2][:3 - 2 * i] if g == 0 else [PB + 2 * (g - 1) + i]

            with nc.Block() as block:
                @block.sync
                def _(sp):
                    def load(n, k, it):
                        for i in range(k):
                            ws.load(sp, n + i, it, PW)

                    def hidden(g, n, j, it):
                        first = 0 if g > 0 else ws.FIRST
                        load(n + first, 4 - first, it)
                        for b in ada_batches(g, 0) + (ada_batches(g, 1) if g == 0 else []):
                            ada.load(sp, b, it, PB)

                    def output(g, n, j, it):
                        load(n, 2, it)
                        if g < GROUPS - 1:
                            for b in ada_batches(g + 1, 1):
                                ada.load(sp, b, it, PB)

                    groups(sp, hidden, output)
                    if next_ws is not None:
                        next_ws.begin_sync(sp, ws, GW * GROUPS + 1)

                @block.tensor
                def _(pe):
                    if next_ada is not None:
                        ada.pe_credit(pe)

                    def job(j, it, parts):
                        if j >= RING:
                            pe.wait_ge(taken, at(it, PJ, j - RING + 1))
                        product(pe, psum[j % RING], parts).then_inc(done, 1)

                    def columns(g, it):
                        if next_ada is not None:
                            for i in range(2):
                                ada.columns(pe, 2 * g + i, 2 * i, at(it, 2, g + 1), it, PB)

                    def hidden(g, n, j, it):
                        if g > 0:
                            columns(g, it)
                        else:
                            first_two(pe, ws, 0, norm.in_ready, done)
                        for i in range(0 if g > 0 else 2, 4):
                            ws.wait(pe, n + i, it, PW)
                            job(j + i, it, full_parts(n + i))

                    def output(g, n, j, it):
                        if g == GROUPS - 1:
                            columns(GROUPS, None)
                        ws.wait(pe, n, it, PW)
                        ws.wait(pe, n + 1, it, PW)
                        pe.wait_ge(s_glo, at(it, PH, 2 * g + 2))
                        for d in range(KT):
                            job(j + d, it, [(w_hi[(n + i) % W_RING][:, d], w_lo[(n + i) % W_RING][:, d],
                                             g_hi[:, (2 * g + i) % 4], g_lo[:, (2 * g + i) % 4])
                                            for i in range(2)])

                    def skip():
                        pe.drain().then_inc(done, KT)
                        columns(0, None)

                    groups(pe, hidden, output, skip)
                    next_norm.pe_total(pe, psum[3])

                @block.scalar
                def _(act):
                    def split(n, it):
                        ws.split_hi(act, n, done, released(n, it), it, PW)

                    norm.act_apply(act, mod_col(layer, 3, 0, KT))

                    def tap(side, f, j, it):
                        act.wait_ge(done, at(it, PJ, j + 1))
                        if f >= 2:
                            act.wait_ge(s_glo, at(it, PH, f - 1))
                        act.activation((ua, ub)[side][f % 2][:], psum[j % RING][:], ACT.Identity,
                                       bias=col(cb + side * FT, f, it),
                                       scale=col(cw + (2 * 2 + side) * FT, f, it)).then_inc(s_tap, 1)

                    def silu(f, j, it):
                        act.wait_ge(taken, at(it, PJ, j + 1))
                        act.activation(ua[f % 2][:], ua[f % 2][:], ACT.Silu).then_inc(s_silu, 1)

                    def take_columns(g, it):
                        if next_ada is not None:
                            ada.take(act, 2 * g + 1, 2, it, PB)

                    def gated_hi(f, it):
                        act.wait_ge(s_gate, at(it, PH, f + 1))
                        act.activation(g_hi[:, f % 4], ua[f % 2][:], ACT.Copy).then_inc(s_ghi, 1)

                    def hidden(g, n, j, it):
                        f = 2 * g
                        split(n + 2, it)
                        split(n + 3, it)
                        tap(0, f, j, it)
                        if g > 0:
                            take_columns(g, it)
                            split(n + 4, it)
                        tap(1, f, j + 1, it)
                        silu(f, j, it)
                        if g > 0:
                            split(n + 5, it)
                        gated_hi(f, it)
                        tap(0, f + 1, j + 2, it)
                        if g == 0:
                            split(GW, it)
                        tap(1, f + 1, j + 3, it)
                        silu(f + 1, j + 2, it)

                    def output(g, n, j, it):
                        if g < 0:
                            split(n + 3, it)
                        gated_hi(2 * g + 3, it)
                        if g >= 0:
                            split(n + 2, it)
                            split(n + 3, it)

                    def last(j):
                        take_columns(GROUPS, None)
                        for d in range(KT):
                            act.wait_ge(taken, j + d + 1)
                            next_norm.act_square(act, d)
                            if d == 0 and next_ws is not None:
                                next_ws.begin_act(act)
                        next_norm.act_rstd(act, psum[3])

                    def skip():
                        output(-1, GW - 2, 0, None)
                        take_columns(0, None)

                    groups(act, hidden, lambda g, n, j, it: output(g, n, j, it) if it is not None
                           else last(j), skip)

                @block.vector
                def _(dve):
                    if next_ws is not None:
                        next_ws.credit(dve)
                    norm.dve_apply(dve, gain[:, (2 * layer + 1) * KT:(2 * layer + 2) * KT],
                                   mod_col(layer, 3, 0, KT))
                    cs = Steps(dve, s_cs)
                    if next_ada is not None:
                        ada.credit(dve)
                        ada_steps = Steps(dve, ada.step_sem)

                    def earlier_taps(side, f, j, it):
                        ps, dst = psum[j % RING], (ua, ub)[side][f % 2]
                        dve.wait_ge(s_tap, at(it, 2 * PH, 2 * f + side + 1))
                        cs.link(dve.scalar_tensor_tensor(
                            dst[:, 1:], ps[:, :S - 1], col(cw + (2 * 1 + side) * FT, f, it),
                            dst[:, 1:], ALU.mult, ALU.add))
                        dve.scalar_tensor_tensor(
                            dst[:, 2:], ps[:, :S - 2], col(cw + side * FT, f, it),
                            dst[:, 2:], ALU.mult, ALU.add).then_inc(taken, 1)

                    def gated(f, j, it):
                        dve.wait_ge(s_silu, at(it, PH, f + 1))
                        dve.wait_ge(taken, at(it, PJ, j + 1))
                        dve.tensor_tensor(ua[f % 2][:], ua[f % 2][:], ub[f % 2][:], ALU.mult)\
                            .then_inc(s_gate, 1)

                    def gated_lo(f, it):
                        dve.wait_ge(s_ghi, at(it, PH, f + 1))
                        dve.tensor_tensor(g_lo[:, f % 4], ua[f % 2][:], g_hi[:, f % 4].bitcast(F32),
                                          ALU.subtract).then_inc(s_glo, 1)

                    def sum_tiles(g, i, it):
                        for b in ada_batches(g, i):
                            ada.sum_tiles(dve, ada_steps, b, it, PB)

                    def hidden(g, n, j, it):
                        f = 2 * g
                        ws.split_lo(dve, n + 2, it, PW)
                        ws.split_lo(dve, n + 3, it, PW)
                        if g == 0:
                            sum_tiles(g, 0, it)
                        earlier_taps(0, f, j, it)
                        if g > 0:
                            ws.split_lo(dve, n + 4, it, PW)
                            sum_tiles(g, 0, it)
                        earlier_taps(1, f, j + 1, it)
                        gated(f, j + 1, it)
                        if g > 0:
                            ws.split_lo(dve, n + 5, it, PW)
                        gated_lo(f, it)
                        if g == 0:
                            sum_tiles(g, 1, it)
                        earlier_taps(0, f + 1, j + 2, it)
                        if g > 0:
                            sum_tiles(g, 1, it)
                        if g == 0:
                            ws.split_lo(dve, GW)
                        earlier_taps(1, f + 1, j + 3, it)

                    def output(g, n, j, it):
                        between = {0: lambda: gated(2 * g + 3, j - 1, it),
                                   1: lambda: gated_lo(2 * g + 3, it),
                                   2: lambda: ws.split_lo(dve, n + 2, it, PW),
                                   3: lambda: ws.split_lo(dve, n + 3, it, PW)}
                        if g < 0:
                            ws.split_lo(dve, n + 3)
                            del between[2], between[3]
                        for d in range(KT):
                            if g >= 0:
                                dve.wait_ge(done, at(it, PJ, j + d + 1))
                                dve.scalar_tensor_tensor(x[:, d], psum[(j + d) % RING][:],
                                                         gate2[:, d:d + 1], x[:, d],
                                                         ALU.mult, ALU.add).then_inc(taken, 1)
                            if g == GROUPS - 1:
                                if d >= 1:
                                    next_norm.dve_sum(dve, d - 1)
                                if d == 2 and next_ws is not None:
                                    next_ws.begin_dve(dve)
                            elif d in between:
                                between[d]()
                        if g == GROUPS - 1:
                            next_norm.dve_sum(dve, KT - 1)

                    def skip():
                        dve.drain().then_inc(taken, KT)
                        output(-1, GW - 2, 4, None)

                    loop_steps = [(cs, STEPS)]
                    if next_ada is not None:
                        loop_steps.append((ada_steps, PB * (KT - 1)))
                    groups(dve, hidden, output, skip, loop_steps)
                    if next_ada is not None:
                        ada.finish(dve, GROUPS + 1, 12 * KT, [(1, 0), (1, 1)])

        def rec_norm_phase(norm, ws, proj_done):
            s_spill = sem("x_spilled")
            with nc.Block() as block:
                @block.sync
                def _(sp):
                    for n in range(2, 4):
                        ws.load(sp, n)
                    sp.dma_start(x_spill, x[:]).then_inc(s_spill, 16)
                    sp.wait_ge(s_spill, 16)

                @block.scalar
                def _(act):
                    norm.act_apply(act, mod_col(1, 0, 0, KT))
                    for n in range(2, 4):
                        ws.split_hi(act, n, None, None)

                @block.vector
                def _(dve):
                    norm.dve_apply(dve, gain[:, 2 * KT:3 * KT], mod_col(1, 0, 0, KT))
                    for n in range(2, 4):
                        ws.split_lo(dve, n)

                @block.tensor
                def _(pe):
                    first_two(pe, ws, 0, norm.in_ready, proj_done)

        def rec_phase(ws, proj_done):
            N_A = 4
            (F, Q, V, GATE) = range(N_A)
            N_B = LEVELS + 6
            VT, L0 = 0, 1
            KT_, UPD, OUT, SS = (L0 + LEVELS + 1 + i for i in range(4))
            assert SS == N_B - 1
            PIECES = 4
            AHEAD = {VT: 2, L0: 1, L0 + 1: 2, OUT: 2}
            done = sem("rec_result_done")
            free = [sem(f"rec_psum{i}_free") for i in range(4)]
            s_masks = sem("rec_masks_landed")
            s_const = sem("rec_const_ready")
            s_sig = sem("rec_sigmoid_ready")
            s_f = sem("rec_f_ready")
            s_ln = sem("rec_logs_ready")
            s_lnf = sem("rec_ln_f_ready")
            s_q = sem("rec_q_next_ready")
            s_vraw = sem("rec_vT_ready")
            s_qk = sem("rec_q_and_k_ready")
            s_G = sem("rec_G_ready")
            s_eg = sem("rec_exp_G_ready")
            s_d = sem("rec_exponent_ready")
            s_e = sem("rec_decay_ready")
            s_x = sem("rec_level_operand_ready")
            s_kn = sem("rec_k_natural_ready")
            s_sq = sem("rec_squares_ready")
            s_rms = sem("rec_rstd_ready")
            s_normed = sem("rec_output_normed")
            s_step = sem("rec_dve_step")
            LN2 = float(np.log(2.0))

            def tiles(t):
                return t[:].rearrange("p (c n) -> p c n", c=TT)

            def count(h, per, k):
                it, off = h
                return at(it, per, off * per + k)

            def column(t, h):
                it, off = h
                return t[:, off:off + 1] if it is None else t[:, bass.ds(it + off, 1)]

            def head(h):
                it, off = h
                return oT[:, off] if it is None else \
                    oT[:, bass.ds(it + off, 1), :].rearrange("p a s -> p (a s)")

            def slot_of(j):
                return 2 + j % 2

            def read(j, h):
                s = slot_of(j)
                per = len([i for i in range(N_B) if slot_of(i) == s])
                before = len([i for i in range(max(j + 1, 0)) if slot_of(i) == s])
                return free[s], count(h, per, before + 1)

            def heads(eng, a, both, b, steps=()):
                a((None, 0))
                with eng.Fori(0, REC_HEADS - 1) as it:
                    for s, k in steps:
                        s.enter(it, k)
                    both((it, 0), (it, 1))
                    for s, k in steps:
                        s.leave(REC_HEADS - 1)
                b((None, REC_HEADS - 1))

            def weight(h, n):
                it, off = h
                return off * N_A + n, it, N_A

            with nc.Block() as block:
                @block.sync
                def _(sp):
                    sp.dma_start(AT[:, 0:LEVELS], masks_in).then_inc(s_masks, 16)

                    def load(h, first, n):
                        for i in range(first, first + n):
                            ws.load(sp, *weight(h, i))

                    heads(sp, lambda h: load(h, 4, 2), lambda hb, h: load(h, 2, 4), lambda h: None)

                @block.gpsimd
                def _(pool):
                    pool.memset(restart[:], 1).then_inc(s_const, 1)
                    pool.wait_ge(s_const, 1)
                    pool.memset(restart[:].rearrange("p (c n) -> p c n", c=TT)[:, :, 0:1], 0)\
                        .then_inc(s_const, 1)

                @block.tensor
                def _(pe):
                    for i in range(4):
                        pe.sem_inc(free[i], 1)

                    def piece(h, i):
                        n, part = divmod(i, PIECES)
                        w, it, per = weight(h, n)
                        if part == 0:
                            ws.wait(pe, w, it, per)
                            pe.wait_ge(free[n % 2], count(h, 2, n // 2 + 1))
                        ks = range(part * KT // PIECES, (part + 1) * KT // PIECES)
                        ins = product(pe, psum[n % 2], full_parts(w), None, ks)
                        if part == PIECES - 1:
                            ins.then_inc(proj_done, 1)

                    def results(h, ha):
                        pieces = iter(range(N_A * PIECES))

                        def per_tile(j, op):
                            if ha is not None:
                                for _ in range(AHEAD.get(j, 1)):
                                    piece(ha, next(pieces))
                            waits(j)
                            pe.wait_ge(*read(j - 2, h))
                            for c in range(TT):
                                ins = op(c, psum[slot_of(j)][:, c * P:(c + 1) * P])
                            ins.then_inc(done, 1)

                        def waits(j):
                            if j == VT:
                                pe.wait_ge(s_vraw, count(h, 1, 1))
                            elif j == L0:
                                pe.wait_ge(s_qk, count(h, 2, 2))
                            elif j <= KT_:
                                pe.wait_ge(s_x, count(h, LEVELS + 1, j - L0))
                            elif j == UPD:
                                pe.wait_ge(s_kn, count(h, 1, 1))
                            elif j == OUT:
                                pe.wait_ge(*read(UPD, h))

                        per_tile(VT, lambda c, o: pe.transpose(o, vT_next[:, c * P:(c + 1) * P], ident[:]))
                        per_tile(L0, lambda c, o: pe.matmul(o, tiles(kh)[:, c], tiles(qh)[:, c],
                                                            start=True, stop=True))
                        for l in range(1, LEVELS + 1):
                            xl = tiles(X[l % 2])
                            per_tile(L0 + l, lambda c, o: pe.matmul(o, xl[:, c], xl[:, c],
                                                                    start=True, stop=True))
                        xl = tiles(X[(LEVELS + 1) % 2])
                        per_tile(KT_, lambda c, o: pe.transpose(o, xl[:, c], ident[:]))
                        kn = tiles(X[1])
                        per_tile(UPD, lambda c, o: pe.matmul(o, kn[:, c], vn[:, c], start=True, stop=True))

                        def output(c, o):
                            ins = pe.matmul(o, vn[:, c], AT[:, c], start=True, stop=(c == 0))
                            if c > 0:
                                ins = pe.matmul(o, state[:, c], tiles(q_decay)[:, c], start=False, stop=True)
                            return ins
                        per_tile(OUT, output)
                        for i in pieces:
                            if ha is not None:
                                piece(ha, i)
                        pe.wait_ge(s_sq, count(h, 1, 1))
                        pe.wait_ge(*read(SS - 2, h))
                        for half in range(2):
                            cut = slice(half * HALF, (half + 1) * HALF)
                            ins = pe.matmul(psum[slot_of(SS)][:, cut], ones[:], f_next[:, cut],
                                            start=True, stop=True)
                        ins.then_inc(done, 1)

                    heads(pe, lambda h: [piece(h, i) for i in range(2 * PIECES, N_A * PIECES)],
                          lambda hb, h: results(hb, h), lambda h: results(h, None))

                @block.scalar
                def _(act):
                    act.wait_ge(s_const, 3)
                    act.activation(lb[:], lb[:], ACT.Exp).then_inc(s_const, 1)

                    def split(h, n):
                        w, it, per = weight(h, n)
                        ws.split_hi(act, w, proj_done, at(it, per, w - N_A + 1) if w >= N_A else None, it, per)

                    def sigmoid_f(h):
                        if h[1] > 0:
                            act.wait_ge(s_normed, count(h, 1, 0))
                        act.wait_ge(proj_done, count(h, N_A, F + 1))
                        act.activation(f_next[:], psum[0][:], ACT.Sigmoid).then_inc(s_sig, 1)
                        act.wait_ge(s_sig, count(h, 3, 1))
                        act.sem_inc(free[0], 1)

                    def logs(h):
                        act.wait_ge(s_f, count(h, 1, 1))
                        act.wait_ge(free[1], count(h, 2, 1))
                        act.activation(sig[:], f_next[:], ACT.Ln, scale=2.0 ** 63).then_inc(s_ln, 1)
                        act.activation(ln_next[:], ln_next[:], ACT.Ln).then_inc(s_ln, 1)

                    def sigmoid_q(h):
                        act.wait_ge(s_lnf, count(h, 1, 1))
                        act.wait_ge(proj_done, count(h, N_A, Q + 1))
                        act.activation(sig[:], psum[1][:], ACT.Sigmoid).then_inc(s_sig, 1)

                    def copy_v(h):
                        act.wait_ge(proj_done, count(h, N_A, V + 1))
                        act.activation(vT_next[:], psum[0][:], ACT.Copy).then_inc(s_vraw, 1)
                        act.wait_ge(s_vraw, count(h, 1, 1))
                        act.sem_inc(free[0], 1)

                    def sigmoid_gate(h):
                        act.wait_ge(proj_done, count(h, N_A, GATE + 1))
                        act.activation(sig[:], psum[1][:], ACT.Sigmoid).then_inc(s_sig, 1)

                    def hand_over(h):
                        act.wait_ge(s_q, count(h, 1, 1))
                        act.activation(qh[:], q_next[:], ACT.Copy).then_inc(s_qk, 1)
                        act.activation(kh[:], f_next[:], ACT.Identity, bias=ones[:, 0:1], scale=-1.0)\
                            .then_inc(s_qk, 1)

                    def first(h):
                        sigmoid_f(h)
                        logs(h)
                        split(h, N_A)
                        sigmoid_q(h)
                        split(h, N_A + 1)
                        copy_v(h)
                        hand_over(h)
                        first_decays(h)
                        sigmoid_gate(h)

                    def decay(h, l):
                        act.wait_ge(s_d, count(h, LEVELS + 1, l))
                        if l <= LEVELS:
                            b = X[l % 2][:].rearrange("p (b n) -> p b n", n=2 ** l)
                            half = 2 ** (l - 1)
                            act.activation(b[:, :, half:], b[:, :, half:], ACT.Exp)
                            act.activation(b[:, :, :half], b[:, :, :half], ACT.Exp, scale=-1.0)\
                                .then_inc(s_e, 1)
                        else:
                            act.activation(X[l % 2][:], X[l % 2][:], ACT.Exp, scale=-1.0)\
                                .then_inc(s_e, 1)

                    def first_decays(h):
                        decay(h, 1)
                        decay(h, 2)

                    def turn(h, ha):
                        def ahead(*ops):
                            if ha is not None:
                                for op in ops:
                                    op(ha)
                        act.activation(q_decay[:], G[:], ACT.Exp).then_inc(s_eg, 1)
                        act.activation(g_last[:], tiles(G)[:, :, P - 1], ACT.Exp).then_inc(s_eg, 1)
                        act.wait_ge(done, count(h, N_B, VT + 1))
                        act.activation(vn[:], tiles(psum[slot_of(VT)]), ACT.Copy)\
                            .then_inc(free[slot_of(VT)], 1)
                        ahead(lambda ha: split(ha, V), sigmoid_f)
                        decay(h, 3)
                        ahead(logs)
                        decay(h, 4)
                        ahead(lambda ha: split(ha, GATE), lambda ha: split(ha, N_A + F))
                        decay(h, 5)
                        ahead(sigmoid_q)
                        decay(h, 6)
                        ahead(lambda ha: split(ha, N_A + Q))
                        decay(h, 7)
                        decay(h, 8)
                        ahead(copy_v)
                        act.wait_ge(done, count(h, N_B, KT_ + 1))
                        act.activation(X[1][:], psum[slot_of(KT_)][:], ACT.Copy).then_inc(s_kn, 1)
                        act.wait_ge(s_kn, count(h, 1, 1))
                        act.sem_inc(free[slot_of(KT_)], 1)
                        ahead(hand_over)
                        act.wait_ge(done, count(h, N_B, OUT + 1))
                        if ha is not None:
                            act.wait_ge(s_qk, count(ha, 2, 2))
                        act.activation(f_next[:], psum[slot_of(OUT)][:], ACT.Square).then_inc(s_sq, 1)
                        ahead(first_decays, sigmoid_gate)
                        act.wait_ge(done, count(h, N_B, SS + 1))
                        act.activation(f_next[:], psum[slot_of(SS)][:], ACT.Ln, bias=eps_col[:, 0:1],
                                       scale=1.0 / P).then_inc(free[slot_of(SS)], 1)
                        act.wait_ge(*read(SS, h))
                        act.activation(f_next[:], f_next[:], ACT.Exp, scale=-0.5).then_inc(s_rms, 1)

                    assert LEVELS == 7
                    heads(act, first, lambda hb, h: turn(hb, h), lambda h: turn(h, None))

                @block.vector
                def _(dve):
                    dve.sem_inc(s_normed, 1)
                    st = Steps(dve, s_step)
                    logits = vec[:, C_LB:C_LB + REC_HEADS]
                    dve.wait_ge(s_const, 2)
                    dve.tensor_tensor(lb[:], logits, logits, ALU.subtract).then_inc(s_const, 1)
                    dve.wait_ge(s_const, 4)
                    st.link(dve.reciprocal(one_minus_lb[:], lb[:]))
                    st.link(dve.tensor_tensor(lb[:], lb[:], one_minus_lb[:], ALU.mult))
                    st.link(dve.tensor_tensor(lb[:], lb[:], lb[:], ALU.subtract))
                    st.link(dve.tensor_scalar(one_minus_lb[:], lb[:], -1.0, 1.0, ALU.mult, ALU.add))
                    dve.wait_ge(s_masks, 16)
                    st.link(dve.tensor_copy(mask[:], AT[:, 0:LEVELS]))

                    def split(h, n):
                        w, it, per = weight(h, n)
                        ws.split_lo(dve, w, it, per)

                    def forget(h):
                        dve.wait_ge(s_sig, count(h, 3, 1))
                        st.link(dve.tensor_scalar(f_next[:], f_next[:], column(one_minus_lb, h),
                                                  column(lb, h), ALU.mult, ALU.add))
                        dve.tensor_scalar(ln_next[:], f_next[:], 2.0 ** -60, None, ALU.max).then_inc(s_f, 1)

                    def ln_f(h):
                        dve.wait_ge(s_ln, count(h, 2, 1))
                        st.link(dve.tensor_scalar(sig[:], sig[:], -3.0 * LN2, 0.0, ALU.add, ALU.min))
                        dve.wait_ge(s_ln, count(h, 2, 2))
                        dve.tensor_tensor(ln_next[:], ln_next[:], sig[:], ALU.add).then_inc(s_lnf, 1)

                    def silu_q(h):
                        dve.wait_ge(s_sig, count(h, 3, 2))
                        dve.tensor_tensor(q_next[:], psum[1][:], sig[:], ALU.mult).then_inc(s_q, 1)
                        dve.wait_ge(s_q, count(h, 1, 1))
                        dve.sem_inc(free[1], 1)

                    def scan(h):
                        dve.wait_ge(s_lnf, count(h, 1, 1))
                        dve.tensor_tensor_scan(G[:], restart[:], ln_next[:], 0.0, ALU.mult, ALU.add)\
                            .then_inc(s_G, 1)

                    def silu_gate(h):
                        dve.wait_ge(s_sig, count(h, 3, 3))
                        dve.tensor_tensor(head(h), psum[1][:], sig[:], ALU.mult).then_inc(free[1], 1)

                    def first(h):
                        forget(h)
                        ln_f(h)
                        split(h, N_A)
                        silu_q(h)
                        split(h, N_A + 1)
                        scan(h)
                        first_exponents(h)
                        silu_gate(h)

                    def exponent(h, l):
                        if l <= LEVELS:
                            n, ref = 2 ** l, 2 ** (l - 1) - 1
                        else:
                            n, ref = P, P - 1
                        if l >= 3:
                            dve.wait_ge(done, count(h, N_B, L0 + l - 2 + 1))
                        g = G[:].rearrange("p (b n) -> p b n", n=n)
                        r = g[:, :, ref:ref + 1].to_broadcast([P, S // n, n])
                        dve.tensor_tensor(X[l % 2][:].rearrange("p (b n) -> p b n", n=n), g, r,
                                          ALU.subtract).then_inc(s_d, 1)

                    def first_exponents(h):
                        dve.wait_ge(s_G, count(h, 1, 1))
                        exponent(h, 1)
                        exponent(h, 2)

                    def operand(h, l):
                        dve.wait_ge(s_e, count(h, LEVELS + 1, l))
                        if l <= LEVELS:
                            n, half = 2 ** l, 2 ** (l - 1)
                            b, q, k = (t[:].rearrange("p (b n) -> p b n", n=n) for t in (X[l % 2], qh, kh))
                            dve.tensor_tensor(b[:, :, half:], b[:, :, half:], q[:, :, half:], ALU.mult)
                            dve.tensor_tensor(b[:, :, :half], b[:, :, :half], k[:, :, :half], ALU.mult)\
                                .then_inc(s_x, 1)
                        else:
                            dve.tensor_tensor(X[l % 2][:], X[l % 2][:], kh[:], ALU.mult).then_inc(s_x, 1)

                    def collect_waits(h, l):
                        dve.wait_ge(done, count(h, N_B, L0 + l + 1))
                        if l >= 1:
                            dve.wait_ge(*read(L0 + l - 1, h))

                    def collect(l):
                        ps = psum[slot_of(L0 + l)]
                        if l == 0:
                            diag = ident[:].unsqueeze(1).to_broadcast([P, TT, P])
                            ins = dve.tensor_tensor(AT[:], tiles(ps), diag, ALU.mult)
                        else:
                            m = mask[:, l - 1, :].unsqueeze(1).to_broadcast([P, TT, P])
                            ins = dve.copy_predicated(AT[:], m, tiles(ps))
                        ins.then_inc(free[slot_of(L0 + l)], 1)

                    def turn(h, ha):
                        def ahead(*ops):
                            if ha is not None:
                                for op in ops:
                                    op(ha)

                        beside = {1: [lambda ha: split(ha, V)],
                                  2: [forget],
                                  3: [ln_f],
                                  4: [lambda ha: split(ha, GATE), lambda ha: split(ha, N_A + F)],
                                  5: [silu_q],
                                  6: [lambda ha: split(ha, N_A + Q)]}
                        dve.wait_ge(s_qk, count(h, 2, 2))
                        for l in range(1, LEVELS + 2):
                            operand(h, l)
                            if l <= LEVELS:
                                collect_waits(h, l - 1)
                                if l == 1:
                                    dve.wait_ge(s_eg, count(h, 2, 2))
                                    st.link(dve.tensor_tensor(q_decay[:], q_decay[:], qh[:], ALU.mult))
                                else:
                                    exponent(h, l + 1)
                                collect(l - 1)
                            ahead(*beside.get(l, []))
                        collect_waits(h, LEVELS)
                        if ha is not None:
                            scan(ha)
                        else:
                            st.link(dve.tensor_copy(state[:, 0, 0:1], g_last[:, 0:1]))
                        collect(LEVELS)
                        dve.wait_ge(done, count(h, N_B, UPD + 1))
                        u = tiles(psum[slot_of(UPD)])
                        st.link(dve.tensor_copy(state[:, 1], u[:, 0]))
                        for c in range(1, TT - 1):
                            ins = dve.scalar_tensor_tensor(state[:, c + 1], state[:, c], g_last[:, c:c + 1],
                                                           u[:, c], ALU.mult, ALU.add)
                            if c < TT - 2:
                                st.link(ins)
                            else:
                                ins.then_inc(free[slot_of(UPD)], 1)
                        ahead(first_exponents, silu_gate)
                        dve.wait_ge(s_rms, count(h, 1, 1))
                        dve.scalar_tensor_tensor(ln_next[:], psum[slot_of(OUT)][:],
                                                 vec[:, C_GNORM:C_GNORM + 1], f_next[:],
                                                 ALU.mult, ALU.mult).then_inc(free[slot_of(OUT)], 1)
                        dve.wait_ge(*read(OUT, h))
                        dve.tensor_tensor(head(h), ln_next[:], head(h), ALU.mult).then_inc(s_normed, 1)

                    heads(dve, first, lambda hb, h: turn(hb, h), lambda h: turn(h, None), ((st, TT + 1),))

        def rec_prepare():
            s_back = sem("x_back")
            s_hi = sem("ro_hi")
            s_lo = sem("ro_lo")

            def sync(sp):
                sp.dma_start(x[:], x_spill).then_inc(s_back, 16)

            def scalar(act):
                for k in range(KT):
                    act.activation(in_hi[:, k], oT[:, k], ACT.Copy).then_inc(s_hi, 1)

            def vector(dve):
                for k in range(KT):
                    dve.wait_ge(s_hi, k + 1)
                    dve.tensor_tensor(in_lo[:, k], oT[:, k], in_hi[:, k].bitcast(F32), ALU.subtract)\
                        .then_inc(s_lo, 1)
                dve.wait_ge(s_back, 16)

            return dict(sync=sync, scalar=scalar, vector=vector, ready=s_lo)

        def final_phase(norm):
            s_y = sem("y_ready")
            s_store = sem("y_stored")
            with nc.Block() as block:
                @block.vector
                def _(dve):
                    for k in range(KT):
                        dve.scalar_tensor_tensor(x[:, k], x[:, k], vec[:, C_FINAL + k:C_FINAL + k + 1],
                                                 norm.rstd, ALU.mult, ALU.mult).then_inc(s_y, 1)

                @block.sync
                def _(sp):
                    for k in range(KT):
                        sp.wait_ge(s_y, k + 1)
                        sp.dma_start(outT[:, k, :], x[:, k]).then_inc(s_store, 16)
                    sp.wait_ge(s_store, 16 * KT)

        sq, scaled = [ua[0][:], ub[0][:]], [ua[1][:], ub[1][:]]
        first_norm = Norm("n0", [ada_raw[:, i] for i in range(2)], [q_raw[:, KT - 2 + i] for i in range(2)],
                          kv_raw[:, 0])
        ffn_norm = [Norm(f"f{layer}", sq, scaled, rstd[:]) for layer in range(DEPTH)]
        rec_norm = Norm("rn", sq, scaled, rstd[:])
        final_norm = Norm("fin", sq, None, rstd[:])
        qkv_ws, ao_ws, rec_ws = WeightStream("qkv", W_QKV), WeightStream("ao", W_AO), WeightStream("rec", W_REC)
        ffn_ws = [WeightStream(f"f{layer}", base, first=4, gap=2)
                  for layer, base in enumerate((W_FFN0, W_FFN1))]
        proj_done = sem("rec_projection_done")
        setup_phase(first_norm, qkv_ws)
        qkv_phase(first_norm, qkv_ws)
        attention_phase(ao_ws)
        out_proj_phase("ao", ao_ws, 0, mod_col(0, 2, 0, KT), ffn_norm[0], ffn_ws[0])
        ffn_phase(0, ffn_ws[0], ffn_norm[0], rec_norm, rec_ws, 6 * KT)
        rec_norm_phase(rec_norm, rec_ws, proj_done)
        rec_phase(rec_ws, proj_done)
        out_proj_phase("ro", rec_ws, N_REC, mod_col(1, 2, 0, KT), ffn_norm[1], ffn_ws[1], rec_prepare())
        ffn_phase(1, ffn_ws[1], ffn_norm[1], final_norm)
        final_phase(final_norm)


def per_column(v):
    return np.reshape(v, (-1, P)).T


def kernel(x, c, positions, ada_w, ada_b, norm1_w, norm2_w, final_norm_w, attn_w_in, attn_w_out,
           attn_sinks, rec_w_in, rec_lb_logits, rec_g_norm, rec_w_out, ffn_w_in, ffn_conv_w,
           ffn_conv_b, ffn_w_out):
    import concourse.bacc as bacc
    from concourse.bass_utils import run_bass_kernel_spmd

    def arr(a):
        return np.asarray(a)

    sinks = arr(attn_sinks)[0]
    sink_cols = np.repeat(sinks.reshape(N_HEADS // 2, 2).T, CHUNK, axis=0)
    row = np.arange(P) % HEAD
    inv_freq = np.float32(ROPE_THETA) ** (-np.arange(0, ROPE, 2, dtype=np.float32) / np.float32(ROPE))
    freq = np.where(row < ROPE, inv_freq.astype(np.float32)[row % (ROPE // 2)], np.float32(0))[:, None]
    sign = np.where(row < ROPE // 2, 1.0, np.where(row < ROPE, -1.0, 0.0)).astype(np.float32)[:, None]
    conv_w = arr(ffn_conv_w)
    vec = np.concatenate(
        [per_column(arr(c)), per_column(arr(ada_b)), per_column(arr(norm1_w)), per_column(arr(norm2_w)),
         per_column(arr(final_norm_w)), per_column(arr(rec_lb_logits)), per_column(arr(rec_g_norm)),
         sink_cols, freq.astype(np.float32), sign, per_column(conv_w), per_column(arr(ffn_conv_b))], axis=1)
    assert vec.shape == (P, N_VEC), vec.shape

    def column_tiles(w):
        return w.reshape(KT, P, -1, P).transpose(2, 1, 0, 3)

    def row_tiles(w):
        return w.reshape(-1, P, KT, P)

    q_order = np.arange(D).reshape(2, KT, HEAD).transpose(1, 0, 2).reshape(-1)
    w_in = arr(attn_w_in)[0]
    qkv = column_tiles(np.concatenate([w_in[:, q_order], w_in[:, D:]], axis=1))
    attn_out = column_tiles(arr(attn_w_out)[0][q_order])

    def ffn_tiles(layer):
        up, down = column_tiles(arr(ffn_w_in)[layer]), row_tiles(arr(ffn_w_out)[layer])
        order = []
        for g in range(GROUPS + 1):
            if g < GROUPS:
                order += [up[2 * g], up[FT + 2 * g], up[2 * g + 1], up[FT + 2 * g + 1]]
            if g > 0:
                order += [down[2 * g - 2], down[2 * g - 1]]
        return np.stack(order)

    rec = column_tiles(arr(rec_w_in)[0]).reshape(4, REC_HEADS, P, KT, P)[[1, 0, 2, 3]]
    rec = rec.transpose(1, 0, 2, 3, 4).reshape(-1, P, KT, P)
    rec_out = column_tiles(arr(rec_w_out)[0])
    w_tiles = np.concatenate([qkv, attn_out, ffn_tiles(0), rec, rec_out, ffn_tiles(1)])
    assert w_tiles.shape[0] == N_WTILES
    ada = np.concatenate([column_tiles(arr(ada_w)[i]) for i in range(DEPTH)])

    s_, t_ = np.arange(P)[:, None], np.arange(P)[None, :]
    masks = np.stack([(s_ >> l == t_ >> l) & (s_ >> (l - 1) & 1 == 0) & (t_ >> (l - 1) & 1 == 1)
                      for l in range(1, LEVELS + 1)], axis=1).astype(np.float32)

    ins = {
        "xT": np.ascontiguousarray(arr(x)[0].T.reshape(KT, P, S).transpose(1, 0, 2)),
        "positions": np.ascontiguousarray(arr(positions)[0]),
        "vec": np.ascontiguousarray(vec),
        "ada_tiles": np.ascontiguousarray(ada.reshape(-1, P, KT * P)),
        "w_tiles": np.ascontiguousarray(w_tiles.reshape(-1, P, KT * P)),
        "ident": np.eye(P, dtype=np.float32),
        "masks": np.ascontiguousarray(masks),
    }
    nc = bacc.Bacc("TRN2", target_bir_lowering=False, num_devices=1)
    aps = [nc.dram_tensor(f"in_{n}", a.shape, mybir.dt.from_np(a.dtype), kind="ExternalInput").ap()
           for n, a in ins.items()]
    out = nc.dram_tensor("out", (P, KT, S), F32, kind="ExternalOutput").ap()
    spill = nc.dram_tensor("x_spill", (P, KT, S), F32, kind="Internal").ap()
    trunk_kernel(nc, *aps, out, spill)
    r = run_bass_kernel_spmd(nc, [{f"in_{n}": a for n, a in ins.items()}], core_ids=[0])
    yT = r.results[0]["out"]
    return np.ascontiguousarray(yT.transpose(1, 0, 2).reshape(D, S).T)[None]
```
